# Optimizing a Trainium2 kernel written in Bass

```python
import jax, jax.numpy as jnp
from jax import lax
import numpy as np
import math

D_MODEL = 2048
BATCH = 1
SEQ = 256
DEPTH = 2

CHUNK = 64
EXPAND = 2
D_INNER = EXPAND * D_MODEL
HEAD_DIM = 128
N_HEADS = D_INNER // HEAD_DIM
N_LEFT_CHUNKS = 8
BAND = (N_LEFT_CHUNKS + 1) * CHUNK
REL_CLIP = 256
N_REL = 2 * REL_CLIP + 1
Q_BLOCK = 128
N_A_LAYERS = DEPTH // 2
N_B_LAYERS = DEPTH - N_A_LAYERS
EPS = 1e-6
NEG_INF = -1e30


def rms_norm(x, g):
    xf = x.astype(jnp.float32)
    y = xf * lax.rsqrt(jnp.mean(xf * xf, axis=-1, keepdims=True) + EPS)
    return (y * g.astype(jnp.float32)).astype(x.dtype)

def split_heads(t):
    return t.reshape(t.shape[0], t.shape[1], N_HEADS, HEAD_DIM)

def chunked_relbias_attention(q, k, v, rel_bias):
    b, s = q.shape[0], q.shape[1]
    n_chunks = s // CHUNK
    pad = N_LEFT_CHUNKS * CHUNK
    k_pad = jnp.pad(k, ((0, 0), (pad, 0), (0, 0), (0, 0)))
    v_pad = jnp.pad(v, ((0, 0), (pad, 0), (0, 0), (0, 0)))
    qi = jnp.arange(CHUNK)[:, None]
    kj = jnp.arange(BAND)[None, :]
    rel_idx = jnp.clip(pad + qi - kj, -REL_CLIP, REL_CLIP) + REL_CLIP
    bias = rel_bias.astype(jnp.float32)[:, rel_idx]
    scale = HEAD_DIM ** -0.5
    band_pos = jnp.arange(BAND)

    def one_chunk(c):
        start = c * CHUNK
        q_c = lax.dynamic_slice_in_dim(q, start, CHUNK, axis=1)
        k_c = lax.dynamic_slice_in_dim(k_pad, start, BAND, axis=1)
        v_c = lax.dynamic_slice_in_dim(v_pad, start, BAND, axis=1)
        sc = jnp.einsum('bqhd,bkhd->bhqk', q_c, k_c).astype(jnp.float32) * scale + bias
        valid = (start + band_pos) >= pad
        sc = jnp.where(valid[None, None, None, :], sc, NEG_INF)
        p = jax.nn.softmax(sc, axis=-1).astype(v.dtype)
        return jnp.einsum('bhqk,bkhd->bqhd', p, v_c)

    out = lax.map(one_chunk, jnp.arange(n_chunks))
    return jnp.moveaxis(out, 0, 1).reshape(b, s, N_HEADS, HEAD_DIM)

def forgetting_attention(q, k, v, cum_logf_h):
    s = q.shape[1]
    scale = HEAD_DIM ** -0.5
    outs = []
    for i in range(s // Q_BLOCK):
        q0 = i * Q_BLOCK
        end = q0 + Q_BLOCK
        q_b = q[:, q0:end]
        k_b = k[:, :end]
        v_b = v[:, :end]
        sc = jnp.einsum('bqhd,bkhd->bhqk', q_b, k_b).astype(jnp.float32) * scale
        decay = cum_logf_h[:, :, q0:end, None] - cum_logf_h[:, :, None, :end]
        causal = (q0 + jnp.arange(Q_BLOCK))[:, None] >= jnp.arange(end)[None, :]
        sc = jnp.where(causal[None, None], sc + decay, NEG_INF)
        p = jax.nn.softmax(sc, axis=-1).astype(v.dtype)
        outs.append(jnp.einsum('bhqk,bkhd->bqhd', p, v_b))
    return jnp.concatenate(outs, axis=1)

def first_inputs(seed: int = 0) -> dict:
    key = jax.random.key(seed)
    ks = jax.random.split(key, 16)
    f32 = jnp.float32
    d_scale = D_MODEL ** -0.5
    out_scale = 0.5 * D_INNER ** -0.5
    x = jax.random.normal(ks[0], (BATCH, SEQ, D_MODEL), f32)
    a_norm = 1.0 + 0.02 * jax.random.normal(ks[1], (N_A_LAYERS, D_MODEL), f32)
    a_w_in = d_scale * jax.random.normal(ks[2], (N_A_LAYERS, D_MODEL, 4 * D_INNER), f32)
    a_rel_bias = 0.1 * jax.random.normal(ks[3], (N_A_LAYERS, N_HEADS, N_REL), f32)
    a_w_out = out_scale * jax.random.normal(ks[4], (N_A_LAYERS, D_INNER, D_MODEL), f32)
    kv_norm = 1.0 + 0.02 * jax.random.normal(ks[5], (D_MODEL,), f32)
    kv_w = d_scale * jax.random.normal(ks[6], (D_MODEL, 2 * D_INNER), f32)
    f_w = d_scale * jax.random.normal(ks[7], (D_MODEL, N_HEADS), f32)
    f_b = jnp.linspace(1.0, 5.0, N_HEADS, dtype=f32) + 0.1 * jax.random.normal(ks[8], (N_HEADS,), f32)
    b_norm = 1.0 + 0.02 * jax.random.normal(ks[9], (N_B_LAYERS, D_MODEL), f32)
    b_w_in = d_scale * jax.random.normal(ks[10], (N_B_LAYERS, D_MODEL, 2 * D_INNER), f32)
    b_w_out = out_scale * jax.random.normal(ks[11], (N_B_LAYERS, D_INNER, D_MODEL), f32)
    final_norm = 1.0 + 0.02 * jax.random.normal(ks[12], (D_MODEL,), f32)
    return {"x": x, "a_norm": a_norm, "a_w_in": a_w_in, "a_rel_bias": a_rel_bias,
            "a_w_out": a_w_out, "kv_norm": kv_norm, "kv_w": kv_w, "f_w": f_w,
            "f_b": f_b, "b_norm": b_norm, "b_w_in": b_w_in, "b_w_out": b_w_out,
            "final_norm": final_norm}

def first_block(x, a_norm, a_w_in, a_rel_bias, a_w_out, kv_norm, kv_w, f_w, f_b,
              b_norm, b_w_in, b_w_out, final_norm):
    b, s, _ = x.shape
    k_sh = v_sh = cum_logf_h = None
    for layer in range(DEPTH):
        if layer < N_A_LAYERS:
            h = rms_norm(x, a_norm[layer])
            q, k, v, g = jnp.split(h @ a_w_in[layer], 4, axis=-1)
            o = chunked_relbias_attention(split_heads(q), split_heads(k), split_heads(v),
                                          a_rel_bias[layer]).reshape(b, s, D_INNER)
            x = x + (o * jax.nn.silu(g)) @ a_w_out[layer]
        else:
            if layer == N_A_LAYERS:
                h_kv = rms_norm(x, kv_norm)
                k_s, v_s = jnp.split(h_kv @ kv_w, 2, axis=-1)
                k_sh, v_sh = split_heads(k_s), split_heads(v_s)
                logf = jax.nn.log_sigmoid((h_kv @ f_w + f_b).astype(jnp.float32))
                cum_logf_h = jnp.transpose(jnp.cumsum(logf, axis=1), (0, 2, 1))
            lb = layer - N_A_LAYERS
            h = rms_norm(x, b_norm[lb])
            q, g = jnp.split(h @ b_w_in[lb], 2, axis=-1)
            o = forgetting_attention(split_heads(q), k_sh, v_sh, cum_logf_h).reshape(b, s, D_INNER)
            x = x + (o * jax.nn.silu(g)) @ b_w_out[lb]
    return rms_norm(x, final_norm)


N_META = 16
D_MIX = D_MODEL
CONV_W = D_MIX // 4
CONV_K = 31
HEAD_DIM_2 = 64
N_HEADS_2 = (D_MIX // 2) // HEAD_DIM_2
N_KV = 4
GROUP = N_HEADS_2 // N_KV
ATT_W = N_HEADS_2 * HEAD_DIM_2
KV_W = N_KV * HEAD_DIM_2
WINDOW = 128
BLOCK = 128
ROT_DIM = HEAD_DIM_2 // 4
ROPE_THETA = 500000.0
LRU_W = D_MIX // 4
LRU_HEADS = 8
LRU_HEAD_DIM = LRU_W // LRU_HEADS
LRU_CONV_K = 4
LRU_C = 8.0
IN_WIDTHS = (CONV_W, CONV_W, CONV_W,
             ATT_W, KV_W, KV_W, ATT_W,
             LRU_W, LRU_W)
IN_TOTAL = sum(IN_WIDTHS)
OUT_IN = CONV_W + ATT_W + LRU_W
LN_EPS = 1e-5
DEEPNORM_ALPHA = (2.0 * DEPTH) ** 0.25
DEEPNORM_BETA = (8.0 * DEPTH) ** -0.25
NEG_INF_2 = -1e30


def _layer_norm(x, g, b):
    xf = x.astype(jnp.float32)
    mu = jnp.mean(xf, axis=-1, keepdims=True)
    var = jnp.mean(jnp.square(xf - mu), axis=-1, keepdims=True)
    y = (xf - mu) * lax.rsqrt(var + LN_EPS)
    return (y * g.astype(jnp.float32) + b.astype(jnp.float32)).astype(x.dtype)

def _causal_depthwise_conv(x, w, b):
    k = w.shape[0]
    y = lax.conv_general_dilated(
        x, w[:, None, :].astype(x.dtype), window_strides=(1,), padding=[(k - 1, 0)],
        dimension_numbers=("NWC", "WIO", "NWC"), feature_group_count=x.shape[-1])
    return y + b

def _partial_rotary(x, pos):
    half = ROT_DIM // 2
    inv_freq = ROPE_THETA ** (-jnp.arange(half, dtype=jnp.float32) / half)
    ang = pos.astype(jnp.float32)[:, None] * inv_freq[None, :]
    cos = jnp.cos(ang)[None, :, None, :]
    sin = jnp.sin(ang)[None, :, None, :]
    x1 = x[..., :half].astype(jnp.float32)
    x2 = x[..., half:ROT_DIM].astype(jnp.float32)
    rot = jnp.concatenate([x1 * cos - x2 * sin, x2 * cos + x1 * sin], axis=-1).astype(x.dtype)
    return jnp.concatenate([rot, x[..., ROT_DIM:]], axis=-1)

def _sliding_window_sink_attention(q, k, v, sinks):
    B, L, H, Dh = q.shape
    S = L - N_META
    nblk = S // BLOCK
    scale = Dh ** -0.5
    sink_kg = sinks.astype(jnp.float32).reshape(N_KV, GROUP)

    qm, qr = q[:, :N_META], q[:, N_META:]
    km, kr = k[:, :N_META], k[:, N_META:]
    vm, vr = v[:, :N_META], v[:, N_META:]

    qb = qr.reshape(B, nblk, BLOCK, N_KV, GROUP, Dh)
    kb = kr.reshape(B, nblk, BLOCK, N_KV, Dh)
    vb = vr.reshape(B, nblk, BLOCK, N_KV, Dh)
    pad = ((0, 0), (1, 0), (0, 0), (0, 0), (0, 0))
    k_band = jnp.concatenate([jnp.pad(kb, pad)[:, :-1], kb], axis=2)
    v_band = jnp.concatenate([jnp.pad(vb, pad)[:, :-1], vb], axis=2)

    s_meta = jnp.einsum("bnqkgd,bmkd->bkgnqm", qb, km).astype(jnp.float32) * scale
    s_band = jnp.einsum("bnqkgd,bnjkd->bkgnqj", qb, k_band).astype(jnp.float32) * scale
    qi = jnp.arange(BLOCK)[:, None]
    kj = jnp.arange(2 * BLOCK)[None, :]
    diff = BLOCK + qi - kj
    in_window = (diff >= 0) & (diff < WINDOW)
    blk = jnp.arange(nblk)[:, None, None]
    valid = in_window[None] & ((kj[None] >= BLOCK) | (blk > 0))
    s_band = jnp.where(valid[None, None, None], s_band, NEG_INF_2)
    sink_col = jnp.broadcast_to(sink_kg[None, :, :, None, None, None], s_meta.shape[:-1] + (1,))
    probs = jax.nn.softmax(jnp.concatenate([s_meta, s_band, sink_col], axis=-1), axis=-1)
    p_meta = probs[..., :N_META].astype(v.dtype)
    p_band = probs[..., N_META:N_META + 2 * BLOCK].astype(v.dtype)
    out_r = (jnp.einsum("bkgnqm,bmkd->bnqkgd", p_meta, vm)
             + jnp.einsum("bkgnqj,bnjkd->bnqkgd", p_band, v_band)).reshape(B, S, H, Dh)

    qmg = qm.reshape(B, N_META, N_KV, GROUP, Dh)
    s_mm = jnp.einsum("bqkgd,bmkd->bkgqm", qmg, km).astype(jnp.float32) * scale
    causal = jnp.tril(jnp.ones((N_META, N_META), dtype=bool))
    s_mm = jnp.where(causal[None, None, None], s_mm, NEG_INF_2)
    sink_mm = jnp.broadcast_to(sink_kg[None, :, :, None, None], s_mm.shape[:-1] + (1,))
    p_mm = jax.nn.softmax(jnp.concatenate([s_mm, sink_mm], axis=-1), axis=-1)[..., :N_META]
    out_m = jnp.einsum("bkgqm,bmkd->bqkgd", p_mm.astype(v.dtype), vm).reshape(B, N_META, H, Dh)

    return jnp.concatenate([out_m, out_r], axis=1)

def _rg_lru(x, w_a, b_a, w_x, b_x, lam):
    B, L, C = x.shape
    xh = x.reshape(B, L, LRU_HEADS, LRU_HEAD_DIM)
    r = jax.nn.sigmoid(jnp.einsum("blhi,hij->blhj", xh, w_a).reshape(B, L, C) + b_a)
    i = jax.nn.sigmoid(jnp.einsum("blhi,hij->blhj", xh, w_x).reshape(B, L, C) + b_x)
    log_a = -LRU_C * r.astype(jnp.float32) * jax.nn.softplus(-lam.astype(jnp.float32))
    a = jnp.exp(log_a)
    u = jnp.sqrt(-jnp.expm1(2.0 * log_a)) * (i * x).astype(jnp.float32)

    def combine(c1, c2):
        a1, b1 = c1
        a2, b2 = c2
        return a1 * a2, a2 * b1 + b2

    _, h = lax.associative_scan(combine, (a, u), axis=1)
    return h.astype(x.dtype)

def _hybrid_layer(h, pos, w_in, conv_dw_w, conv_dw_b, conv_ln_g, conv_ln_b, conv_pw_w, conv_pw_b,
                  attn_sinks, lru_conv_w, lru_conv_b, lru_wa, lru_ba, lru_wx, lru_bx, lru_lambda,
                  w_out, ln_post_g, ln_post_b):
    B, L, _ = h.shape
    proj = h @ w_in
    split_pts = [int(s) for s in np.cumsum(IN_WIDTHS)[:-1]]
    (c_val, c_glu, c_gate, q, k, v, a_gate, r_x, r_gate) = jnp.split(proj, split_pts, axis=-1)

    c = c_val * jax.nn.sigmoid(c_glu)
    c = _causal_depthwise_conv(c, conv_dw_w, conv_dw_b)
    c = jax.nn.silu(_layer_norm(c, conv_ln_g, conv_ln_b))
    c = c @ conv_pw_w + conv_pw_b
    y_conv = c * jax.nn.silu(c_gate)

    q = _partial_rotary(q.reshape(B, L, N_HEADS_2, HEAD_DIM_2), pos)
    k = _partial_rotary(k.reshape(B, L, N_KV, HEAD_DIM_2), pos)
    v = v.reshape(B, L, N_KV, HEAD_DIM_2)
    att = _sliding_window_sink_attention(q, k, v, attn_sinks).reshape(B, L, ATT_W)
    y_attn = att * jax.nn.silu(a_gate)

    r = _causal_depthwise_conv(r_x, lru_conv_w, lru_conv_b)
    r = _rg_lru(r, lru_wa, lru_ba, lru_wx, lru_bx, lru_lambda)
    y_lru = r * jax.nn.silu(r_gate)

    mixed = jnp.concatenate([y_conv, y_attn, y_lru], axis=-1) @ w_out
    return _layer_norm(DEEPNORM_ALPHA * h + mixed, ln_post_g, ln_post_b)

def second_inputs(seed: int = 0) -> dict:
    key = jax.random.key(seed)
    ks = jax.random.split(key, 24)
    f32 = jnp.float32
    nrm = lambda k, shape, s: jax.random.normal(k, shape, f32) * s
    u = jax.random.uniform(ks[17], (DEPTH, LRU_W), f32, 0.9, 0.999)
    s = u ** (1.0 / LRU_C)
    lam = jnp.log(s) - jnp.log1p(-s)
    return {
        "x": nrm(ks[0], (BATCH, SEQ, D_MODEL), 1.0),
        "meta_tokens": nrm(ks[1], (N_META, D_MODEL), 1.0),
        "ln_in_g": 1.0 + nrm(ks[2], (D_MODEL,), 0.02),
        "ln_in_b": nrm(ks[3], (D_MODEL,), 0.02),
        "w_in": nrm(ks[4], (DEPTH, D_MODEL, IN_TOTAL), D_MODEL ** -0.5),
        "conv_dw_w": nrm(ks[5], (DEPTH, CONV_K, CONV_W), CONV_K ** -0.5),
        "conv_dw_b": nrm(ks[6], (DEPTH, CONV_W), 0.01),
        "conv_ln_g": 1.0 + nrm(ks[7], (DEPTH, CONV_W), 0.02),
        "conv_ln_b": nrm(ks[8], (DEPTH, CONV_W), 0.02),
        "conv_pw_w": nrm(ks[9], (DEPTH, CONV_W, CONV_W), DEEPNORM_BETA * CONV_W ** -0.5),
        "conv_pw_b": nrm(ks[10], (DEPTH, CONV_W), 0.01),
        "attn_sinks": nrm(ks[11], (DEPTH, N_HEADS_2), 0.5),
        "lru_conv_w": nrm(ks[12], (DEPTH, LRU_CONV_K, LRU_W), LRU_CONV_K ** -0.5),
        "lru_conv_b": nrm(ks[13], (DEPTH, LRU_W), 0.01),
        "lru_wa": nrm(ks[14], (DEPTH, LRU_HEADS, LRU_HEAD_DIM, LRU_HEAD_DIM), LRU_HEAD_DIM ** -0.5),
        "lru_ba": nrm(ks[15], (DEPTH, LRU_W), 0.01),
        "lru_wx": nrm(ks[16], (DEPTH, LRU_HEADS, LRU_HEAD_DIM, LRU_HEAD_DIM), LRU_HEAD_DIM ** -0.5),
        "lru_bx": nrm(ks[18], (DEPTH, LRU_W), 0.01),
        "lru_lambda": lam,
        "w_out": nrm(ks[19], (DEPTH, OUT_IN, D_MODEL), DEEPNORM_BETA * OUT_IN ** -0.5),
        "ln_post_g": 1.0 + nrm(ks[20], (DEPTH, D_MODEL), 0.02),
        "ln_post_b": nrm(ks[21], (DEPTH, D_MODEL), 0.02),
    }

def second_block(x, meta_tokens, ln_in_g, ln_in_b, w_in, conv_dw_w, conv_dw_b, conv_ln_g, conv_ln_b,
              conv_pw_w, conv_pw_b, attn_sinks, lru_conv_w, lru_conv_b, lru_wa, lru_ba, lru_wx,
              lru_bx, lru_lambda, w_out, ln_post_g, ln_post_b):
    B = x.shape[0]
    meta = jnp.broadcast_to(meta_tokens[None].astype(x.dtype), (B, N_META, x.shape[-1]))
    h = jnp.concatenate([meta, x], axis=1)
    h = _layer_norm(h, ln_in_g, ln_in_b)
    pos = jnp.arange(h.shape[1], dtype=jnp.int32)
    for l in range(DEPTH):
        h = _hybrid_layer(h, pos, w_in[l], conv_dw_w[l], conv_dw_b[l], conv_ln_g[l], conv_ln_b[l],
                          conv_pw_w[l], conv_pw_b[l], attn_sinks[l], lru_conv_w[l], lru_conv_b[l],
                          lru_wa[l], lru_ba[l], lru_wx[l], lru_bx[l], lru_lambda[l],
                          w_out[l], ln_post_g[l], ln_post_b[l])
    return h[:, N_META:]


def setup_inputs(seed=0):
    out = dict(first_inputs(seed))
    for name, value in second_inputs(seed + 1).items():
        if name != "x":
            out[name + "_2"] = value
    return out


def reference(
    x, a_norm, a_w_in, a_rel_bias, a_w_out, kv_norm, kv_w, f_w, f_b, b_norm, b_w_in, b_w_out,
    final_norm, meta_tokens_2, ln_in_g_2, ln_in_b_2, w_in_2, conv_dw_w_2, conv_dw_b_2,
    conv_ln_g_2, conv_ln_b_2, conv_pw_w_2, conv_pw_b_2, attn_sinks_2, lru_conv_w_2,
    lru_conv_b_2, lru_wa_2, lru_ba_2, lru_wx_2, lru_bx_2, lru_lambda_2, w_out_2, ln_post_g_2,
    ln_post_b_2,
):
    x = first_block(
        x, a_norm, a_w_in, a_rel_bias, a_w_out, kv_norm, kv_w, f_w, f_b, b_norm, b_w_in,
        b_w_out, final_norm,
    )
    return second_block(
        x, meta_tokens_2, ln_in_g_2, ln_in_b_2, w_in_2, conv_dw_w_2, conv_dw_b_2, conv_ln_g_2,
        conv_ln_b_2, conv_pw_w_2, conv_pw_b_2, attn_sinks_2, lru_conv_w_2, lru_conv_b_2,
        lru_wa_2, lru_ba_2, lru_wx_2, lru_bx_2, lru_lambda_2, w_out_2, ln_post_g_2, ln_post_b_2,
    )


_drawn_inputs = setup_inputs


def setup_inputs(seed=0):
    import zlib

    import numpy as np

    out = dict(_drawn_inputs(seed))
    spreads = {}
    factors = {'a_norm': 8.0,
     'a_rel_bias': 8.0,
     'kv_norm': 8.0,
     'f_w': 2.912,
     'b_norm': 8.0,
     'final_norm': 2.888,
     'ln_in_g_2': 2.863,
     'conv_dw_b_2': 8.0,
     'conv_ln_g_2': 52.633,
     'conv_ln_b_2': 52.553,
     'conv_pw_b_2': 38.531,
     'attn_sinks_2': 48.367,
     'lru_conv_b_2': 8.0,
     'lru_ba_2': 200.0,
     'lru_bx_2': 64.0,
     'ln_in_b_2': 4.008}
    for name, (base, spread) in spreads.items():
        noise = np.random.default_rng([zlib.crc32(name.encode()), seed]).standard_normal(out[name].shape)
        drawn = base * np.exp(spread * noise) if base else spread * noise
        out[name] = __import__('jax').numpy.asarray(drawn.astype(out[name].dtype))
    for name, factor in factors.items():
        out[name] = (out[name] * factor).astype(out[name].dtype)
    return out
```

```python
from contextlib import ExitStack

import concourse.bass as bass
from concourse import mybir
import numpy as np

F32 = mybir.dt.float32
F32R = mybir.dt.float32r
ALU = mybir.AluOpType
ACT = mybir.ActivationFunctionType
AX_X = mybir.AxisListType.X

P = 128
D = 2048
KT = D // P
S = 256
META = 16
T = S + META
INNER = 4096
HEADS = INNER // P
PAIRS = HEADS // 2
UNIT_N = 256
PIECES = 4
PK = KT // PIECES
QKVG = 4
OUT_N = D // UNIT_N
EPS = 1e-6
LN_EPS = 1e-5
NEG = -1e30
SCALE = float(P) ** -0.5
CHUNK = 64
REL = 513

UNITS_ATT = QKVG * PAIRS
UNITS_OUT = 2 * OUT_N
UNIT0 = {"A": 0, "B": UNITS_ATT + UNITS_OUT}
OUTPUT0 = {"A": 0, "B": UNITS_ATT + OUT_N}
DEPTH = 2
HD = 64
HEADS_2 = 16
PAIRS_2 = HEADS_2 // 2
KV_HEADS = 4
ROT = 16
TAPS = 31
TAPS_PADDED = 33
CT = 4
COL = {"val": 0, "glu": 512, "c_gate": 1024, "q": 1536, "k": 2560, "v": 2816, "a_gate": 3072, "r_x": 4096,
       "r_gate": 4608}
U_VAL, U_K, U_V, U_Q, U_RX, U_CGATE, U_AGATE, U_RGATE, U_SMALL, U_OUT, UNITS_2 = 0, 4, 5, 6, 10, 12, 14, 18, 20, 21, 29
O_SMALL, O_OUT, OUTPUTS_2 = 20, 26, 34
LAYER_VECTORS = ["ln_post_g", "ln_post_b", "conv_dw_b", "conv_ln_g", "conv_ln_b", "conv_pw_b", "lru_conv_b", "lru_ba",
                 "lru_bx", "lru_lambda", "lru_conv_w"]
VEC = {"ln_post_g": 0, "ln_post_b": 16, "conv_dw_b": 32, "conv_ln_g": 36, "conv_ln_b": 40, "conv_pw_b": 44,
       "lru_conv_b": 48, "lru_ba": 52, "lru_bx": 56, "lru_lambda": 60, "lru_conv_w": 64}
VEC_ROWS = 80
CONV_ROWS = TAPS * CT
CONV_D = CT * P
ALPHA = (2.0 * DEPTH) ** 0.25
LRU_C = 8.0
UNIT_2 = 2 * (UNITS_ATT + UNITS_OUT)
OUTPUT_2 = 2 * (UNITS_ATT + OUT_N)


def shape_constants():
    q = np.arange(P)[:, None]
    k = np.arange(P)[None, :]
    parts = {}
    parts["ident"] = (q == k).astype(np.float32)
    parts["ones"] = np.ones((P, P), np.float32)
    parts["tri"] = (q <= k).astype(np.float32)
    chunked = np.where(k < (q // CHUNK + 1) * CHUNK, 0.0, NEG).astype(np.float32)
    causal = np.where(k <= q, 0.0, NEG).astype(np.float32)
    seen = np.zeros((P, P), np.float32)
    parts["mask_a"] = np.concatenate([chunked, seen, chunked], 1)
    parts["mask_b"] = np.concatenate([causal, seen, causal], 1)
    meta = np.zeros((P, META), np.float32)
    window = np.where(k > q, 0.0, NEG).astype(np.float32)
    parts["mask_2"] = np.concatenate([meta, causal, meta, window, causal], 1)
    half = ROT // 2
    inv = (np.float32(500000.0) ** (-np.arange(half, dtype=np.float32) / np.float32(half))).astype(np.float32)
    angle = np.arange(T, dtype=np.float32)[None, :] * inv[:, None]
    cos, sin = np.ones((P, T), np.float32), np.zeros((P, T), np.float32)
    partner = np.zeros(HD, int)
    for d in range(ROT):
        partner[d] = d + half if d < half else d - half
        for e in range(2):
            cos[HD * e + d] = np.cos(angle[d % half])
            sin[HD * e + d] = np.sin(angle[d % half]) * (-1.0 if d < half else 1.0)
    parts["cos"], parts["sin"] = cos, sin
    perm = np.zeros((P, P), np.float32)
    spread = np.zeros((2, 2, P, P), np.float32)
    for m in range(P):
        d = m % HD
        if d < ROT:
            perm[HD * (m // HD) + partner[d], m] = 1.0
        for e in range(2):
            spread[e, 0, HD * e + d, m] = 1.0
            if d < ROT:
                spread[e, 1, HD * e + partner[d], m] = 1.0
    parts["perm"] = perm
    parts["spread"] = spread.reshape(4, P, P).transpose(1, 0, 2).reshape(P, 4 * P)
    at, columns = {}, 0
    for name, a in parts.items():
        at[name] = (columns, a.shape[1])
        columns += a.shape[1]
    return at, np.concatenate(list(parts.values()), 1)


class Region:

    def __init__(self, tensor):
        self.tensor, self.at = tensor, 0

    def take(self, *shape):
        n = int(np.prod(shape))
        flat = self.tensor[:, self.at:self.at + n]
        self.at += n
        assert self.at <= self.tensor.shape[1], self.at
        if len(shape) == 1:
            return flat
        names = "abc"[:len(shape)]
        sizes = {x: s for x, s in zip(names, shape)}
        return flat.rearrange(f"p ({' '.join(names)}) -> p {' '.join(names)}", **sizes)


class Steps:

    def __init__(self, engine, sem):
        self.engine, self.sem, self.base, self.done = engine, sem, 0, 0

    def start(self, base):
        self.base, self.done = base, 0

    def __call__(self, instruction):
        instruction.then_inc(self.sem, 1)
        self.done += 1
        self.engine.wait_ge(self.sem, self.base + self.done)


VECTORS = ["a_norm", "b_norm", "kv_norm", "final_norm", "ln_in_g_2", "ln_in_b_2"]


def build_program(nc, io, const_at):
    with ExitStack() as ctx:
        def sb(name, shape, dt=F32):
            return ctx.enter_context(nc.sbuf_tensor(name, shape, dt))

        def sem(name):
            return ctx.enter_context(nc.semaphore(name))

        w_raw = sb("w_raw", [P, PIECES, PK, UNIT_N])
        w_hi = sb("w_hi", [P, PIECES, PK, UNIT_N], F32R)
        w_lo = sb("w_lo", [P, PIECES, PK, UNIT_N], F32R)
        operand = sb("operand", [P, 4 * KT * T], F32R)
        x_res = sb("x_res", [P, KT, T])
        scratch = sb("scratch", [P, 17568])
        consts = sb("consts", [P, 2 * P])
        gains = sb("gains", [P, len(VECTORS) * KT])
        eps = sb("eps", [P, 2])
        proj = ctx.enter_context(nc.psum_tensor("proj", [P, 4, 512], F32))
        ps_s = ctx.enter_context(nc.psum_tensor("ps_s", [P, 2, 512], F32))
        ps_t = ctx.enter_context(nc.psum_tensor("ps_t", [P, 2, 512], F32))
        cum_dram = nc.dram_tensor("cumulative_log_forget", (HEADS, S), F32).ap()

        ident, ones = consts[:, 0:P], consts[:, P:2 * P]
        x1 = x_res[:, :, META:T]
        h_kv = operand[:, 0:KT * 512].rearrange("p (k n) -> p k n", n=512)
        h_q = operand[:, KT * 512:2 * KT * 512].rearrange("p (k n) -> p k n", n=512)
        gated = operand[:, 0:2 * KT * 512].rearrange("p (k n) -> p k n", n=512)

        one = Region(scratch)
        og = one.take(HEADS, S)
        qkvg = [one.take(2, S) for _ in range(QKVG)]
        q_t, k_t, v_t, g_t = qkvg
        part = one.take(2, S)
        bias_raw = one.take(2, S)
        bias = one.take(2, 384)
        scores = one.take(2, 384)
        p_t = one.take(2, 384)
        v_tok = one.take(2, S)
        tanh_g = one.take(2, S)
        sumsq = one.take(2, S)
        norm_mean, norm_root, norm_rstd, norm_spare = (one.take(S + 2) for _ in range(4))
        rstd, rstd_column = norm_rstd[:, 0:S], norm_rstd[:, S:S + 2]
        masks = {"A": one.take(384), "B": one.take(384)}
        tri = one.take(P)
        fb = one.take(2, HEADS)
        cum = one.take(2, HEADS)
        cum_pair = one.take(2, 2)
        row_max = one.take(2, 2)
        row_sum = one.take(2, 2)
        before = p_t.rearrange("p a b -> p (a b)")
        vec_rows = before[:, 0:P]
        gate, gate_t, gate_u = (before[:, P + 2 * HEADS * n:P + 2 * HEADS * (n + 1)]
                                .rearrange("p (t h) -> p t h", t=2) for n in range(3))
        fw = og.rearrange("p h s -> p (h s)")[:, 3 * D:3 * D + KT * HEADS].rearrange("p (k h) -> p k h", k=KT)
        cum_row = bias.rearrange("p a b -> p (a b)")[0:HEADS, 0:S]
        squares = g_t
        x_in = og.rearrange("p (t k) s -> p t (k s)", t=2)[:, :, 0:D]
        fw_hi = sb("fw_hi", [P, KT, HEADS], F32R)
        fw_lo = sb("fw_lo", [P, KT, HEADS], F32R)

        two = Region(scratch)
        slots = two.take(28, T)
        val, a_gates = slots[:, 0:4, :], slots[:, 0:8, :]
        att = slots[:, 8:16, :]
        k_spread = slots[:, 16:20, :]
        c_gates, r_gates = slots[:, 20:24, :], slots[:, 24:28, :]
        rows_in = scratch[:, 24 * T:24 * T + 2 * P].rearrange("p (a b) -> p a b", a=2)
        r_pad = two.take(CT, T + 3)
        c_pad = two.take(CT, T + TAPS_PADDED - 1)
        conv = two.take(CT, T)
        v_space = two.take(3, T)
        v_all = v_space[:, :, 0:KV_HEADS * HD]
        temp0 = two.at
        s2 = two.take(2, 146 + T)
        pt2 = two.take(2, 384)
        ptm = two.take(2, T)
        q_now = two.take(2, T)
        k_now = two.take(T)
        spare = Region(scratch)
        spare.at = temp0
        k_raw = spare.take(2, T)
        v_raw = spare.take(2, T)
        spare.at = temp0
        tanh_2 = spare.take(CT, T)
        rc = spare.take(CT, T)
        tapped = spare.take(CT, T)
        sm = two.take(2, META + 1)
        v_now = two.take(3, HD)
        turn_t = two.take(2, T)
        mask_2 = two.take(2 * META + 3 * P)
        cos, sin = two.take(T), two.take(T)
        perm = two.take(P)
        spread = two.take(4, P)
        sinks = two.take(HEADS_2)
        vec = two.take(VEC_ROWS)
        taps = two.take(TAPS_PADDED * CT)
        lru_c8 = two.take(2, CT)
        small = two.take(4, CT)
        neg_max = two.take(3, 2)
        sums_2 = two.take(3, 2)
        half_ln = two.take(2, CT)
        lru_r, lru_i = slots[:, 8:12, :], slots[:, 12:16, :]
        lru_a, lru_t, lru_v = slots[:, 16:20, :], slots[:, 0:4, :], slots[:, 4:8, :]
        c_stat = v_space
        stats = slots[:, 8:28, :]
        ln_mu, ln_mean, ln_root, ln_rstd, ln_spare = (stats[:, n, :] for n in range(5))
        ln_sums = stats[:, 6:8, :]
        ln_sq = [stats[:, 8:12, :], stats[:, 12:16, :]]
        meta_in = scratch[0:META, 0:D]
        out_rows = scratch[:, 0:2 * D].rearrange("p (t n) -> p t n", t=2)
        in_hi, in_lo, y_hi, y_lo = (operand[:, n * KT * T:(n + 1) * KT * T].rearrange("p (k n) -> p k n", n=T)
                                    for n in range(4))
        raw_landed = [sem(f"raw_landed_{s}") for s in range(PIECES)]
        hi_ready = sem("hi_ready")
        pieces_split = sem("pieces_split")
        pieces_used = sem("pieces_used")
        half_copied = sem("half_copied")
        proj_free = sem("proj_free")
        consts_in = sem("consts_in")
        x_landed = sem("x_landed")
        x_turned = sem("x_turned")
        x_copied = sem("x_copied")
        vec_turned = sem("vec_turned")
        vec_copied = sem("vec_copied")
        squared = sem("squared")
        x_updated = sem("x_updated")
        sumsq_ready = sem("sumsq_ready")
        norm_summed = sem("norm_summed")
        root_ready = sem("root_ready")
        mean_ready = sem("mean_ready")
        rstd_ready = sem("rstd_ready")
        scaled = sem("scaled")
        h_hi = sem("h_hi")
        h_split = sem("h_split")
        fw_hi_ready = sem("fw_hi_ready")
        fw_split = sem("fw_split")
        z_done = sem("z_done")
        gate_exp_in = sem("gate_exp_in")
        gate_exp = sem("gate_exp")
        logf_ready = sem("logf_ready")
        cum_done = sem("cum_done")
        cum_copied = sem("cum_copied")
        cum_stored = sem("cum_stored")
        bias_landed = sem("bias_landed")
        bias_ready = sem("bias_ready")
        cum_picked = sem("cum_picked")
        decay_ready = sem("decay_ready")
        scores_done = sem("scores_done")
        s_added = sem("s_added")
        maxed = sem("maxed")
        negmax_ready = sem("negmax_ready")
        exp_done = sem("exp_done")
        recip_ready = sem("recip_ready")
        p_ready = sem("p_ready")
        turned = sem("turned")
        pt_ready = sem("pt_ready")
        v_tok_ready = sem("v_tok_ready")
        tanh_done = sem("tanh_done")
        silu_ready = sem("silu_ready")
        o_done = sem("o_done")
        og_done = sem("og_done")
        og_hi = sem("og_hi")
        og_split = sem("og_split")
        dve_step = sem("dve_step")
        out_stored = sem("out_stored")

        meta_landed = sem("meta_landed")
        meta_turned = sem("meta_turned")
        meta_copied = sem("meta_copied")
        final_scaled = sem("final_scaled")
        x_normed = sem("x_normed")
        consts_2_in = sem("consts_2_in")
        rows_landed = sem("rows_landed")
        rows_turned = sem("rows_turned")
        rows_copied = sem("rows_copied")
        ln_summable = sem("ln_summable")
        ln_summed = sem("ln_summed")
        ln_mu_ready = sem("ln_mu_ready")
        centred = sem("centred")
        ln_squared = sem("ln_squared")
        ln_sq_used = sem("ln_sq_used")
        ln_mean_ready = sem("ln_mean_ready")
        ln_root_ready = sem("ln_root_ready")
        ln_scaled = sem("ln_scaled")
        affine_act = sem("affine_act")
        affine_scaled = sem("affine_scaled")
        affine_pool = sem("affine_pool")
        in_hi_ready = sem("in_hi_ready")
        in_split = sem("in_split")
        glu_tanh = sem("glu_tanh")
        pads_ready = sem("pads_ready")
        conv_in = sem("conv_in")
        conv_done = sem("conv_done")
        kv_turned = sem("kv_turned")
        k_spread_ready = sem("k_spread_ready")
        v_turned = sem("v_turned")
        v_all_ready = sem("v_all_ready")
        kv_now_ready = sem("kv_now_ready")
        q_turned = sem("q_turned")
        q_now_ready = sem("q_now_ready")
        scores_2_done = sem("scores_2_done")
        neg_max_ready = sem("neg_max_ready")
        exp_2_done = sem("exp_2_done")
        recip_2_ready = sem("recip_2_ready")
        p_2_ready = sem("p_2_ready")
        turned_2 = sem("turned_2")
        pt2_ready = sem("pt2_ready")
        ptm_ready = sem("ptm_ready")
        o_2_done = sem("o_2_done")
        o_2_taken = sem("o_2_taken")
        c_summed = sem("c_summed")
        c_mu_ready = sem("c_mu_ready")
        c_centred = sem("c_centred")
        c_squared = sem("c_squared")
        c_sq_summed = sem("c_sq_summed")
        c_mean_ready = sem("c_mean_ready")
        c_root_ready = sem("c_root_ready")
        c_affine = sem("c_affine")
        gate_tanh = sem("gate_tanh")
        gate_used = sem("gate_used")
        y_ready = sem("y_ready")
        y_hi_ready = sem("y_hi_ready")
        y_split = sem("y_split")
        exp_lam_in = sem("exp_lam_in")
        exp_lam = sem("exp_lam")
        lru_c_ready = sem("lru_c_ready")
        lru_act = sem("lru_act")
        lru_v_ready = sem("lru_v_ready")
        lru_root = sem("lru_root")
        lru_ix = sem("lru_ix")
        conv_tap = sem("conv_tap")
        pair_step = sem("pair_step")
        rc_tap = sem("rc_tap")
        rc_lo = sem("rc_lo")
        rows_turned_out = sem("rows_turned_out")
        copied_out_act = sem("copied_out_act")
        copied_out_dve = sem("copied_out_dve")
        w_of = {
            "A": [io["a_w_in"][0][:, c * INNER:(c + 1) * INNER] for c in range(QKVG)],
            "B": [io["b_w_in"][0][:, 0:INNER], io["kv_w"][:, 0:INNER], io["kv_w"][:, INNER:2 * INNER],
                  io["b_w_in"][0][:, INNER:2 * INNER]],
        }
        w_out_of = {"A": io["a_w_out"][0], "B": io["b_w_out"][0]}
        phases = ("A", "B")

        def gain(vector, k):
            column = VECTORS.index(vector) * KT + k
            return gains[:, column:column + 1]

        pair0 = {"A": 0, "B": PAIRS}

        block = ctx.enter_context(nc.Block())

        @block.sync
        def _(sp):
            def load_unit(unit, w, row0, column):
                for s in range(PIECES):
                    sp.wait_ge(pieces_split, unit * PIECES + s + 1)
                    rows = w[row0 + s * PK * P:row0 + (s + 1) * PK * P, :]
                    src = rows.rearrange("(k p) n -> p k n", p=P)[:, :, bass.ds(column, UNIT_N)]
                    sp.dma_start(w_raw[:, s], src).then_inc(raw_landed[s], 16)

            sp.dma_start(x_in, io["x"][0].rearrange("(t p) n -> p t n", p=P)).then_inc(x_landed, 16)
            load_unit(0, w_of["A"][0], 0, 0)
            c = io["shape_constants"]
            for dst, name in ((consts[:, 0:P], "ident"), (consts[:, P:2 * P], "ones"), (tri, "tri"),
                              (masks["A"], "mask_a"), (masks["B"], "mask_b")):
                at, n = const_at[name]
                sp.dma_start(dst, c[:, at:at + n]).then_inc(consts_in, 16)
            for v, name in enumerate(VECTORS):
                src = io[name]
                src = src[0] if len(src.shape) == 2 else src
                sp.dma_start(vec_rows[v * KT:(v + 1) * KT, :],
                             src.rearrange("(k p) -> k p", p=P)).then_inc(consts_in, 16)
            sp.dma_start(fw, io["f_w"].rearrange("(k p) n -> p k n", p=P)).then_inc(consts_in, 16)
            for t in range(2):
                sp.dma_start(fb[:, t, :], io["f_b"].rearrange("(a n) -> a n", a=1).to_broadcast([P, HEADS]))\
                  .then_inc(consts_in, 16)

            def load_pair(phase, i, last):
                unit = UNIT0[phase] + QKVG * i
                n = pair0[phase] + i
                sp.wait_ge(bias_ready, n + 1)
                if phase == "A":
                    rb = io["a_rel_bias"]
                    src = bass.AP(rb.tensor, rb.offset + 2 * i * REL + (REL - 2 * S + P), [[1, P], [REL, 2], [1, S]])
                else:
                    src = bass.AP(cum_dram.tensor, 2 * i * S, [[0, P], [S, 2], [1, S]])
                sp.dma_start(bias_raw, src).then_inc(bias_landed, 16)
                for c in (2, 3):
                    load_unit(unit + c, w_of[phase][c], 0, i * UNIT_N)
                if not last:
                    for c in (0, 1):
                        load_unit(unit + QKVG + c, w_of[phase][c], 0, (i + 1) * UNIT_N)

            for phase in phases:
                if phase == "A":
                    load_unit(1, w_of[phase][1], 0, 0)
                else:
                    for c in (0, 1):
                        load_unit(UNIT0[phase] + c, w_of[phase][c], 0, 0)
                    sp.wait_ge(cum_copied, 1)
                    sp.dma_start(cum_dram, cum_row).then_inc(cum_stored, 16)
                    sp.wait_ge(cum_stored, 16)
                with sp.Fori(0, PAIRS - 1) as i:
                    load_pair(phase, i, False)
                load_pair(phase, PAIRS - 1, True)
                with sp.Fori(0, OUT_N) as j:
                    for half in range(2):
                        load_unit(UNIT0[phase] + UNITS_ATT + 2 * j + half, w_out_of[phase], half * D, j * UNIT_N)
            sp.wait_ge(og_split, 16)
            sp.dma_start(meta_in, io["meta_tokens_2"]).then_inc(meta_landed, 16)
            load_unit(UNIT_2, io["w_in_2"][0], 0, COL["val"])
            sp.wait_ge(x_normed, 2)
            for dst, name in ((mask_2, "mask_2"), (cos, "cos"), (sin, "sin"), (perm, "perm"),
                              (spread.rearrange("p a b -> p (a b)"), "spread")):
                at, n = const_at[name]
                sp.dma_start(dst, io["shape_constants"][:, at:at + n]).then_inc(consts_2_in, 16)
            w_in = io["w_in_2"].rearrange("l d n -> (l d) n")
            w_out = io["w_out_2"].rearrange("l d n -> (l d) n")

            def load_rows(unit, w, row0, column):
                for s in range(PIECES):
                    sp.wait_ge(pieces_split, unit * PIECES + s + 1)
                    rows = w[bass.ds(row0 + s * PK * P, PK * P), :]
                    src = rows.rearrange("(k p) n -> p k n", p=P)[:, :, bass.ds(column, UNIT_N)]
                    sp.dma_start(w_raw[:, s], src).then_inc(raw_landed[s], 16)

            with sp.Fori(0, DEPTH) as l:
                u0 = UNIT_2 + UNITS_2 * l
                sp.wait_ge(affine_act, 4 * l + 4)
                sp.wait_ge(affine_pool, 4 * l + 4)
                sp.dma_start(rows_in[0:VEC_ROWS, 0, :], io["layer_rows"][bass.ds(l, 1)].rearrange("a r p -> (a r) p"))\
                  .then_inc(rows_landed, 16)
                sp.dma_start(rows_in[0:CONV_ROWS, 1, :], io["conv_rows"][bass.ds(l, 1)].rearrange("a r p -> (a r) p"))\
                  .then_inc(rows_landed, 16)
                sp.dma_start(sinks, io["attn_sinks_2"][bass.ds(l, 1), :].to_broadcast([P, HEADS_2]))\
                  .then_inc(rows_landed, 16)
                for j in (1, 2, 3):
                    load_rows(u0 + j, w_in, l * D, UNIT_N * j)
                load_rows(u0 + U_K, w_in, l * D, COL["k"])
                load_rows(u0 + U_V, w_in, l * D, COL["v"])
                for first, column, count in ((U_Q, COL["q"], 4), (U_RX, COL["r_x"], 2), (U_CGATE, COL["c_gate"], 2),
                                             (U_AGATE, COL["a_gate"], 4), (U_RGATE, COL["r_gate"], 2)):
                    with sp.Fori(0, count) as j:
                        load_rows(u0 + first + j, w_in, l * D, column + j * UNIT_N)
                u = u0 + U_SMALL
                for s in range(2):
                    sp.wait_ge(pieces_split, u * PIECES + s + 1)
                    src = io["conv_pw_w_2"][bass.ds(l, 1)].rearrange("a (k p) n -> p (a k) n", p=P)
                    sp.dma_start(w_raw[:, s], src[:, :, s * UNIT_N:(s + 1) * UNIT_N]).then_inc(raw_landed[s], 16)
                for s in range(2, 4):
                    sp.wait_ge(pieces_split, u * PIECES + s + 1)
                    src = io["lru_blocks"][bass.ds(l, 1)].rearrange("a p t n -> p (a t) n")
                    sp.dma_start(w_raw[:, s, 0:2], src[:, 2 * s - 4:2 * s - 2, :]).then_inc(raw_landed[s], 16)
                with sp.Fori(0, OUT_N) as j:
                    load_rows(u0 + U_OUT + j, w_out, l * D, j * UNIT_N)
                load_rows(u0 + UNITS_2, w_in, l * -D + (DEPTH - 1) * D, COL["val"])
            for c in range(4):
                for t in range(2):
                    sp.wait_ge(copied_out_dve if t == 0 else copied_out_act, c + 1)
                    sp.dma_start(io["out"][0, t * P:(t + 1) * P, c * 512:(c + 1) * 512],
                                 out_rows[:, t, c * 512:(c + 1) * 512]).then_inc(out_stored, 16)
            sp.wait_ge(out_stored, 16 * 8)

        @block.gpsimd
        def _(pool):
            pool.wait_ge(consts_in, 16 * (5 + len(VECTORS) + 3))

            for phase in phases:
                if phase == "B":
                    pool.wait_ge(cum_copied, 1)
                with pool.Fori(0, PAIRS) as i:
                    n = pair0[phase] + i
                    pool.wait_ge(bias_landed, 16 * n + 16)
                    pool.wait_ge(s_added, n + 1)
                    mask = masks[phase]
                    if phase == "B":
                        m = pool.tensor_copy(cum_pair, cum[:, :, bass.ds(2 * i, 2)]).then_inc(cum_picked, 1)
                        pool.wait_ge(cum_picked, i + 1)
                    if phase == "A":
                        for h in range(2):
                            pool.tensor_tensor(bias[:, h, 0:P], bias_raw[:, h, 0:P][:, ::-1], mask[:, 0:P], ALU.add)
                            m = pool.tensor_tensor(bias[:, h, P:384], bias_raw[:, h, :][:, ::-1], mask[:, P:384], ALU.add)
                    else:
                        for t, cols, keys in ((0, slice(0, P), P), (1, slice(P, 384), S)):
                            m = pool.tensor_tensor(bias[:, :, cols], bias_raw[:, :, 0:keys],
                                                   cum_pair[:, t, :].unsqueeze(2).to_broadcast([P, 2, keys]), ALU.add)
                        m.then_inc(decay_ready, 1)
                        pool.wait_ge(decay_ready, i + 1)
                        m = pool.tensor_tensor(bias, bias, mask.unsqueeze(1).to_broadcast([P, 2, 384]), ALU.add)
                    m.then_inc(bias_ready, 1)

            pool.wait_ge(rstd_ready, 3)
            mine = range(2, KT, 3)
            for k in mine:
                m = pool.tensor_tensor(x1[:, k, :], x1[:, k, :], rstd, ALU.mult)
            m.then_inc(final_scaled, 1)
            pool.wait_ge(final_scaled, 1)
            for k in mine:
                m = pool.tensor_scalar(x1[:, k, :], x1[:, k, :], gain("final_norm", k), None, ALU.mult)
            m.then_inc(x_normed, 1)

            def affine_half(n, g, b):
                for c in range(4):
                    pool.wait_ge(ln_scaled, 4 * n + c + 1)
                    rows = slice(4 * c + 2, 4 * c + 4)
                    over_rows = [a[:, rows].unsqueeze(2).to_broadcast([P, 2, T]) for a in (g, b)]
                    pool.tensor_tensor(x_res[:, rows, :], x_res[:, rows, :], over_rows[0], ALU.mult).then_inc(affine_scaled, 1)
                    pool.wait_ge(affine_scaled, 4 * n + c + 1)
                    pool.tensor_tensor(x_res[:, rows, :], x_res[:, rows, :], over_rows[1], ALU.add).then_inc(affine_pool, 1)

            g, b = (gains[:, VECTORS.index(v) * KT:(VECTORS.index(v) + 1) * KT] for v in ("ln_in_g_2", "ln_in_b_2"))
            affine_half(0, g, b)
            pool.wait_ge(x_normed, 2)
            pool.memset(r_pad[:, :, 0:3], 0.0)
            pool.memset(c_pad[:, :, 0:TAPS - 1], 0.0)
            pool.memset(c_pad[:, :, TAPS - 1 + T:T + TAPS_PADDED - 1], 0.0).then_inc(pads_ready, 1)
            with pool.Fori(0, DEPTH) as l:
                with pool.Fori(0, KV_HEADS) as kv:
                    pool.wait_ge(o_2_done, PAIRS_2 * l + 2 * kv + 1)
                    pool.wait_ge(k_spread_ready, KV_HEADS * l + KV_HEADS)
                    pool.wait_ge(v_all_ready, 3 * l + 3)
                    pool.tensor_copy(k_now.unsqueeze(1), k_spread[:, bass.ds(kv, 1), :])
                    pool.tensor_copy(v_now[0:META, 0, :], v_all[0:META, 0, bass.ds(kv * HD, HD)])
                    pool.tensor_copy(v_now[:, 1:3, :], v_all[:, 1:3, bass.ds(kv * HD, HD)]).then_inc(kv_now_ready, 1)
                    for e in range(2):
                        n = PAIRS_2 * l + 2 * kv + e
                        pool.wait_ge(recip_2_ready, n + 1)
                        for rows, dst, part_sums, width in ((P, s2[:, :, 0:144], sums_2[:, 0, :], 144),
                                                            (P, s2[:, :, 146:418], sums_2[:, 1, :], T),
                                                            (META, sm[0:META, :, 0:META], sums_2[0:META, 2, :], META)):
                            m = pool.tensor_tensor(dst, dst, part_sums.unsqueeze(2).to_broadcast([rows, 2, width]), ALU.mult)
                        m.then_inc(p_2_ready, 1)
                pool.wait_ge(o_2_taken, PAIRS_2 * (l + 1) + 1)
                pool.wait_ge(proj_free, OUTPUT_2 + OUTPUTS_2 * l + U_CGATE + 2)
                def tap_of(column):
                    return vec[:, column:column + CT].unsqueeze(2).to_broadcast([P, CT, T])

                w = VEC["lru_conv_w"]
                pool.tensor_tensor(rc, r_pad[:, :, 0:T], tap_of(w), ALU.mult).then_inc(rc_tap, 1)
                pool.wait_ge(rc_tap, 8 * l + 1)
                pool.tensor_tensor(rc, rc, tap_of(VEC["lru_conv_b"]), ALU.add).then_inc(rc_tap, 1)
                for j in range(1, 4):
                    pool.tensor_tensor(tapped, r_pad[:, :, j:j + T], tap_of(w + 4 * j), ALU.mult).then_inc(rc_tap, 1)
                    pool.wait_ge(rc_tap, 8 * l + 2 * j + 1)
                    pool.tensor_tensor(rc, rc, tapped, ALU.add).then_inc(rc_tap, 1)
                    pool.wait_ge(rc_tap, 8 * l + 2 * j + 2)
                pool.wait_ge(proj_free, OUTPUT_2 + OUTPUTS_2 * l + O_OUT + 2)
                pool.tensor_tensor(lru_i, lru_i, rc, ALU.mult).then_inc(lru_ix, 1)
                affine_half(l + 1, vec[:, 0:KT], vec[:, KT:2 * KT])

        @block.scalar
        def _(act):
            act.sem_inc(s_added, 1)
            act.sem_inc(o_2_taken, 1)

            def split_hi(unit, s):
                piece = unit * PIECES + s
                act.wait_ge(raw_landed[s], 16 * unit + 16)
                act.wait_ge(pieces_used, piece + 1)
                act.activation(w_hi[:, s], w_raw[:, s], ACT.Copy).then_inc(hi_ready, 1)

            def copy_half(last_unit, output, bank):
                act.wait_ge(pieces_used, PIECES * (last_unit + 2))
                act.wait_ge(proj_free, output + 2)
                act.activation(part, proj[:, 2 * bank:2 * bank + 2, S:512], ACT.Copy).then_inc(half_copied, 1)

            def root_of(n):
                act.wait_ge(mean_ready, n + 1)
                act.activation(norm_root, norm_mean, ACT.Sqrt).then_inc(root_ready, 1)

            def h_his(vector, dst, pairs):
                for pair_of_tiles in pairs:
                    for k in (2 * pair_of_tiles, 2 * pair_of_tiles + 1):
                        m = act.activation(dst[:, k, 0:S], x1[:, k, :], ACT.Identity, scale=gain(vector, k))
                    m.then_inc(h_hi, 1)

            act.wait_ge(consts_in, 16 * (5 + len(VECTORS) + 3))
            act.activation(fw_hi[:], fw, ACT.Copy).then_inc(fw_hi_ready, 1)
            for s in range(PIECES):
                split_hi(0, s)
            for j in range(KT // 2):
                act.wait_ge(x_copied, j + 1)
                if j == 0:
                    act.wait_ge(vec_copied, 1)
                h_his("a_norm", h_q, (j,))
                if j >= 1:
                    act.wait_ge(sumsq_ready, j)
                act.activation(squares, x1[:, 2 * j:2 * j + 2, :], ACT.Square).then_inc(squared, 1)

            def gated_hi(og0, c):
                act.wait_ge(og_done, og0 + 2 * c + 3)
                act.activation(gated[:, 4 * c:4 * c + 4, 0:S], og[:, 4 * c:4 * c + 4, :], ACT.Copy).then_inc(og_hi, 1)

            def pair(phase, i, last):
                n = pair0[phase] + i
                unit = UNIT0[phase] + QKVG * i
                output = OUTPUT0[phase] + QKVG * i
                for s in range(PIECES):
                    split_hi(unit + 2, s)
                copy_half(unit + 1, output + 1, 1)
                for s in range(PIECES):
                    split_hi(unit + 3, s)
                copy_half(unit + 2, output + 2, 0)
                split_hi(unit + 4, 0)
                split_hi(unit + 4, 1)
                act.wait_ge(negmax_ready, n + 1)
                for h in range(2):
                    for t, (a, b) in enumerate(((0, P), (P, 384))):
                        act.activation(scores[:, h, a:b], scores[:, h, a:b], ACT.Exp, bias=row_max[:, t, h:h + 1],
                                       accum_out=row_sum[:, t, h:h + 1]).then_inc(exp_done, 1)
                split_hi(unit + 4, 2)
                split_hi(unit + 4, 3)
                if last:
                    gated_hi(pair0[phase], 0)
                    gated_hi(pair0[phase], 1)
                copy_half(unit + 3, output + 3, 1)
                act.wait_ge(turned, n + 1)
                act.activation(p_t, ps_t[:, :, 0:384], ACT.Copy).then_inc(pt_ready, 1)
                act.wait_ge(scaled, QKVG * n + 4)
                act.activation(tanh_g, g_t, ACT.Tanh).then_inc(tanh_done, 1)
                if not last:
                    for s in range(PIECES):
                        split_hi(unit + 5, s)
                    copy_half(unit + 4, output + 4, 0)

            for phase in phases:
                r = phases.index(phase)
                if phase == "B":
                    h_his("b_norm", h_q, range(0, 4))
                root_of(r)
                if phase == "B":
                    h_his("b_norm", h_q, range(4, 8))
                    act.wait_ge(gate_exp_in, 1)
                    act.activation(gate_t, gate_u, ACT.Exp, scale=-1.0).then_inc(gate_exp, 1)
                for s in range(PIECES):
                    split_hi(UNIT0[phase] + 1, s)
                copy_half(UNIT0[phase], OUTPUT0[phase], 0)
                with act.Fori(0, PAIRS - 1) as i:
                    pair(phase, i, False)
                pair(phase, PAIRS - 1, True)

                unit = UNIT0[phase] + UNITS_ATT
                og0 = pair0[phase]
                for c in range(8):
                    if 1 <= c < 7:
                        gated_hi(og0, c + 1)
                    split_hi(unit + 1 + c // 4, c % 4)

                def out_update(phase, j, bank, last=False):
                    unit = UNIT0[phase] + UNITS_ATT + 2 * j
                    output = OUTPUT0[phase] + UNITS_ATT + j
                    copy_half(unit + 1, output, bank)
                    act.wait_ge(x_updated, 8 * phases.index(phase) + j + 1)
                    if last and phase == "A":
                        h_his("kv_norm", h_kv, (7,))
                    act.activation(squares, x1[:, bass.ds(2 * j, 2), :], ACT.Square).then_inc(squared, 1)

                out_update(phase, 0, 0)
                with act.Fori(0, (OUT_N - 2) // 2) as m:
                    for jj in range(2):
                        j = 2 * m + 1 + jj
                        u = unit + 2 * j
                        for half in range(2):
                            for s in range(PIECES):
                                split_hi(u + 1 + half, s)
                        out_update(phase, j, (1 + jj) % 2)
                j = OUT_N - 1
                u = unit + 2 * j
                for s in range(PIECES):
                    split_hi(u + 1, s)
                if phase == "A":
                    act.wait_ge(pieces_used, PIECES * (u + 2))
                for s in range(PIECES):
                    if phase == "A":
                        h_his("kv_norm", h_kv, (2 * s, 2 * s + 1) if s < 3 else (6,))
                    split_hi(u + 2, s)
                out_update(phase, j, 1, last=True)

            root_of(2)

            def layer_norm(n, g, b):
                act.wait_ge(ln_summed, n + 1)
                act.activation(ln_mu, ps_t[:, 0, 0:T], ACT.Copy, scale=1.0 / D).then_inc(ln_mu_ready, 1)
                for c in range(4):
                    act.wait_ge(centred, 4 * n + c + 1)
                    if c >= 2:
                        act.wait_ge(ln_sq_used, 4 * n + c - 1)
                    act.activation(ln_sq[c % 2], x_res[:, 4 * c:4 * c + 4, :], ACT.Square).then_inc(ln_squared, 1)
                act.wait_ge(ln_mean_ready, n + 1)
                act.activation(ln_root, ln_mean, ACT.Sqrt).then_inc(ln_root_ready, 1)
                for c in range(4):
                    act.wait_ge(ln_scaled, 4 * n + c + 1)
                    for k in (4 * c, 4 * c + 1):
                        m = act.activation(x_res[:, k, :], x_res[:, k, :], ACT.Identity, scale=g[:, k:k + 1], bias=b[:, k:k + 1])
                    m.then_inc(affine_act, 1)

            g, b = (gains[:, VECTORS.index(v) * KT:(VECTORS.index(v) + 1) * KT] for v in ("ln_in_g_2", "ln_in_b_2"))
            layer_norm(0, g, b)

            def copy_output(unit, output, bank, dst, scale=1.0):
                act.wait_ge(pieces_used, PIECES * (unit + 2))
                act.wait_ge(proj_free, output + 2)
                act.activation(dst, proj[:, 2 * bank:2 * bank + 2, 0:T], ACT.Copy, scale=scale).then_inc(proj_free, 1)

            def hi_of(dst, src):
                act.activation(dst, src, ACT.Copy).then_inc(y_hi_ready, 1)

            with act.Fori(0, DEPTH) as l:
                u0 = UNIT_2 + UNITS_2 * l
                o0 = OUTPUT_2 + OUTPUTS_2 * l
                for c in range(4):
                    act.wait_ge(affine_act, 4 * l + c + 1)
                    act.wait_ge(affine_pool, 4 * l + c + 1)
                    act.activation(in_hi[:, 4 * c:4 * c + 4, :], x_res[:, 4 * c:4 * c + 4, :], ACT.Copy).then_inc(in_hi_ready, 1)
                act.wait_ge(exp_lam_in, l + 1)
                act.activation(small[:, 1, :], small[:, 0, :], ACT.Exp, scale=-1.0).then_inc(exp_lam, 1)
                for j in range(4):
                    for s in range(PIECES):
                        split_hi(u0 + j + 1, s)
                    copy_output(u0 + j, o0 + j, j % 2, slots[:, 2 * j:2 * j + 2, :], 0.5)
                act.wait_ge(proj_free, o0 + 4 + 2)
                act.activation(tanh_2, slots[:, 4:8, :], ACT.Tanh).then_inc(glu_tanh, 1)
                act.wait_ge(conv_in, l + 1)
                for j in range(4, 10):
                    for s in range(PIECES):
                        split_hi(u0 + j + 1, s)
                    dst = k_raw if j == U_K else v_raw if j == U_V else slots[:, 8 + 2 * (j - U_Q):10 + 2 * (j - U_Q), :]
                    copy_output(u0 + j, o0 + j, j % 2, dst)

                def exponentials(n):
                    act.wait_ge(neg_max_ready, n + 1)
                    for h in range(2):
                        act.activation(s2[:, h, 0:145], s2[:, h, 0:145], ACT.Exp, bias=neg_max[:, 0, h:h + 1],
                                       accum_out=sums_2[:, 0, h:h + 1])
                        act.activation(s2[:, h, 145:418], s2[:, h, 145:418], ACT.Exp, bias=neg_max[:, 1, h:h + 1],
                                       accum_out=sums_2[:, 1, h:h + 1])
                        m = act.activation(sm[0:META, h, :], sm[0:META, h, :], ACT.Exp, bias=neg_max[0:META, 2, h:h + 1],
                                           accum_out=sums_2[0:META, 2, h:h + 1])
                    m.then_inc(exp_2_done, 1)

                def attention_turn(kv, u, j, dst_of):
                    for e in range(2):
                        n = PAIRS_2 * l + 2 * kv + e
                        split_hi(u + e + 1, 0)
                        if e == 1:
                            act.wait_ge(o_2_done, n + 1)
                            act.activation(att[:, bass.ds(2 * kv, 1), :], ps_t[:, 0:1, 0:T], ACT.Copy).then_inc(o_2_taken, 1)
                            copy_output(u, j, 0, *dst_of(0))
                        exponentials(n)
                        for s in range(1, PIECES):
                            split_hi(u + e + 1, s)
                        act.wait_ge(turned_2, n + 1)
                        act.activation(pt2, ps_t[:, :, 0:384], ACT.Copy).then_inc(pt2_ready, 1)
                    copy_output(u + 1, j + 1, 1, *dst_of(1))
                    act.wait_ge(o_2_done, n + 2)
                    act.activation(att[:, bass.ds(2 * kv + 1, 1), :], ps_t[:, 0:1, 0:T], ACT.Copy).then_inc(o_2_taken, 1)

                attention_turn(0, u0 + U_RX, o0 + U_RX, lambda e: (r_pad[:, 2 * e:2 * e + 2, 3:3 + T], 1.0))
                attention_turn(1, u0 + U_CGATE, o0 + U_CGATE, lambda e: (c_gates[:, 2 * e:2 * e + 2, :], 0.5))
                with act.Fori(0, 2) as m2:
                    attention_turn(m2 + 2, u0 + U_AGATE + 2 * m2, o0 + U_AGATE + 2 * m2,
                                   lambda e: (a_gates[:, bass.ds(4 * m2 + 2 * e, 2), :], 0.5))

                def gate_tanhs(count, src):
                    if count:
                        act.wait_ge(gate_used, 5 * l + count)
                    act.activation(tanh_2, src, ACT.Tanh).then_inc(gate_tanh, 1)

                u, o = u0 + U_RGATE, o0 + U_RGATE
                act.wait_ge(c_summed, l + 1)
                act.activation(c_stat[:, 0, :], ps_s[:, 0, 0:T], ACT.Copy, scale=1.0 / CONV_D).then_inc(c_mu_ready, 1)
                act.wait_ge(proj_free, o + 2)
                gate_tanhs(0, a_gates[:, 0:4, :])
                act.wait_ge(c_centred, l + 1)
                act.activation(lru_a, conv, ACT.Square).then_inc(c_squared, 1)
                split_hi(u + 1, 0)
                split_hi(u + 1, 1)
                act.wait_ge(y_ready, 4 * l + 1)
                hi_of(y_hi[:, 4:8, :], att[:, 0:4, :])
                split_hi(u + 1, 2)
                gate_tanhs(1, a_gates[:, 4:8, :])
                split_hi(u + 1, 3)
                copy_output(u, o, 0, r_gates[:, 0:2, :], 0.5)
                act.wait_ge(c_mean_ready, l + 1)
                act.activation(c_stat[:, 2, :], c_stat[:, 1, :], ACT.Sqrt).then_inc(c_root_ready, 1)
                split_hi(u + 2, 0)
                act.wait_ge(y_ready, 4 * l + 2)
                hi_of(y_hi[:, 8:12, :], att[:, 4:8, :])
                act.wait_ge(rc_tap, 8 * l + 8)
                hi_of(y_hi[:, 12:16, :], rc)
                split_hi(u + 2, 1)
                act.wait_ge(c_affine, l + 1)
                gate_tanhs(2, conv)
                act.wait_ge(gate_used, 5 * l + 3)
                hi_of(y_hi[:, 0:4, :], conv)
                gate_tanhs(3, c_gates)
                for s in range(2, 4):
                    piece = (u + 2) * PIECES + s
                    act.wait_ge(raw_landed[s], 16 * (u + 2) + 16)
                    act.wait_ge(pieces_used, piece + 1)
                    act.activation(w_hi[:, s, 0:2], w_raw[:, s, 0:2], ACT.Copy).then_inc(hi_ready, 1)
                copy_output(u + 1, o + 1, 1, r_gates[:, 2:4, :], 0.5)
                act.wait_ge(proj_free, o + 1 + 3)
                gate_tanhs(4, r_gates)
                u, o = u0 + U_SMALL, o0 + O_SMALL
                for s in range(PIECES):
                    act.wait_ge(pieces_used, PIECES * (u + 1) + s + 1)
                    if s < 2:
                        act.wait_ge(proj_free, o + s + 2)
                        for t in range(2):
                            col = VEC["conv_pw_b"] + 2 * s + t
                            m = act.activation(conv[:, 2 * s + t, :], proj[:, 2 * s + t, 0:T], ACT.Identity,
                                               bias=vec[:, col:col + 1])
                        m.then_inc(proj_free, 1)
                    else:
                        for t in (2 * s - 4, 2 * s - 3):
                            act.wait_ge(proj_free, o + 2 + t + 2)
                            bank = t % 2
                            act.activation(lru_r[:, t, :], proj[:, 2 * bank, 0:T], ACT.Sigmoid,
                                           bias=vec[:, VEC["lru_ba"] + t:VEC["lru_ba"] + t + 1])
                            act.activation(lru_i[:, t, :], proj[:, 2 * bank + 1, 0:T], ACT.Sigmoid,
                                           bias=vec[:, VEC["lru_bx"] + t:VEC["lru_bx"] + t + 1]).then_inc(proj_free, 1)
                    if s == 1:
                        act.wait_ge(y_ready, 4 * l + 3)
                        hi_of(y_hi[:, 0:4, :], conv)
                act.wait_ge(lru_c_ready, l + 1)
                act.wait_ge(proj_free, o + 6 + 2)
                for t in range(CT):
                    act.activation(lru_a[:, t, :], lru_r[:, t, :], ACT.Exp, scale=lru_c8[:, 1, t:t + 1])
                    m = act.activation(lru_t[:, t, :], lru_r[:, t, :], ACT.Tanh, scale=lru_c8[:, 0, t:t + 1])
                m.then_inc(lru_act, 1)
                split_hi(u + 1, 0)
                act.wait_ge(lru_v_ready, l + 1)
                act.activation(lru_v, lru_v, ACT.Sqrt).then_inc(lru_root, 1)
                for s in range(1, PIECES):
                    split_hi(u + 1, s)
                act.wait_ge(y_ready, 4 * l + 4)
                hi_of(y_hi[:, 12:16, :], lru_t)
                with act.Fori(0, OUT_N) as j:
                    for s in range(PIECES):
                        split_hi(u0 + U_OUT + 1 + j, s)
                layer_norm(l + 1, vec[:, 0:KT], vec[:, KT:2 * KT])
            for c in range(4):
                act.wait_ge(rows_turned_out, 2 * c + 2)
                act.activation(out_rows[:, 1, c * 512:(c + 1) * 512], proj[:, (2 * c + 1) % 4, :], ACT.Copy)\
                   .then_inc(copied_out_act, 1)

        @block.tensor
        def _(pe):
            pe.sem_inc(pieces_used, PIECES)
            pe.sem_inc(o_2_done, 1)

            def multiply(unit, bank, rhs, first=True, last=True, chunk_wait=None):
                for s in range(PIECES):
                    pe.wait_ge(pieces_split, unit * PIECES + s + 1 + PIECES)
                    if chunk_wait is not None:
                        chunk_wait(s)
                    for kk in range(PK):
                        k = s * PK + kk
                        for t in range(2):
                            cols = slice(t * P, (t + 1) * P)
                            end = k == KT - 1
                            pe.matmul(proj[:, 2 * bank + t, :], w_hi[:, s, kk, cols], rhs[:, k, :],
                                      start=first and k == 0, stop=False)
                            m = pe.matmul(proj[:, 2 * bank + t, 0:S], w_lo[:, s, kk, cols], rhs[:, k, 0:S],
                                          start=False, stop=last and end)
                    m.then_inc(pieces_used, 1)

            def norm_sum(n, ready):
                pe.wait_ge(sumsq_ready, ready)
                pe.matmul(ps_t[:, 0, 0:S], ones, sumsq[:, 0, :], start=True, stop=False)
                pe.matmul(ps_t[:, 0, 0:S], ones, sumsq[:, 1, :], start=False, stop=True)
                for t in range(2):
                    for a in range(2):
                        m = pe.matmul(ps_t[:, 1, t:t + 1], sumsq[:, a, t * P:(t + 1) * P], ones[:, 0:1], start=a == 0, stop=a == 1)
                m.then_inc(norm_summed, 1)

            pe.wait_ge(consts_in, 16 * (5 + len(VECTORS) + 3))
            pe.transpose(ps_s[:, 0, 0:len(VECTORS) * KT], vec_rows[0:len(VECTORS) * KT, :],
                         ident[0:len(VECTORS) * KT, 0:len(VECTORS) * KT]).then_inc(vec_turned, 1)
            pe.wait_ge(x_landed, 16)
            for j in range(KT // 2):
                if j >= 4:
                    pe.wait_ge(x_copied, j - 3)
                for kk in range(2):
                    for t in range(2):
                        k = 2 * j + kk
                        m = pe.transpose(proj[:, j % 4, kk * S + t * P:kk * S + (t + 1) * P],
                                         x_in[:, t, k * P:(k + 1) * P], ident)
                m.then_inc(x_turned, 1)

            def pair(phase, i, last):
                n = pair0[phase] + i
                unit = UNIT0[phase] + QKVG * i
                output = OUTPUT0[phase] + QKVG * i
                other = h_q if phase == "A" else h_kv
                pe.wait_ge(proj_free, output + 2)
                multiply(unit + 1, 1, other)
                pe.wait_ge(proj_free, output + 3)
                multiply(unit + 2, 0, other)
                pe.wait_ge(scaled, QKVG * n + 2)
                pe.wait_ge(og_done, n + 1)
                for h in range(2):
                    pe.matmul(ps_s[:, h, 0:P], q_t[:, h, 0:P], k_t[:, h, 0:P], start=True, stop=True)
                    m = pe.matmul(ps_s[:, h, P:384], q_t[:, h, P:S], k_t[:, h, :], start=True, stop=True)
                m.then_inc(scores_done, 1)
                multiply(unit + 3, 1, h_q)
                pe.wait_ge(scaled, QKVG * n + 3)
                pe.wait_ge(p_ready, n + 1)
                for h in range(2):
                    for c in range(3):
                        pe.transpose(ps_t[:, h, c * P:(c + 1) * P], scores[:, h, (0, P, 2 * P)[c]:(0, P, 2 * P)[c] + P], ident)
                    for t in range(2):
                        m = pe.transpose(ps_s[:, h, t * P:(t + 1) * P], v_t[:, h, t * P:(t + 1) * P], ident)
                m.then_inc(turned, 1)
                if not last:
                    pe.wait_ge(proj_free, output + 5)
                    multiply(unit + 4, 0, h_q)
                    values(n)

            def values(n):
                pe.wait_ge(pt_ready, n + 1)
                pe.wait_ge(v_tok_ready, n + 1)
                for h in range(2):
                    pe.matmul(ps_s[:, h, 0:S], v_tok[:, h, 0:P], p_t[:, h, 0:S], start=True, stop=False)
                    m = pe.matmul(ps_s[:, h, P:S], v_tok[:, h, P:S], p_t[:, h, S:384], start=False, stop=True)
                m.then_inc(o_done, 1)

            def gates():
                pe.wait_ge(fw_split, 1)
                for k in range(KT):
                    if k % 2 == 0:
                        pe.wait_ge(h_split, KT // 2 + k // 2 + 1)
                    for t in range(2):
                        hi = h_kv[:, k, t * P:(t + 1) * P]
                        lo = h_kv[:, k, S + t * P:S + (t + 1) * P]
                        out = ps_s[:, t, 0:HEADS]
                        pe.matmul(out, hi, fw_hi[:, k, :], start=k == 0, stop=False)
                        pe.matmul(out, hi, fw_lo[:, k, :], start=False, stop=False)
                        m = pe.matmul(out, lo, fw_hi[:, k, :], start=False, stop=k == KT - 1)
                m.then_inc(z_done, 1)

            def running_sums():
                pe.wait_ge(logf_ready, 1)
                pe.matmul(ps_s[:, 0, 0:HEADS], tri, gate[:, 0, :], start=True, stop=True)
                pe.matmul(ps_s[:, 0, HEADS:2 * HEADS], ones, gate[:, 0, :], start=True, stop=False)
                pe.matmul(ps_s[:, 0, HEADS:2 * HEADS], tri, gate[:, 1, :], start=False, stop=True)
                pe.matmul(ps_s[0:HEADS, 1, 0:P], gate[:, 0, :], tri, start=True, stop=True)
                pe.matmul(ps_s[0:HEADS, 1, P:S], gate[:, 0, :], ones, start=True, stop=False)
                pe.matmul(ps_s[0:HEADS, 1, P:S], gate[:, 1, :], tri, start=False, stop=True).then_inc(cum_done, 1)

            for phase in phases:
                r = phases.index(phase)
                if phase == "B":
                    gates()
                else:
                    pe.wait_ge(x_copied, KT // 2 - 2)
                h0 = 0 if phase == "A" else KT
                pe.wait_ge(proj_free, OUTPUT0[phase] + 1)

                def first_wait(s):
                    if s == (2 if phase == "A" else 1):
                        norm_sum(r, 8 * (r + 1))
                    pe.wait_ge(h_split, h0 + 2 * s + 2)

                multiply(UNIT0[phase], 0, h_q, chunk_wait=first_wait)
                if phase == "B":
                    running_sums()
                with pe.Fori(0, PAIRS - 1) as i:
                    pair(phase, i, False)
                pair(phase, PAIRS - 1, True)

                def halves(j, bank, peeled=False):
                    unit = UNIT0[phase] + UNITS_ATT + 2 * j
                    pe.wait_ge(proj_free, OUTPUT0[phase] + UNITS_ATT + j + 1)

                    def first_wait(s):
                        if s == 1:
                            values(pair0[phase] + PAIRS - 1)
                        pe.wait_ge(og_split, 8 * r + s + 1)

                    multiply(unit, bank, gated[:, 0:KT], last=False, chunk_wait=first_wait if peeled else None)
                    wait = (lambda s: pe.wait_ge(og_split, 8 * r + 4 + s + 1)) if peeled else None
                    multiply(unit + 1, bank, gated[:, KT:2 * KT], first=False, chunk_wait=wait)

                halves(0, 0, peeled=True)
                with pe.Fori(0, (OUT_N - 2) // 2) as m:
                    for jj in range(2):
                        halves(2 * m + 1 + jj, (1 + jj) % 2)
                halves(OUT_N - 1, 1)

            norm_sum(2, 24)
            pe.wait_ge(meta_landed, 16)
            for k in range(KT):
                m = pe.transpose(ps_s[:, 0, k * META:(k + 1) * META], meta_in[:, k * P:(k + 1) * P], ident[0:META, 0:META])
            m.then_inc(meta_turned, 1)

            def layer_norm_sums(n, summable):
                pe.wait_ge(ln_summable, summable)
                pe.matmul(ps_t[:, 0, 0:T], ones, ln_sums[:, 0, :], start=True, stop=False)
                pe.matmul(ps_t[:, 0, 0:T], ones, ln_sums[:, 1, :], start=False, stop=True).then_inc(ln_summed, 1)
                for c in range(4):
                    pe.wait_ge(ln_squared, 4 * n + c + 1)
                    for k in range(4):
                        m = pe.matmul(ps_t[:, 1, 0:T], ones, ln_sq[c % 2][:, k, :], start=c + k == 0, stop=c + k == 6)
                    m.then_inc(ln_sq_used, 1)

            layer_norm_sums(0, 1)

            def products(bank, t, s, kk, cols, hi, lo, first, last):
                out = proj[:, 2 * bank + t, 0:T]
                pe.matmul(out, w_hi[:, s, kk, cols], hi, start=first, stop=False)
                pe.matmul(out, w_hi[:, s, kk, cols], lo, start=False, stop=False)
                return pe.matmul(out, w_lo[:, s, kk, cols], hi, start=False, stop=last)

            def multiply_piece(unit, bank, s, hi, lo, chunk_wait=None):
                pe.wait_ge(pieces_split, unit * PIECES + s + 1 + PIECES)
                if chunk_wait is not None:
                    chunk_wait(s)
                for kk in range(PK):
                    k = s * PK + kk
                    for t in range(2):
                        m = products(bank, t, s, kk, slice(t * P, (t + 1) * P), hi[:, k, :], lo[:, k, :], k == 0, k == KT - 1)
                m.then_inc(pieces_used, 1)

            def multiply_2(unit, output, bank, hi, lo, chunk_wait=None):
                pe.wait_ge(proj_free, output + 1)
                for s in range(PIECES):
                    multiply_piece(unit, bank, s, hi, lo, chunk_wait)

            with pe.Fori(0, DEPTH) as l:
                u0 = UNIT_2 + UNITS_2 * l
                o0 = OUTPUT_2 + OUTPUTS_2 * l
                pe.wait_ge(rows_landed, 48 * l + 48)
                pe.transpose(ps_s[:, 0, 0:VEC_ROWS], rows_in[0:VEC_ROWS, 0, :], ident[0:VEC_ROWS, 0:VEC_ROWS])
                pe.transpose(ps_s[:, 1, 0:CONV_ROWS], rows_in[0:CONV_ROWS, 1, :], ident[0:CONV_ROWS, 0:CONV_ROWS])\
                  .then_inc(rows_turned, 1)
                for j in range(U_K):
                    wait = (lambda s: pe.wait_ge(in_split, 4 * l + s + 1)) if j == 0 else None
                    multiply_2(u0 + j, o0 + j, j % 2, in_hi, in_lo, wait)
                multiply_2(u0 + U_K, o0 + U_K, 0, in_hi, in_lo)
                multiply_2(u0 + U_V, o0 + U_V, 1, in_hi, in_lo)
                pe.wait_ge(consts_2_in, 16 * 5)
                for r in range(2):
                    if r == 0:
                        pe.wait_ge(proj_free, o0 + U_K + 3)
                    else:
                        pe.wait_ge(k_spread_ready, KV_HEADS * l + 2)
                    for e, banks in ((0, ps_s), (1, ps_t)):
                        for turned_side in range(2):
                            m = pe.matmul(banks[:, turned_side, 0:T], spread[:, 2 * e + turned_side, :], k_raw[:, r, :],
                                          start=True, stop=True)
                        m.then_inc(kv_turned, 1)
                    multiply_2(u0 + U_Q + r, o0 + U_Q + r, r % 2, in_hi, in_lo)
                pe.wait_ge(k_spread_ready, KV_HEADS * l + 4)
                pe.wait_ge(proj_free, o0 + U_V + 3)
                for t in range(2):
                    pe.transpose(ps_s[0:META, 0, t * P:(t + 1) * P], v_raw[:, t, 0:META], ident)
                    for r in range(2):
                        m = pe.transpose(ps_t[:, r, t * P:(t + 1) * P], v_raw[:, t, META + r * P:META + (r + 1) * P], ident)
                m.then_inc(v_turned, 1)
                for r in range(2, 4):
                    multiply_2(u0 + U_Q + r, o0 + U_Q + r, r % 2, in_hi, in_lo)

                def turn_probabilities(n):
                    pe.wait_ge(p_2_ready, n + 1)
                    pe.wait_ge(o_2_taken, n + 1)
                    for h in range(2):
                        pe.transpose(ps_t[:, h, 0:P], s2[:, h, META:144], ident)
                        pe.transpose(ps_t[:, h, P:2 * P], s2[:, h, 162:290], ident)
                        pe.transpose(ps_t[:, h, 2 * P:3 * P], s2[:, h, 290:418], ident)
                        pe.transpose(ps_s[0:META, h, 0:META], sm[0:META, h, 0:META], ident[0:META, 0:META])
                        pe.transpose(ps_s[0:META, h, META:144], s2[:, h, 0:META], ident)
                        m = pe.transpose(ps_s[0:META, h, 144:T], s2[:, h, 146:162], ident)
                    m.then_inc(turned_2, 1)

                def head_values(n):
                    pe.wait_ge(pt2_ready, n + 1)
                    pe.wait_ge(ptm_ready, n + 1)
                    for h in range(2):
                        out = ps_t[HD * h:HD * h + HD, 0, :]
                        pe.matmul(out[:, 0:T], v_now[0:META, 0, :], ptm[0:META, h, :], start=True, stop=False)
                        pe.matmul(out[:, META:T], v_now[:, 1, :], pt2[:, h, 0:2 * P], start=False, stop=False)
                        m = pe.matmul(out[:, META + P:T], v_now[:, 2, :], pt2[:, h, 2 * P:3 * P], start=False, stop=True)
                    m.then_inc(o_2_done, 1)

                def attention_turn(kv, u, o):
                    for e in range(2):
                        m = pe.matmul(ps_s[:, e, 0:T], perm, att[:, bass.ds(2 * kv + e, 1), :], start=True, stop=True)
                    m.then_inc(q_turned, 1)
                    turn = KV_HEADS * l + kv
                    for e in range(2):
                        n = PAIRS_2 * l + 2 * kv + e
                        pe.wait_ge(proj_free, o + e + 1)
                        multiply_piece(u + e, e, 0, in_hi, in_lo)
                        if e == 1:
                            head_values(n - 1)
                        pe.wait_ge(q_now_ready, turn + 1)
                        pe.wait_ge(kv_now_ready, turn + 1)
                        for h in range(2):
                            rows = slice(HD * h, HD * h + HD)
                            q, k = q_now[rows, e, :], k_now[rows, :]
                            pe.matmul(ps_s[:, h, 0:144], q[:, META:META + P], k[:, 0:META + P], start=True, stop=True)
                            pe.matmul(ps_s[:, h, 144:416], q[:, META + P:T], k, start=True, stop=True)
                            m = pe.matmul(ps_s[0:META, h, 416:432], q[:, 0:META], k[:, 0:META], start=True, stop=True)
                        m.then_inc(scores_2_done, 1)
                        for s in range(1, PIECES):
                            multiply_piece(u + e, e, s, in_hi, in_lo)
                        turn_probabilities(n)
                    head_values(n)

                pe.wait_ge(proj_free, o0 + U_RX + 2)
                pe.wait_ge(v_all_ready, 3 * l + 3)
                for kv, first in ((0, U_RX), (1, U_CGATE)):
                    attention_turn(kv, u0 + first, o0 + first)
                with pe.Fori(0, 2) as m2:
                    attention_turn(m2 + 2, u0 + U_AGATE + 2 * m2, o0 + U_AGATE + 2 * m2)

                pe.wait_ge(conv_done, l + 1)
                for t in range(CT):
                    m = pe.matmul(ps_s[:, 0, 0:T], ones, conv[:, t, :], start=t == 0, stop=t == CT - 1)
                m.then_inc(c_summed, 1)
                multiply_2(u0 + U_RGATE, o0 + U_RGATE, 0, in_hi, in_lo)
                pe.wait_ge(c_squared, l + 1)
                for t in range(CT):
                    m = pe.matmul(ps_s[:, 1, 0:T], ones, lru_a[:, t, :], start=t == 0, stop=t == CT - 1)
                m.then_inc(c_sq_summed, 1)
                multiply_2(u0 + U_RGATE + 1, o0 + U_RGATE + 1, 1, in_hi, in_lo)

                u, o = u0 + U_SMALL, o0 + O_SMALL
                for s in range(2):
                    pe.wait_ge(pieces_split, u * PIECES + s + 1 + PIECES)
                    pe.wait_ge(proj_free, o + s + 1)
                    pe.wait_ge(y_split, 6 * l + 4)
                    for kk in range(CT):
                        for t in range(2):
                            m = products(s, t, s, kk, slice(t * P, (t + 1) * P), y_hi[:, kk, :], y_lo[:, kk, :],
                                         kk == 0, kk == CT - 1)
                    m.then_inc(pieces_used, 1)
                for s in range(2, 4):
                    pe.wait_ge(pieces_split, u * PIECES + s + 1 + PIECES)
                    for tt in range(2):
                        tile = 2 * s - 4 + tt
                        pe.wait_ge(proj_free, o + 2 + tile + 1)
                        for gate_side in range(2):
                            m = products(tile % 2, gate_side, s, tt, slice(gate_side * P, (gate_side + 1) * P),
                                         y_hi[:, 12 + tile, :], y_lo[:, 12 + tile, :], True, True)
                    m.then_inc(pieces_used, 1)
                splits = (5, 5, 5, 6)
                multiply_2(u0 + U_OUT, o0 + O_OUT, 0, y_hi, y_lo, lambda s: pe.wait_ge(y_split, 6 * l + splits[s]))
                with pe.Fori(0, (OUT_N - 2) // 2) as m3:
                    for jj in range(2):
                        j = 2 * m3 + 1 + jj
                        multiply_2(u0 + U_OUT + j, o0 + O_OUT + j, (1 + jj) % 2, y_hi, y_lo)
                multiply_2(u0 + U_OUT + OUT_N - 1, o0 + O_OUT + OUT_N - 1, 1, y_hi, y_lo)
                layer_norm_sums(l + 1, OUT_N * l + OUT_N + 1)
            for c in range(4):
                pe.wait_ge(affine_act, 4 * DEPTH + c + 1)
                pe.wait_ge(affine_pool, 4 * DEPTH + c + 1)
                for t in range(2):
                    bank = (2 * c + t) % 4
                    if c >= 2:
                        pe.wait_ge(copied_out_dve if t == 0 else copied_out_act, c - 1)
                    for kk in range(4):
                        m = pe.transpose(proj[:, bank, kk * P:(kk + 1) * P],
                                         x_res[:, 4 * c + kk, META + t * P:META + (t + 1) * P], ident)
                    m.then_inc(rows_turned_out, 1)

        @block.vector
        def _(dve):
            step = Steps(dve, dve_step)
            dve.sem_inc(pieces_split, PIECES)
            dve.sem_inc(proj_free, 2)
            dve.sem_inc(og_done, 1)
            dve.sem_inc(bias_ready, 1)

            def split_lo(unit, s):
                dve.wait_ge(hi_ready, unit * PIECES + s + 1)
                dve.tensor_tensor(w_lo[:, s], w_raw[:, s], w_hi[:, s].bitcast(F32), ALU.subtract).then_inc(pieces_split, 1)

            def take_output(output, bank, dst):
                dve.wait_ge(half_copied, output + 1)
                dve.tensor_tensor(dst, proj[:, 2 * bank:2 * bank + 2, 0:S], part, ALU.add).then_inc(proj_free, 1)

            def take_scaled(output, bank, dst, scale=1.0):
                take_output(output, bank, dst)
                dve.wait_ge(proj_free, output + 3)
                dve.scalar_tensor_tensor(dst, dst, scale, rstd.unsqueeze(1).to_broadcast([P, 2, S]), ALU.mult, ALU.mult)\
                   .then_inc(scaled, 1)

            def refine(rstd, mean, spare):
                step(dve.tensor_tensor(spare, mean, rstd, ALU.mult))
                step(dve.scalar_tensor_tensor(spare, spare, -0.5, rstd, ALU.mult, ALU.mult))
                return dve.scalar_tensor_tensor(rstd, spare, 1.5, rstd, ALU.add, ALU.mult)

            def mean_squares(n):
                dve.wait_ge(norm_summed, n + 1)
                dve.tensor_scalar(norm_mean[:, 0:S], ps_t[:, 0, 0:S], 1.0 / D, EPS, ALU.mult, ALU.add)
                dve.tensor_scalar(norm_mean[:, S:S + 2], ps_t[:, 1, 0:2], 1.0 / D, EPS, ALU.mult, ALU.add).then_inc(mean_ready, 1)

            def reciprocal_of_root(n):
                dve.wait_ge(root_ready, n + 1)
                step(dve.reciprocal(norm_rstd, norm_root))
                refine(norm_rstd, norm_mean, norm_spare).then_inc(rstd_ready, 1)
                dve.wait_ge(rstd_ready, n + 1)

            def h_los(first, vector, dst, pairs):
                for pair_of_tiles in pairs:
                    dve.wait_ge(h_hi, first + pair_of_tiles + 1)
                    for k in (2 * pair_of_tiles, 2 * pair_of_tiles + 1):
                        m = dve.scalar_tensor_tensor(dst[:, k, S:512], x1[:, k, :], gain(vector, k),
                                                     dst[:, k, 0:S].bitcast(F32), ALU.mult, ALU.subtract)
                    m.then_inc(h_split, 1)

            dve.memset(eps[:, 0:1], EPS).then_inc(dve_step, 1)
            dve.memset(eps[:, 1:2], LN_EPS).then_inc(dve_step, 1)
            step(dve.memset(sumsq, 0.0))
            dve.wait_ge(dve_step, 3)
            step.start(3)
            dve.wait_ge(fw_hi_ready, 1)
            dve.tensor_tensor(fw_lo[:], fw, fw_hi[:].bitcast(F32), ALU.subtract).then_inc(fw_split, 1)
            for s in range(PIECES):
                split_lo(0, s)
            dve.wait_ge(vec_turned, 1)
            dve.tensor_copy(gains[:], ps_s[:, 0, 0:len(VECTORS) * KT]).then_inc(vec_copied, 1)
            dve.wait_ge(vec_copied, 1)
            for j in range(KT // 2):
                dve.wait_ge(x_turned, j + 1)
                dve.tensor_copy(x1[:, 2 * j:2 * j + 2, :], proj[:, j % 4, :].rearrange("p (k s) -> p k s", k=2))\
                   .then_inc(x_copied, 1)
                if j >= 1:
                    h_los(0, "a_norm", h_q, (j - 1,))
                    dve.wait_ge(squared, j)
                    if j >= 2:
                        dve.wait_ge(sumsq_ready, j - 1)
                    dve.tensor_tensor(sumsq, sumsq, squares, ALU.add).then_inc(sumsq_ready, 1)
            h_los(0, "a_norm", h_q, (KT // 2 - 1,))
            dve.wait_ge(squared, KT // 2)
            dve.wait_ge(sumsq_ready, KT // 2 - 1)
            dve.tensor_tensor(sumsq, sumsq, squares, ALU.add).then_inc(sumsq_ready, 1)

            def gated_lo(r, c):
                dve.wait_ge(og_hi, 8 * r + c + 1)
                chunk = slice(4 * c, 4 * c + 4)
                dve.tensor_tensor(gated[:, chunk, S:512], og[:, chunk, :], gated[:, chunk, 0:S].bitcast(F32), ALU.subtract)\
                   .then_inc(og_split, 1)

            def pair(phase, i, last):
                n = pair0[phase] + i
                unit = UNIT0[phase] + QKVG * i
                output = OUTPUT0[phase] + QKVG * i
                for s in range(PIECES):
                    split_lo(unit + 2, s)
                take_scaled(output + 1, 1, k_t)
                for s in range(PIECES):
                    split_lo(unit + 3, s)
                take_scaled(output + 2, 0, v_t)
                dve.wait_ge(scores_done, n + 1)
                dve.wait_ge(bias_ready, n + 2)
                dve.tensor_tensor(scores, ps_s[:, :, 0:384], bias, ALU.add).then_inc(s_added, 1)
                split_lo(unit + 4, 0)
                dve.wait_ge(s_added, n + 2)
                dve.tensor_reduce(row_max[:, 0, :], scores[:, :, 0:P], AX_X, ALU.max)
                dve.tensor_reduce(row_max[:, 1, :], scores[:, :, P:384], AX_X, ALU.max).then_inc(maxed, 1)
                dve.wait_ge(maxed, n + 1)
                dve.tensor_scalar(row_max, row_max, -1.0, None, ALU.mult).then_inc(negmax_ready, 1)
                split_lo(unit + 4, 1)
                dve.wait_ge(exp_done, 4 * n + 4)
                dve.reciprocal(row_sum, row_sum).then_inc(recip_ready, 1)
                dve.wait_ge(recip_ready, n + 1)
                for h in range(2):
                    for t, (a, b) in enumerate(((0, P), (P, 384))):
                        m = dve.tensor_scalar(scores[:, h, a:b], scores[:, h, a:b], row_sum[:, t, h:h + 1], None, ALU.mult)
                m.then_inc(p_ready, 1)
                split_lo(unit + 4, 2)
                split_lo(unit + 4, 3)
                if last:
                    gated_lo(phases.index(phase), 0)
                    gated_lo(phases.index(phase), 1)
                take_scaled(output + 3, 1, g_t, scale=0.5)
                dve.wait_ge(turned, n + 1)
                dve.tensor_copy(v_tok, ps_s[:, :, 0:S]).then_inc(v_tok_ready, 1)
                if not last:
                    split_lo(unit + 5, 0)
                dve.wait_ge(tanh_done, n + 1)
                dve.scalar_tensor_tensor(tanh_g, tanh_g, 1.0, g_t, ALU.add, ALU.mult).then_inc(silu_ready, 1)
                if not last:
                    for s in range(1, PIECES):
                        split_lo(unit + 5, s)
                    take_scaled(output + 4, 0, q_t, scale=SCALE)
                    gate_heads(n, 2 * i)

            def gate_heads(n, head):
                dve.wait_ge(o_done, n + 1)
                dve.wait_ge(silu_ready, n + 1)
                dve.tensor_tensor(og[:, bass.ds(head, 2), :], ps_s[:, :, 0:S], tanh_g, ALU.mult).then_inc(og_done, 1)

            def forget_gates():
                dve.wait_ge(z_done, 1)
                for t in range(2):
                    m = dve.scalar_tensor_tensor(gate[:, t, :], ps_s[:, t, 0:HEADS], rstd_column[:, t:t + 1],
                                                 fb[:, t, :], ALU.mult, ALU.add)
                step(m)
                dve.scalar_tensor_tensor(gate_u, gate, -1.0, gate, ALU.mult, ALU.max).then_inc(gate_exp_in, 1)
                step(dve.tensor_scalar(gate, gate, 0.0, None, ALU.min))
                dve.wait_ge(gate_exp, 1)
                step(dve.tensor_scalar(gate_u, gate_t, 2.0, None, ALU.add))
                step(dve.reciprocal(gate_u, gate_u))
                step(dve.tensor_tensor(gate_t, gate_t, gate_u, ALU.mult))
                step(dve.tensor_tensor(gate_u, gate_t, gate_t, ALU.mult))
                step(dve.tensor_scalar(cum, gate_u, 1.0 / 19, None, ALU.mult))
                for c in range(8, 0, -1):
                    step(dve.scalar_tensor_tensor(cum, cum, 1.0 / (2 * c + 1), gate_u, ALU.add, ALU.mult))
                step(dve.scalar_tensor_tensor(cum, cum, 1.0, gate_t, ALU.add, ALU.mult))
                dve.scalar_tensor_tensor(gate, cum, -2.0, gate, ALU.mult, ALU.add).then_inc(logf_ready, 1)

            def copy_sums():
                dve.wait_ge(cum_done, 1)
                dve.tensor_copy(cum, ps_s[:, 0, 0:2 * HEADS].rearrange("p (t h) -> p t h", t=2))
                dve.tensor_scalar(cum_row, ps_s[0:HEADS, 1, 0:S], -1.0, None, ALU.mult).then_inc(cum_copied, 1)

            for phase in phases:
                r = phases.index(phase)
                if phase == "B":
                    h_los(KT // 2, "kv_norm", h_kv, (7,))
                    dve.wait_ge(squared, 8 * (r + 1))
                    dve.tensor_tensor(sumsq, sumsq, squares, ALU.add).then_inc(sumsq_ready, 1)
                    h_los(KT, "b_norm", h_q, range(0, 2))
                mean_squares(r)
                if phase == "B":
                    h_los(KT, "b_norm", h_q, range(2, 4))
                reciprocal_of_root(r)
                if phase == "B":
                    h_los(KT, "b_norm", h_q, range(4, 8))
                    forget_gates()
                for s in range(PIECES):
                    split_lo(UNIT0[phase] + 1, s)
                if phase == "B":
                    copy_sums()
                take_scaled(OUTPUT0[phase], 0, q_t, scale=SCALE)
                with dve.Fori(0, PAIRS - 1) as i:
                    pair(phase, i, False)
                pair(phase, PAIRS - 1, True)

                unit = UNIT0[phase] + UNITS_ATT

                gate_heads(pair0[phase] + PAIRS - 1, 2 * (PAIRS - 1))
                for c in range(8):
                    if 1 <= c < 7:
                        gated_lo(r, c + 1)
                    split_lo(unit + 1 + c // 4, c % 4)

                def out_update(j, bank, last=False):
                    output = OUTPUT0[phase] + UNITS_ATT + j
                    take_output(output, bank, v_t)
                    dve.wait_ge(proj_free, output + 3)
                    xs = x1[:, bass.ds(2 * j, 2), :]
                    dve.tensor_tensor(xs, xs, v_t, ALU.add).then_inc(x_updated, 1)
                    if not last:
                        dve.wait_ge(squared, 8 * (r + 1) + j + 1)
                        dve.tensor_tensor(sumsq, sumsq, squares, ALU.add).then_inc(sumsq_ready, 1)

                step(dve.memset(sumsq, 0.0))
                out_update(0, 0)
                with dve.Fori(0, (OUT_N - 2) // 2) as m:
                    for jj in range(2):
                        j = 2 * m + 1 + jj
                        u = unit + 2 * j
                        for half in range(2):
                            for s in range(PIECES):
                                split_lo(u + 1 + half, s)
                        out_update(j, (1 + jj) % 2)
                j = OUT_N - 1
                u = unit + 2 * j
                for s in range(PIECES):
                    split_lo(u + 1, s)
                for s in range(PIECES):
                    if phase == "A":
                        h_los(KT // 2, "kv_norm", h_kv, (2 * s, 2 * s + 1) if s < 3 else (6,))
                    split_lo(u + 2, s)
                out_update(j, 1, last=True)
            dve.wait_ge(squared, 24)
            dve.tensor_tensor(sumsq, sumsq, squares, ALU.add).then_inc(sumsq_ready, 1)
            mean_squares(2)
            reciprocal_of_root(2)
            for k in range(KT):
                if k % 3 != 2:
                    m = dve.scalar_tensor_tensor(x1[:, k, :], x1[:, k, :], gain("final_norm", k), rstd, ALU.mult, ALU.mult)
            m.then_inc(x_normed, 1)
            dve.wait_ge(meta_turned, 1)
            dve.tensor_copy(x_res[:, :, 0:META], ps_s[:, 0, 0:KT * META].rearrange("p (k m) -> p k m", m=META))\
               .then_inc(meta_copied, 1)
            dve.wait_ge(meta_copied, 1)
            dve.wait_ge(x_normed, 2)
            dve.memset(taps[:, CONV_ROWS:], 0.0)
            dve.memset(ln_sums[:, 1, :], 0.0)
            dve.tensor_reduce(ln_sums[:, 0, :], x_res.rearrange("p k t -> p t k"), AX_X, ALU.add).then_inc(ln_summable, 1)

            def over(row, n):
                return row.unsqueeze(1).to_broadcast([P, n, T])

            def layer_norm(n):
                dve.wait_ge(ln_mu_ready, n + 1)
                for c in range(4):
                    chunk = x_res[:, 4 * c:4 * c + 4, :]
                    dve.tensor_tensor(chunk, chunk, over(ln_mu, 4), ALU.subtract).then_inc(centred, 1)
                dve.wait_ge(ln_sq_used, 4 * n + 4)
                dve.tensor_scalar(ln_mean, ps_t[:, 1, 0:T], 1.0 / D, LN_EPS, ALU.mult, ALU.add).then_inc(ln_mean_ready, 1)
                dve.wait_ge(ln_root_ready, n + 1)
                step(dve.reciprocal(ln_rstd, ln_root))
                step(refine(ln_rstd, ln_mean, ln_spare))
                for c in range(4):
                    chunk = x_res[:, 4 * c:4 * c + 4, :]
                    dve.tensor_tensor(chunk, chunk, over(ln_rstd, 4), ALU.mult).then_inc(ln_scaled, 1)

            layer_norm(0)
            steps_before = step.base + step.done
            LAYER_STEPS = 32

            def half_piece_lo(unit, s):
                dve.wait_ge(hi_ready, unit * PIECES + s + 1)
                dve.tensor_tensor(w_lo[:, s, 0:2], w_raw[:, s, 0:2], w_hi[:, s, 0:2].bitcast(F32), ALU.subtract)\
                   .then_inc(pieces_split, 1)

            def lo_of(count, chunk, src):
                dve.wait_ge(y_hi_ready, 6 * l + count)
                rows = slice(4 * chunk, 4 * chunk + 4)
                return dve.tensor_tensor(y_lo[:, rows, :], src, y_hi[:, rows, :].bitcast(F32), ALU.subtract)\
                          .then_inc(y_split, 1)

            def silu_of(count, dst, half):
                dve.wait_ge(gate_tanh, 5 * l + count)
                dve.scalar_tensor_tensor(dst, tanh_2, 1.0, half, ALU.add, ALU.mult).then_inc(gate_used, 1)
                dve.wait_ge(gate_used, 5 * l + count)

            with dve.Fori(0, DEPTH) as l:
                u0 = UNIT_2 + UNITS_2 * l
                o0 = OUTPUT_2 + OUTPUTS_2 * l
                step.start(steps_before + LAYER_STEPS * l)
                for c in range(4):
                    rows = slice(4 * c, 4 * c + 4)
                    dve.wait_ge(in_hi_ready, 4 * l + c + 1)
                    dve.tensor_tensor(in_lo[:, rows, :], x_res[:, rows, :], in_hi[:, rows, :].bitcast(F32), ALU.subtract)\
                       .then_inc(in_split, 1)
                dve.wait_ge(rows_turned, l + 1)
                dve.tensor_copy(vec, ps_s[:, 0, 0:VEC_ROWS])
                dve.tensor_copy(taps[:, 0:CONV_ROWS], ps_s[:, 1, 0:CONV_ROWS]).then_inc(rows_copied, 1)
                dve.wait_ge(rows_copied, l + 1)
                lam = vec[:, VEC["lru_lambda"]:VEC["lru_lambda"] + CT]
                dve.scalar_tensor_tensor(small[:, 0, :], lam, -1.0, lam, ALU.mult, ALU.max).then_inc(exp_lam_in, 1)
                dve.tensor_scalar(small[:, 2, :], lam, -1.0, 0.0, ALU.mult, ALU.max)
                dve.tensor_scalar(half_ln, vec[:, VEC["conv_ln_g"]:VEC["conv_ln_b"] + CT].rearrange("p (a b) -> p a b", a=2),
                                  0.5, None, ALU.mult)
                dve.wait_ge(exp_lam, l + 1)
                step(dve.tensor_scalar(small[:, 0, :], small[:, 1, :], 2.0, None, ALU.add))
                step(dve.reciprocal(small[:, 0, :], small[:, 0, :]))
                step(dve.tensor_tensor(small[:, 1, :], small[:, 1, :], small[:, 0, :], ALU.mult))
                step(dve.tensor_tensor(small[:, 0, :], small[:, 1, :], small[:, 1, :], ALU.mult))
                step(dve.tensor_scalar(small[:, 3, :], small[:, 0, :], 1.0 / 19, None, ALU.mult))
                for c in range(8, 0, -1):
                    step(dve.scalar_tensor_tensor(small[:, 3, :], small[:, 3, :], 1.0 / (2 * c + 1), small[:, 0, :],
                                                  ALU.add, ALU.mult))
                step(dve.scalar_tensor_tensor(small[:, 3, :], small[:, 3, :], 1.0, small[:, 1, :], ALU.add, ALU.mult))
                step(dve.scalar_tensor_tensor(small[:, 3, :], small[:, 3, :], 2.0, small[:, 2, :], ALU.mult, ALU.add))
                dve.tensor_scalar(lru_c8[:, 0, :], small[:, 3, :], LRU_C, None, ALU.mult)
                dve.tensor_scalar(lru_c8[:, 1, :], small[:, 3, :], -LRU_C, None, ALU.mult).then_inc(lru_c_ready, 1)
                for j in range(4):
                    for s in range(PIECES):
                        split_lo(u0 + j + 1, s)
                dve.wait_ge(glu_tanh, l + 1)
                dve.wait_ge(pads_ready, 1)
                dve.scalar_tensor_tensor(c_pad[:, :, TAPS - 1:TAPS - 1 + T], tanh_2, 1.0, val, ALU.add, ALU.mult).then_inc(conv_in, 1)
                dve.wait_ge(conv_in, l + 1)
                for t in range(CT):
                    b = VEC["conv_dw_b"] + t
                    m = dve.tensor_scalar(conv[:, t, :], c_pad[:, t, 0:T], taps[:, t:t + 1], vec[:, b:b + 1], ALU.mult, ALU.add)
                m.then_inc(conv_tap, 1)
                for j in range(U_K, U_RX):
                    for s in range(PIECES):
                        split_lo(u0 + j + 1, s)
                    if j in (U_Q, U_Q + 1):
                        for e, banks in ((0, ps_s), (1, ps_t)):
                            kv = 2 * (j - U_Q) + e
                            dve.wait_ge(kv_turned, 4 * l + kv + 1)
                            if kv:
                                dve.wait_ge(k_spread_ready, 4 * l + kv)
                            dve.tensor_tensor(k_spread[:, kv, :], banks[:, 0, 0:T], cos, ALU.mult)
                            step(dve.tensor_tensor(turn_t[:, 0, :], banks[:, 1, 0:T], sin, ALU.mult))
                            dve.tensor_tensor(k_spread[:, kv, :], k_spread[:, kv, :], turn_t[:, 0, :], ALU.add)\
                               .then_inc(k_spread_ready, 1)
                    if j == U_Q + 2:
                        dve.wait_ge(v_turned, l + 1)
                        dve.tensor_copy(v_all[0:META, 0, :], ps_s[0:META, 0, 0:2 * P]).then_inc(v_all_ready, 1)
                        for r in range(2):
                            dve.tensor_copy(v_all[:, 1 + r, :], ps_t[:, r, 0:2 * P]).then_inc(v_all_ready, 1)

                chain = Steps(dve, pair_step)

                def tap_group(count, j):
                    dve.wait_ge(conv_tap, TAPS_PADDED * l + count)
                    for t in range(CT):
                        m = dve.scalar_tensor_tensor(conv[:, t, :].unsqueeze(1), c_pad[:, t:t + 1, bass.ds(j, T)],
                                                     taps[:, bass.ds(CT * j + t, 1)], conv[:, t, :].unsqueeze(1), ALU.mult, ALU.add)
                    m.then_inc(conv_tap, 1)

                def attention_turn(kv, u):
                    turn = KV_HEADS * l + kv
                    dve.wait_ge(q_turned, turn + 1)
                    q = att[:, bass.ds(2 * kv, 2), :]
                    chain.start(5 * turn)
                    dve.scalar_tensor_tensor(q_now, q, HD ** -0.5, over(cos, 2), ALU.mult, ALU.mult)
                    chain(dve.scalar_tensor_tensor(turn_t, ps_s[:, :, 0:T], HD ** -0.5, over(sin, 2), ALU.mult, ALU.mult))
                    dve.tensor_tensor(q_now, q_now, turn_t, ALU.add).then_inc(q_now_ready, 1)
                    for e in range(2):
                        n = PAIRS_2 * l + 2 * kv + e
                        head = 4 * kv + 2 * e
                        split_lo(u + e + 1, 0)
                        dve.wait_ge(scores_2_done, n + 1)
                        dve.tensor_copy(s2[:, :, 144:146], sinks[:, bass.ds(head, 2)].unsqueeze(2).to_broadcast([P, 2, 2]))
                        dve.tensor_copy(sm[0:META, :, META:META + 1], sinks[0:META, bass.ds(head, 2)].unsqueeze(2))
                        dve.tensor_tensor(s2[:, :, 0:144], ps_s[:, :, 0:144],
                                          mask_2[:, 0:144].unsqueeze(1).to_broadcast([P, 2, 144]), ALU.add)
                        dve.tensor_tensor(s2[:, :, 146:418], ps_s[:, :, 144:416],
                                          mask_2[:, 144:416].unsqueeze(1).to_broadcast([P, 2, T]), ALU.add)
                        chain(dve.tensor_tensor(sm[0:META, :, 0:META], ps_s[0:META, :, 416:432],
                                                mask_2[0:META, META:2 * META].unsqueeze(1).to_broadcast([META, 2, META]), ALU.add))
                        dve.tensor_reduce(neg_max[:, 0, :], s2[:, :, 0:145], AX_X, ALU.max)
                        dve.tensor_reduce(neg_max[:, 1, :], s2[:, :, 145:418], AX_X, ALU.max)
                        chain(dve.tensor_reduce(neg_max[0:META, 2, :], sm[0:META], AX_X, ALU.max))
                        dve.tensor_scalar(neg_max[:, 0:2, :], neg_max[:, 0:2, :], -1.0, None, ALU.mult)
                        dve.tensor_scalar(neg_max[0:META, 2, :], neg_max[0:META, 2, :], -1.0, None, ALU.mult)\
                           .then_inc(neg_max_ready, 1)
                        tap_group(8 * kv + 4 * e + 1, 8 * kv + 4 * e + 1)
                        split_lo(u + e + 1, 1)
                        dve.wait_ge(exp_2_done, n + 1)
                        dve.reciprocal(sums_2[:, 0:2, :], sums_2[:, 0:2, :])
                        dve.reciprocal(sums_2[0:META, 2, :], sums_2[0:META, 2, :]).then_inc(recip_2_ready, 1)
                        tap_group(8 * kv + 4 * e + 2, 8 * kv + 4 * e + 2)
                        split_lo(u + e + 1, 2)
                        tap_group(8 * kv + 4 * e + 3, 8 * kv + 4 * e + 3)
                        split_lo(u + e + 1, 3)
                        dve.wait_ge(turned_2, n + 1)
                        dve.tensor_copy(ptm[0:META], ps_s[0:META, :, 0:T]).then_inc(ptm_ready, 1)
                        tap_group(8 * kv + 4 * e + 4, 8 * kv + 4 * e + 4)

                attention_turn(0, u0 + U_RX)
                attention_turn(1, u0 + U_CGATE)
                with dve.Fori(0, 2) as m2:
                    attention_turn(m2 + 2, u0 + U_AGATE + 2 * m2)
                dve.wait_ge(conv_tap, TAPS_PADDED * l + TAPS_PADDED)
                dve.sem_inc(conv_done, 1)

                u, o = u0 + U_RGATE, o0 + U_RGATE
                dve.wait_ge(c_mu_ready, l + 1)
                dve.tensor_tensor(conv, conv, over(c_stat[:, 0, :], CT), ALU.subtract).then_inc(c_centred, 1)
                split_lo(u + 1, 0)
                silu_of(1, a_gates[:, 0:4, :], a_gates[:, 0:4, :])
                dve.tensor_tensor(att[:, 0:4, :], att[:, 0:4, :], a_gates[:, 0:4, :], ALU.mult).then_inc(y_ready, 1)
                split_lo(u + 1, 1)
                lo_of(1, 1, att[:, 0:4, :])
                split_lo(u + 1, 2)
                split_lo(u + 1, 3)
                silu_of(2, a_gates[:, 4:8, :], a_gates[:, 4:8, :])
                dve.tensor_tensor(att[:, 4:8, :], att[:, 4:8, :], a_gates[:, 4:8, :], ALU.mult).then_inc(y_ready, 1)
                dve.wait_ge(c_sq_summed, l + 1)
                dve.tensor_scalar(c_stat[:, 1, :], ps_s[:, 1, 0:T], 1.0 / CONV_D, LN_EPS, ALU.mult, ALU.add)\
                   .then_inc(c_mean_ready, 1)
                split_lo(u + 2, 0)
                dve.wait_ge(c_root_ready, l + 1)
                step(dve.reciprocal(c_stat[:, 2, :], c_stat[:, 2, :]))
                step(refine(c_stat[:, 2, :], c_stat[:, 1, :], c_stat[:, 0, :]))
                step(dve.tensor_tensor(conv, conv, over(c_stat[:, 2, :], CT), ALU.mult))
                for t in range(CT):
                    m = dve.tensor_scalar(conv[:, t, :], conv[:, t, :], half_ln[:, 0, t:t + 1], half_ln[:, 1, t:t + 1],
                                          ALU.mult, ALU.add)
                m.then_inc(c_affine, 1)
                lo_of(2, 2, att[:, 4:8, :])
                lo_of(3, 3, rc)
                split_lo(u + 2, 1)
                dve.wait_ge(c_affine, l + 1)
                silu_of(3, conv, conv)
                lo_of(4, 0, conv)
                half_piece_lo(u + 2, 2)
                half_piece_lo(u + 2, 3)
                silu_of(4, c_gates, c_gates)
                u, o = u0 + U_SMALL, o0 + O_SMALL
                dve.wait_ge(proj_free, o + 2 + 2)
                dve.tensor_tensor(conv, conv, c_gates, ALU.mult).then_inc(y_ready, 1)
                lo_of(5, 0, conv)
                silu_of(5, r_gates, r_gates)
                dve.wait_ge(lru_act, l + 1)
                step(dve.tensor_tensor(lru_v, lru_a, lru_a, ALU.mult))
                dve.scalar_tensor_tensor(lru_v, lru_v, 1.0, lru_t, ALU.add, ALU.mult).then_inc(lru_v_ready, 1)
                split_lo(u + 1, 0)
                dve.wait_ge(lru_root, l + 1)
                dve.wait_ge(lru_ix, l + 1)
                step(dve.tensor_tensor(lru_v, lru_v, lru_i, ALU.mult))
                for t in range(CT):
                    m = dve.tensor_tensor_scan(lru_t[:, t, :], lru_a[:, t, :], lru_v[:, t, :], 0.0, ALU.mult, ALU.add)
                step(m)
                dve.tensor_tensor(lru_t, lru_t, r_gates, ALU.mult).then_inc(y_ready, 1)
                step(dve.memset(ln_sums, 0.0))
                for s in range(1, PIECES):
                    split_lo(u + 1, s)
                lo_of(6, 3, lru_t)

                def mixed(j, bank):
                    unit = u0 + U_OUT + j
                    output = o0 + O_OUT + j
                    dve.wait_ge(pieces_used, PIECES * (unit + 2))
                    dve.wait_ge(proj_free, output + 2)
                    xs = x_res[:, bass.ds(2 * j, 2), :]
                    dve.scalar_tensor_tensor(xs, xs, ALPHA, proj[:, 2 * bank:2 * bank + 2, 0:T], ALU.mult, ALU.add)\
                       .then_inc(proj_free, 1)
                    dve.wait_ge(proj_free, output + 3)
                    dve.wait_ge(ln_summable, OUT_N * l + j + 1)
                    dve.tensor_tensor(ln_sums, ln_sums, xs, ALU.add).then_inc(ln_summable, 1)

                with dve.Fori(0, OUT_N // 2) as m3:
                    for jj in range(2):
                        j = 2 * m3 + jj
                        for s in range(PIECES):
                            split_lo(u0 + U_OUT + 1 + j, s)
                        mixed(j, jj)
                layer_norm(l + 1)
                assert step.done == LAYER_STEPS, step.done
            for c in range(4):
                dve.wait_ge(rows_turned_out, 2 * c + 1)
                dve.tensor_copy(out_rows[:, 0, c * 512:(c + 1) * 512], proj[:, 2 * c % 4, :]).then_inc(copied_out_dve, 1)


NAMES = ["x", "a_norm", "a_w_in", "a_rel_bias", "a_w_out", "kv_norm", "kv_w", "f_w", "f_b", "b_norm", "b_w_in",
         "b_w_out", "final_norm", "meta_tokens_2", "ln_in_g_2", "ln_in_b_2", "w_in_2", "attn_sinks_2", "w_out_2",
         "conv_pw_w_2"]


def layout(inputs):
    arrays = {name: np.ascontiguousarray(inputs[name]) for name in NAMES}
    rows = [inputs[name + "_2"].reshape(DEPTH, -1, P) for name in LAYER_VECTORS]
    arrays["layer_rows"] = np.ascontiguousarray(np.concatenate(rows, 1))
    arrays["conv_rows"] = np.ascontiguousarray(inputs["conv_dw_w_2"].reshape(DEPTH, -1, P))
    blocks = np.zeros((DEPTH, P, CT, 2 * P), inputs["lru_wa_2"].dtype)
    for g, name in enumerate(("lru_wa_2", "lru_wx_2")):
        w = inputs[name]
        for e in range(2):
            rows, cols = slice(64 * e, 64 * e + 64), slice(P * g + 64 * e, P * g + 64 * e + 64)
            blocks[:, rows, :, cols] = w[:, e::2].transpose(0, 2, 1, 3)
    arrays["lru_blocks"] = blocks
    return arrays


def kernel(**inputs):
    import concourse.bacc as bacc
    from concourse.bass_utils import run_bass_kernel_spmd

    nc = bacc.Bacc("TRN2", target_bir_lowering=False, num_devices=1)
    const_at, constants = shape_constants()
    arrays = layout({name: np.asarray(a) for name, a in inputs.items()})
    arrays["shape_constants"] = constants
    io = {name: nc.dram_tensor(f"in_{name}_dram", a.shape, mybir.dt.from_np(a.dtype), kind="ExternalInput").ap()
          for name, a in arrays.items()}
    io["out"] = nc.dram_tensor("out_dram", (1, S, D), F32, kind="ExternalOutput").ap()
    build_program(nc, io, const_at)
    result = run_bass_kernel_spmd(nc, [{f"in_{name}_dram": a for name, a in arrays.items()}], core_ids=[0])
    return result.results[0]["out_dram"]
```

```python
from contextlib import ExitStack

import concourse.bass as bass
from concourse import mybir
import numpy as np

F32 = mybir.dt.float32
F32R = mybir.dt.float32r
ALU = mybir.AluOpType
ACT = mybir.ActivationFunctionType
AX_X = mybir.AxisListType.X

P = 128
D = 2048
KT = D // P
S = 256
META = 16
T = S + META
INNER = 4096
HEADS = INNER // P
PAIRS = HEADS // 2
UNIT_N = 256
PIECES = 4
PK = KT // PIECES
QKVG = 4
OUT_N = D // UNIT_N
EPS = 1e-6
LN_EPS = 1e-5
NEG = -1e30
SCALE = float(P) ** -0.5
CHUNK = 64
REL = 513

UNITS_ATT = QKVG * PAIRS
UNITS_OUT = 2 * OUT_N
UNIT0 = {"A": 0, "B": UNITS_ATT + UNITS_OUT}
OUTPUT0 = {"A": 0, "B": UNITS_ATT + OUT_N}
DEPTH = 2
HD = 64
HEADS_2 = 16
PAIRS_2 = HEADS_2 // 2
KV_HEADS = 4
ROT = 16
TAPS = 31
CT = 4
COL = {"val": 0, "glu": 512, "c_gate": 1024, "q": 1536, "k": 2560, "v": 2816, "a_gate": 3072, "r_x": 4096,
       "r_gate": 4608}
U_VAL, U_K, U_V, U_Q, U_RX, U_CGATE, U_AGATE, U_LRU, U_RGATE, U_PW, U_OUT, UNITS_2 = 0, 4, 5, 6, 10, 12, 14, 18, 19, 21, 22, 30
O_LRU, O_RGATE, O_PW, O_OUT, OUTPUTS_2 = 18, 22, 24, 28, 36
TAPS_DURING = (4, 4, 2, 2, 1, 1, 3, 3, 3, 3, 2, 2)
LAYER_VECTORS = ["ln_post_g", "ln_post_b", "conv_dw_b", "conv_ln_g", "conv_ln_b", "conv_pw_b", "lru_conv_b", "lru_ba",
                 "lru_bx", "lru_lambda", "lru_conv_w"]
VEC = {"ln_post_g": 0, "ln_post_b": 16, "conv_dw_b": 32, "conv_ln_g": 36, "conv_ln_b": 40, "conv_pw_b": 44,
       "lru_conv_b": 48, "lru_ba": 52, "lru_bx": 56, "lru_lambda": 60, "lru_conv_w": 64}
VEC_ROWS = 80
CONV_ROWS = TAPS * CT
CONV_D = CT * P
ALPHA = (2.0 * DEPTH) ** 0.25
LRU_C = 8.0
UNIT_2 = 2 * (UNITS_ATT + UNITS_OUT)
OUTPUT_2 = 2 * (UNITS_ATT + OUT_N)


def shape_constants():
    q = np.arange(P)[:, None]
    k = np.arange(P)[None, :]
    parts = {}
    parts["ident"] = (q == k).astype(np.float32)
    parts["ones"] = np.ones((P, P), np.float32)
    parts["tri"] = (q <= k).astype(np.float32)
    chunked = np.where(k < (q // CHUNK + 1) * CHUNK, 0.0, NEG).astype(np.float32)
    causal = np.where(k <= q, 0.0, NEG).astype(np.float32)
    seen = np.zeros((P, P), np.float32)
    parts["mask_a"] = np.concatenate([chunked, seen, chunked], 1)
    parts["mask_b"] = np.concatenate([causal, seen, causal], 1)
    meta = np.zeros((P, META), np.float32)
    window = np.where(k > q, 0.0, NEG).astype(np.float32)
    parts["mask_2"] = np.concatenate([meta, causal, meta, window, causal], 1)
    half = ROT // 2
    inv = (np.float32(500000.0) ** (-np.arange(half, dtype=np.float32) / np.float32(half))).astype(np.float32)
    angle = np.arange(T, dtype=np.float32)[None, :] * inv[:, None]
    cos, sin = np.ones((P, T), np.float32), np.zeros((P, T), np.float32)
    partner = np.zeros(HD, int)
    for d in range(ROT):
        partner[d] = d + half if d < half else d - half
        for e in range(2):
            cos[HD * e + d] = np.cos(angle[d % half])
            sin[HD * e + d] = np.sin(angle[d % half]) * (-1.0 if d < half else 1.0)
    parts["cos"], parts["sin"] = cos, sin
    perm = np.zeros((P, P), np.float32)
    spread = np.zeros((2, 2, P, P), np.float32)
    for m in range(P):
        d = m % HD
        if d < ROT:
            perm[HD * (m // HD) + partner[d], m] = 1.0
        for e in range(2):
            spread[e, 0, HD * e + d, m] = 1.0
            if d < ROT:
                spread[e, 1, HD * e + partner[d], m] = 1.0
    parts["perm"] = perm
    parts["spread"] = spread.reshape(4, P, P).transpose(1, 0, 2).reshape(P, 4 * P)
    at, columns = {}, 0
    for name, a in parts.items():
        at[name] = (columns, a.shape[1])
        columns += a.shape[1]
    return at, np.concatenate(list(parts.values()), 1)


class Region:

    def __init__(self, tensor):
        self.tensor, self.at = tensor, 0

    def take(self, *shape):
        n = int(np.prod(shape))
        flat = self.tensor[:, self.at:self.at + n]
        self.at += n
        assert self.at <= self.tensor.shape[1], self.at
        if len(shape) == 1:
            return flat
        names = "abc"[:len(shape)]
        sizes = {x: s for x, s in zip(names, shape)}
        return flat.rearrange(f"p ({' '.join(names)}) -> p {' '.join(names)}", **sizes)


class Steps:

    def __init__(self, engine, sem):
        self.engine, self.sem, self.base, self.done = engine, sem, 0, 0

    def start(self, base):
        self.base, self.done = base, 0

    def __call__(self, instruction):
        instruction.then_inc(self.sem, 1)
        self.done += 1
        self.engine.wait_ge(self.sem, self.base + self.done)


VECTORS = ["a_norm", "b_norm", "kv_norm", "final_norm", "ln_in_g_2", "ln_in_b_2"]


def part_of(w, s, shape):
    return w[:, s, 0:1, :] if shape == "tile" else w[:, s, :, 0:P]


def build_program(nc, io, const_at):
    with ExitStack() as ctx:
        def sb(name, shape, dt=F32):
            return ctx.enter_context(nc.sbuf_tensor(name, shape, dt))

        def sem(name):
            return ctx.enter_context(nc.semaphore(name))

        w_raw = sb("w_raw", [P, PIECES, PK, UNIT_N])
        w_hi = sb("w_hi", [P, PIECES, PK, UNIT_N], F32R)
        w_lo = sb("w_lo", [P, PIECES, PK, UNIT_N], F32R)
        operand = sb("operand", [P, 4 * KT * T], F32R)
        x_res = sb("x_res", [P, KT, T])
        scratch = sb("scratch", [P, 17730])
        consts = sb("consts", [P, 2 * P])
        gains = sb("gains", [P, len(VECTORS) * KT])
        proj = ctx.enter_context(nc.psum_tensor("proj", [P, 4, 512], F32))
        ps_s = ctx.enter_context(nc.psum_tensor("ps_s", [P, 2, 512], F32))
        ps_t = ctx.enter_context(nc.psum_tensor("ps_t", [P, 2, 512], F32))
        cum_dram = nc.dram_tensor("cumulative_log_forget", (HEADS, S), F32).ap()

        ident, ones = consts[:, 0:P], consts[:, P:2 * P]
        x1 = x_res[:, :, META:T]
        h_kv = operand[:, 0:KT * 512].rearrange("p (k n) -> p k n", n=512)
        h_q = operand[:, KT * 512:2 * KT * 512].rearrange("p (k n) -> p k n", n=512)
        gated = operand[:, 0:2 * KT * 512].rearrange("p (k n) -> p k n", n=512)

        one = Region(scratch)
        og = one.take(HEADS, S)
        qkvg = [one.take(2, S) for _ in range(QKVG)]
        q_t, k_t, v_t, g_t = qkvg
        part = one.take(2, S)
        bias_raw = one.take(2, S)
        bias = one.take(2, 384)
        scores = one.take(2, 384)
        p_t = one.take(2, 384)
        v_tok = one.take(2, S)
        tanh_g = one.take(2, S)
        sumsq = one.take(2, S)
        norm_mean, norm_root, norm_rstd, norm_spare = (one.take(S + 2) for _ in range(4))
        rstd, rstd_column = norm_rstd[:, 0:S], norm_rstd[:, S:S + 2]
        masks = {"A": one.take(384), "B": one.take(384)}
        tri = one.take(P)
        fb = one.take(2, HEADS)
        cum = one.take(2, HEADS)
        cum_pair = one.take(2, 2)
        row_max = one.take(2, 2)
        row_sum = one.take(2, 2)
        before = p_t.rearrange("p a b -> p (a b)")
        vec_rows = before[:, 0:P]
        gate, gate_t, gate_u = (before[:, P + 2 * HEADS * n:P + 2 * HEADS * (n + 1)]
                                .rearrange("p (t h) -> p t h", t=2) for n in range(3))
        fw = og.rearrange("p h s -> p (h s)")[:, 3 * D:3 * D + KT * HEADS].rearrange("p (k h) -> p k h", k=KT)
        cum_row = bias.rearrange("p a b -> p (a b)")[0:HEADS, 0:S]
        squares = g_t
        x_in = og.rearrange("p (t k) s -> p t (k s)", t=2)[:, :, 0:D]
        fw_hi = sb("fw_hi", [P, KT, HEADS], F32R)
        fw_lo = sb("fw_lo", [P, KT, HEADS], F32R)

        two = Region(scratch)
        slots = two.take(28, T)
        val, a_gates = slots[:, 0:4, :], slots[:, 0:8, :]
        att = slots[:, 8:16, :]
        k_spread = slots[:, 16:20, :]
        c_gates, r_gates = slots[:, 20:24, :], slots[:, 24:28, :]
        rows_in = scratch[:, 24 * T:24 * T + 2 * P].rearrange("p (a b) -> p a b", a=2)
        r_pad = two.take(CT, T + 3)
        c_pad = two.take(CT, T + TAPS - 1)
        conv = two.take(CT, T)
        v_all = two.take(3, KV_HEADS * HD)
        temp0 = two.at
        s2 = two.take(2, 146 + T)
        pt2 = two.take(2, 384)
        ptm = two.take(2, T)
        sm = two.take(2, META + 1)
        turn_t = two.take(2, T)
        rc = two.take(CT, T)
        spare = Region(scratch)
        spare.at = temp0
        k_raw = spare.take(2, T)
        v_raw = spare.take(2, T)
        spare.at = temp0
        tanh_2 = spare.take(CT, T)
        lru_a = spare.take(CT, T)
        tapped = slots[:, 0:4, :]
        mask_2 = two.take(2 * META + 3 * P)
        cos, sin = two.take(T), two.take(T)
        perm = two.take(P)
        spread = two.take(4, P)
        sinks = two.take(HEADS_2)
        vec = two.take(VEC_ROWS)
        taps = two.take(TAPS * CT)
        lru_c8 = two.take(2, CT)
        small = two.take(4, CT)
        neg_max = two.take(3, 2)
        sums_2 = two.take(3, 2)
        half_ln = two.take(2, CT)
        lru_r, lru_i, lru_t = slots[:, 16:20, :], c_pad[:, :, TAPS - 1:TAPS - 1 + T], rc
        conv_sq = slots[:, 24:28, :]
        c_stat = r_pad[:, :, 3:3 + T]
        stats = slots[:, 8:28, :]
        ln_mu, ln_mean, ln_root, ln_rstd, ln_spare = (stats[:, n, :] for n in range(5))
        ln_sums = stats[:, 6:8, :]
        ln_sq = [stats[:, 8:12, :], stats[:, 12:16, :]]
        meta_in = scratch[0:META, 0:D]
        out_rows = scratch[:, 0:2 * D].rearrange("p (t n) -> p t n", t=2)
        in_hi, in_lo, y_hi, y_lo = (operand[:, n * KT * T:(n + 1) * KT * T].rearrange("p (k n) -> p k n", n=T)
                                    for n in range(4))
        raw_landed = [sem(f"raw_landed_{s}") for s in range(PIECES)]
        hi_ready = sem("hi_ready")
        pieces_split = sem("pieces_split")
        pieces_used = sem("pieces_used")
        half_copied = sem("half_copied")
        proj_free = sem("proj_free")
        consts_in = sem("consts_in")
        x_landed = [sem(f"x_landed_{c}") for c in range(4)]
        early_in = sem("early_in")
        x_turned = sem("x_turned")
        x_copied = sem("x_copied")
        vec_turned = sem("vec_turned")
        vec_copied = sem("vec_copied")
        squared = sem("squared")
        x_updated = sem("x_updated")
        sumsq_ready = sem("sumsq_ready")
        norm_summed = sem("norm_summed")
        root_ready = sem("root_ready")
        mean_ready = sem("mean_ready")
        rstd_ready = sem("rstd_ready")
        scaled = sem("scaled")
        h_hi = sem("h_hi")
        h_split = sem("h_split")
        fw_hi_ready = sem("fw_hi_ready")
        fw_split = sem("fw_split")
        z_done = sem("z_done")
        gate_exp_in = sem("gate_exp_in")
        gate_exp = sem("gate_exp")
        logf_ready = sem("logf_ready")
        cum_done = sem("cum_done")
        cum_copied = sem("cum_copied")
        cum_stored = sem("cum_stored")
        bias_landed = sem("bias_landed")
        bias_ready = sem("bias_ready")
        cum_picked = sem("cum_picked")
        decay_ready = sem("decay_ready")
        scores_done = sem("scores_done")
        s_added = sem("s_added")
        maxed = sem("maxed")
        negmax_ready = sem("negmax_ready")
        exp_done = sem("exp_done")
        recip_ready = sem("recip_ready")
        p_ready = sem("p_ready")
        turned = sem("turned")
        pt_ready = sem("pt_ready")
        tanh_done = sem("tanh_done")
        silu_ready = sem("silu_ready")
        o_done = sem("o_done")
        og_done = sem("og_done")
        og_hi = sem("og_hi")
        og_split = sem("og_split")
        dve_step = sem("dve_step")
        out_stored = sem("out_stored")

        meta_landed = sem("meta_landed")
        meta_turned = sem("meta_turned")
        meta_copied = sem("meta_copied")
        final_scaled = sem("final_scaled")
        gain_summed = sem("gain_summed")
        ln_mu_raw = sem("ln_mu_raw")
        final_chunk = sem("final_chunk")
        x_normed = sem("x_normed")
        consts_2_in = sem("consts_2_in")
        rows_landed = sem("rows_landed")
        rows_turned = sem("rows_turned")
        rows_copied = sem("rows_copied")
        ln_summable = sem("ln_summable")
        ln_summed = sem("ln_summed")
        ln_mu_ready = sem("ln_mu_ready")
        centred = sem("centred")
        ln_squared = sem("ln_squared")
        ln_sq_used = sem("ln_sq_used")
        ln_mean_ready = sem("ln_mean_ready")
        ln_root_ready = sem("ln_root_ready")
        ln_scaled = sem("ln_scaled")
        affine_act = sem("affine_act")
        affine_scaled = sem("affine_scaled")
        affine_pool = sem("affine_pool")
        in_hi_ready = sem("in_hi_ready")
        in_split = sem("in_split")
        glu_tanh = sem("glu_tanh")
        pads_ready = sem("pads_ready")
        conv_in = sem("conv_in")
        kv_turned = sem("kv_turned")
        k_spread_ready = sem("k_spread_ready")
        v_turned = sem("v_turned")
        v_all_ready = sem("v_all_ready")
        q_turned = sem("q_turned")
        q_rotated = sem("q_rotated")
        scores_2_done = sem("scores_2_done")
        neg_max_ready = sem("neg_max_ready")
        exp_2_done = sem("exp_2_done")
        recip_2_ready = sem("recip_2_ready")
        p_2_ready = sem("p_2_ready")
        turned_2 = sem("turned_2")
        pt2_ready = sem("pt2_ready")
        ptm_ready = sem("ptm_ready")
        o_2_done = sem("o_2_done")
        o_2_taken = sem("o_2_taken")
        c_summed = sem("c_summed")
        c_mu_ready = sem("c_mu_ready")
        c_centred = sem("c_centred")
        c_squared = sem("c_squared")
        c_sq_summed = sem("c_sq_summed")
        c_mean_ready = sem("c_mean_ready")
        c_root_ready = sem("c_root_ready")
        c_affine = sem("c_affine")
        gate_tanh = sem("gate_tanh")
        gate_used = sem("gate_used")
        y_ready = sem("y_ready")
        y_ready_pool = sem("y_ready_pool")
        y_hi_ready = sem("y_hi_ready")
        y_split = sem("y_split")
        exp_lam_in = sem("exp_lam_in")
        exp_lam = sem("exp_lam")
        lru_c_ready = sem("lru_c_ready")
        lru_act = sem("lru_act")
        lru_v_ready = sem("lru_v_ready")
        lru_root = sem("lru_root")
        lru_ix = sem("lru_ix")
        conv_tap = sem("conv_tap")
        rc_tap = sem("rc_tap")
        rows_turned_out = sem("rows_turned_out")
        copied_out_act = sem("copied_out_act")
        copied_out_dve = sem("copied_out_dve")
        w_of = {
            "A": [io["a_w_in"][0][:, c * INNER:(c + 1) * INNER] for c in range(QKVG)],
            "B": [io["b_w_in"][0][:, 0:INNER], io["kv_w"][:, 0:INNER], io["kv_w"][:, INNER:2 * INNER],
                  io["b_w_in"][0][:, INNER:2 * INNER]],
        }
        w_out_of = {"A": io["a_w_out"][0], "B": io["b_w_out"][0]}
        phases = ("A", "B")

        def gain(vector, k):
            column = VECTORS.index(vector) * KT + k
            return gains[:, column:column + 1]

        pair0 = {"A": 0, "B": PAIRS}

        block = ctx.enter_context(nc.Block())

        @block.sync
        def _(sp):
            def load_unit(unit, w, row0, column):
                for s in range(PIECES):
                    sp.wait_ge(pieces_split, unit * PIECES + s + 1)
                    rows = w[row0 + s * PK * P:row0 + (s + 1) * PK * P, :]
                    src = rows.rearrange("(k p) n -> p k n", p=P)[:, :, bass.ds(column, UNIT_N)]
                    sp.dma_start(w_raw[:, s], src).then_inc(raw_landed[s], 16)

            for c in range(4):
                columns = slice(c * D // 4, (c + 1) * D // 4)
                sp.dma_start(x_in[:, :, columns], io["x"][0, :, columns].rearrange("(t p) n -> p t n", p=P))\
                  .then_inc(x_landed[c], 16)
            load_unit(0, w_of["A"][0], 0, 0)
            def load_pair(phase, i, last):
                unit = UNIT0[phase] + QKVG * i
                n = pair0[phase] + i
                sp.wait_ge(bias_ready, n + 1)
                if phase == "A":
                    rb = io["a_rel_bias"]
                    src = bass.AP(rb.tensor, rb.offset + 2 * i * REL + (REL - 2 * S + P), [[1, P], [REL, 2], [1, S]])
                else:
                    src = bass.AP(cum_dram.tensor, 2 * i * S, [[0, P], [S, 2], [1, S]])
                sp.dma_start(bias_raw, src).then_inc(bias_landed, 16)
                for c in (2, 3):
                    load_unit(unit + c, w_of[phase][c], 0, i * UNIT_N)
                if not last:
                    for c in (0, 1):
                        load_unit(unit + QKVG + c, w_of[phase][c], 0, (i + 1) * UNIT_N)

            for phase in phases:
                if phase == "A":
                    load_unit(1, w_of[phase][1], 0, 0)
                else:
                    for c in (0, 1):
                        load_unit(UNIT0[phase] + c, w_of[phase][c], 0, 0)
                    sp.wait_ge(cum_copied, 1)
                    sp.dma_start(cum_dram, cum_row).then_inc(cum_stored, 16)
                    sp.wait_ge(cum_stored, 16)
                with sp.Fori(0, PAIRS - 1) as i:
                    load_pair(phase, i, False)
                load_pair(phase, PAIRS - 1, True)
                with sp.Fori(0, OUT_N) as j:
                    for half in range(2):
                        load_unit(UNIT0[phase] + UNITS_ATT + 2 * j + half, w_out_of[phase], half * D, j * UNIT_N)
            sp.wait_ge(og_split, 16)
            sp.dma_start(meta_in, io["meta_tokens_2"]).then_inc(meta_landed, 16)
            load_unit(UNIT_2, io["w_in_2"][0], 0, COL["val"])
            sp.wait_ge(x_normed, 1)
            sp.wait_ge(final_scaled, 6)
            for dst, name in ((mask_2, "mask_2"), (cos, "cos"), (sin, "sin"), (perm, "perm"),
                              (spread.rearrange("p a b -> p (a b)"), "spread")):
                at, n = const_at[name]
                sp.dma_start(dst, io["shape_constants"][:, at:at + n]).then_inc(consts_2_in, 16)
            w_in = io["w_in_2"].rearrange("l d n -> (l d) n")
            w_out = io["w_out_2"].rearrange("l d n -> (l d) n")

            def load_rows(unit, w, row0, column, first=0):
                for s in range(PIECES):
                    sp.wait_ge(pieces_split, unit * PIECES + s + 1)
                    rows = w[bass.ds(row0 + (s + first) % PIECES * PK * P, PK * P), :]
                    src = rows.rearrange("(k p) n -> p k n", p=P)[:, :, bass.ds(column, UNIT_N)]
                    sp.dma_start(w_raw[:, s], src).then_inc(raw_landed[s], 16)

            with sp.Fori(0, DEPTH) as l:
                u0 = UNIT_2 + UNITS_2 * l
                sp.wait_ge(affine_act, 4 * l + 4)
                sp.wait_ge(affine_pool, 4 * l + 4)
                sp.dma_start(rows_in[0:VEC_ROWS, 0, :], io["layer_rows"][bass.ds(l, 1)].rearrange("a r p -> (a r) p"))\
                  .then_inc(rows_landed, 16)
                sp.dma_start(rows_in[0:CONV_ROWS, 1, :], io["conv_rows"][bass.ds(l, 1)].rearrange("a r p -> (a r) p"))\
                  .then_inc(rows_landed, 16)
                sp.dma_start(sinks, io["attn_sinks_2"][bass.ds(l, 1), :].to_broadcast([P, HEADS_2]))\
                  .then_inc(rows_landed, 16)
                for j in (1, 2, 3):
                    load_rows(u0 + j, w_in, l * D, UNIT_N * j)
                load_rows(u0 + U_K, w_in, l * D, COL["k"])
                load_rows(u0 + U_V, w_in, l * D, COL["v"])
                def load_columns(first, column, count):
                    with sp.Fori(0, count) as j:
                        load_rows(u0 + first + j, w_in, l * D, column + j * UNIT_N)

                for first, column, count in ((U_Q, COL["q"], 4), (U_RX, COL["r_x"], 2), (U_CGATE, COL["c_gate"], 2),
                                             (U_AGATE, COL["a_gate"], 4)):
                    load_columns(first, column, count)
                for s in range(PIECES):
                    sp.wait_ge(pieces_split, (u0 + U_LRU) * PIECES + s + 1)
                    src = io["lru_blocks"][bass.ds(l, 1)].rearrange("a p t n -> p (a t) n")
                    sp.dma_start(w_raw[:, s, 0:1], src[:, s:s + 1, :]).then_inc(raw_landed[s], 16)
                load_columns(U_RGATE, COL["r_gate"], 2)
                for s in range(PIECES):
                    sp.wait_ge(pieces_split, (u0 + U_PW) * PIECES + s + 1)
                    src = io["conv_pw_w_2"][bass.ds(l, 1)].rearrange("a (k p) n -> p (a k) n", p=P)
                    sp.dma_start(w_raw[:, s, :, 0:P], src[:, :, s * P:(s + 1) * P]).then_inc(raw_landed[s], 16)
                with sp.Fori(0, OUT_N) as j:
                    load_rows(u0 + U_OUT + j, w_out, l * D, j * UNIT_N, first=1)
                load_rows(u0 + UNITS_2, w_in, l * -D + (DEPTH - 1) * D, COL["val"])
            for c in range(4):
                for t in range(2):
                    sp.wait_ge(copied_out_dve if t == 0 else copied_out_act, c + 1)
                    sp.dma_start(io["out"][0, t * P:(t + 1) * P, c * 512:(c + 1) * 512],
                                 out_rows[:, t, c * 512:(c + 1) * 512]).then_inc(out_stored, 16)
            sp.wait_ge(out_stored, 16 * 8)

        @block.gpsimd
        def _(pool):
            pool.wait_ge(consts_in, 16 * 7)

            for phase in phases:
                if phase == "B":
                    pool.wait_ge(cum_copied, 1)
                with pool.Fori(0, PAIRS) as i:
                    n = pair0[phase] + i
                    pool.wait_ge(bias_landed, 16 * n + 16)
                    pool.wait_ge(s_added, n + 1)
                    mask = masks[phase]
                    if phase == "B":
                        m = pool.tensor_copy(cum_pair, cum[:, :, bass.ds(2 * i, 2)]).then_inc(cum_picked, 1)
                        pool.wait_ge(cum_picked, i + 1)
                    if phase == "A":
                        for h in range(2):
                            pool.tensor_tensor(bias[:, h, 0:P], bias_raw[:, h, 0:P][:, ::-1], mask[:, 0:P], ALU.add)
                            m = pool.tensor_tensor(bias[:, h, P:384], bias_raw[:, h, :][:, ::-1], mask[:, P:384], ALU.add)
                    else:
                        for t, cols, keys in ((0, slice(0, P), P), (1, slice(P, 384), S)):
                            m = pool.tensor_tensor(bias[:, :, cols], bias_raw[:, :, 0:keys],
                                                   cum_pair[:, t, :].unsqueeze(2).to_broadcast([P, 2, keys]), ALU.add)
                        m.then_inc(decay_ready, 1)
                        pool.wait_ge(decay_ready, i + 1)
                        m = pool.tensor_tensor(bias, bias, mask.unsqueeze(1).to_broadcast([P, 2, 384]), ALU.add)
                    m.then_inc(bias_ready, 1)

            pool.wait_ge(rstd_ready, 3)
            for c in (1, 2, 3):
                k = 4 * c + 3
                pool.tensor_tensor(x1[:, k, :], x1[:, k, :], rstd, ALU.mult).then_inc(final_scaled, 1)
                pool.wait_ge(final_scaled, 2 * c - 1)
                pool.tensor_tensor(x1[:, k, :], x1[:, k, :], gain("final_norm", k).to_broadcast([P, S]), ALU.mult)\
                    .then_inc(final_scaled, 1)
            pool.wait_ge(final_scaled, 6)

            def affine_rest(n, g, b):
                for c in range(4):
                    pool.wait_ge(ln_scaled, 4 * n + c + 1)
                    rows = slice(4 * c + 2, 4 * c + 4)
                    over_rows = [a[:, rows].unsqueeze(2).to_broadcast([P, 2, T]) for a in (g, b)]
                    pool.tensor_tensor(x_res[:, rows, :], x_res[:, rows, :], over_rows[0], ALU.mult).then_inc(affine_scaled, 1)
                    pool.wait_ge(affine_scaled, 4 * n + c + 1)
                    pool.tensor_tensor(x_res[:, rows, :], x_res[:, rows, :], over_rows[1], ALU.add).then_inc(affine_pool, 1)

            g, b = (gains[:, VECTORS.index(v) * KT:(VECTORS.index(v) + 1) * KT] for v in ("ln_in_g_2", "ln_in_b_2"))
            affine_rest(0, g, b)
            pool.wait_ge(x_normed, 1)
            pool.memset(r_pad[:, :, 0:3], 0.0)
            pool.memset(c_pad[:, :, 0:TAPS - 1], 0.0).then_inc(pads_ready, 1)
            with pool.Fori(0, DEPTH) as l:
                def divide_by_sums(i):
                    pool.wait_ge(recip_2_ready, PAIRS_2 * l + i + 1)
                    for rows, dst, part_sums, width in ((P, s2[:, :, 0:144], sums_2[:, 0, :], 144),
                                                        (P, s2[:, :, 146:418], sums_2[:, 1, :], T),
                                                        (META, sm[0:META, :, 0:META], sums_2[0:META, 2, :], META)):
                        m = pool.tensor_tensor(dst, dst, part_sums.unsqueeze(2).to_broadcast([rows, 2, width]), ALU.mult)
                    m.then_inc(p_2_ready, 1)

                with pool.Fori(0, 3) as i:
                    divide_by_sums(i)
                pool.wait_ge(proj_free, OUTPUT_2 + OUTPUTS_2 * l + U_RX + 1 + 3)

                def tap_of(column):
                    return vec[:, column:column + CT].unsqueeze(2).to_broadcast([P, CT, T])

                w = VEC["lru_conv_w"]
                pool.tensor_tensor(rc, r_pad[:, :, 0:T], tap_of(w), ALU.mult).then_inc(rc_tap, 1)
                pool.wait_ge(rc_tap, 8 * l + 1)
                pool.tensor_tensor(rc, rc, tap_of(VEC["lru_conv_b"]), ALU.add).then_inc(rc_tap, 1)
                for j in range(1, 4):
                    pool.tensor_tensor(tapped, r_pad[:, :, j:j + T], tap_of(w + 4 * j), ALU.mult).then_inc(rc_tap, 1)
                    pool.wait_ge(rc_tap, 8 * l + 2 * j + 1)
                    pool.tensor_tensor(rc, rc, tapped, ALU.add).then_inc(rc_tap, 1)
                    if j < 3:
                        pool.wait_ge(rc_tap, 8 * l + 2 * j + 2)
                with pool.Fori(3, PAIRS_2) as i:
                    divide_by_sums(i)
                pool.wait_ge(proj_free, OUTPUT_2 + OUTPUTS_2 * l + O_LRU + 3 + 3)
                pool.wait_ge(rc_tap, 8 * l + 8)
                pool.tensor_tensor(lru_i, lru_i, rc, ALU.mult).then_inc(lru_ix, 1)
                pool.wait_ge(gate_used, 5 * l + 3)
                pool.tensor_tensor(att[:, 4:8, :], att[:, 4:8, :], a_gates[:, 4:8, :], ALU.mult).then_inc(y_ready_pool, 1)
                pool.wait_ge(gate_used, 5 * l + 5)
                pool.wait_ge(proj_free, OUTPUT_2 + OUTPUTS_2 * l + O_PW + 3 + 3)
                pool.tensor_tensor(conv, conv, c_gates, ALU.mult).then_inc(y_ready_pool, 1)
                affine_rest(l + 1, vec[:, 0:KT], vec[:, KT:2 * KT])

        @block.scalar
        def _(act):
            act.sem_inc(s_added, 1)
            act.sem_inc(o_2_taken, 1)

            def split_hi(unit, s):
                piece = unit * PIECES + s
                act.wait_ge(raw_landed[s], 16 * unit + 16)
                act.wait_ge(pieces_used, piece + 1)
                act.activation(w_hi[:, s], w_raw[:, s], ACT.Copy).then_inc(hi_ready, 1)

            def copy_half(last_unit, output, bank):
                act.wait_ge(pieces_used, PIECES * (last_unit + 2))
                act.wait_ge(proj_free, output + 2)
                act.activation(part, proj[:, 2 * bank:2 * bank + 2, S:512], ACT.Copy).then_inc(half_copied, 1)

            def take_values(last_unit, output, bank):
                act.wait_ge(pieces_used, PIECES * (last_unit + 2))
                for t in range(2):
                    act.activation(v_tok[:, :, t * P:(t + 1) * P],
                                   proj[:, 2 * bank + t, 0:S].rearrange("p (h d) -> p h d", h=2), ACT.Copy,
                                   scale=rstd_column[:, t:t + 1]).then_inc((half_copied, proj_free)[t], 1)

            def root_of(n):
                act.wait_ge(mean_ready, n + 1)
                act.activation(norm_root, norm_mean, ACT.Sqrt).then_inc(root_ready, 1)

            def h_his(vector, dst, pairs):
                for pair_of_tiles in pairs:
                    for k in (2 * pair_of_tiles, 2 * pair_of_tiles + 1):
                        m = act.activation(dst[:, k, 0:S], x1[:, k, :], ACT.Identity, scale=gain(vector, k))
                    m.then_inc(h_hi, 1)

            c = io["shape_constants"]
            at, n = const_at["ident"]
            act.dma_start(consts[:, 0:P], c[:, at:at + n]).then_inc(early_in, 16)
            act.dma_start(vec_rows[0:len(VECTORS) * KT, :], io["norm_rows"]).then_inc(early_in, 16)
            for dst, name in ((consts[:, P:2 * P], "ones"), (tri, "tri"), (masks["A"], "mask_a"), (masks["B"], "mask_b")):
                at, n = const_at[name]
                act.dma_start(dst, c[:, at:at + n]).then_inc(consts_in, 16)
            act.dma_start(fw, io["f_w"].rearrange("(k p) n -> p k n", p=P)).then_inc(consts_in, 16)
            for t in range(2):
                act.dma_start(fb[:, t, :], io["f_b"].rearrange("(a n) -> a n", a=1).to_broadcast([P, HEADS]))\
                   .then_inc(consts_in, 16)

            for j in range(KT // 2):
                act.wait_ge(x_copied, j + 1)
                if j == 0:
                    act.wait_ge(vec_copied, 1)
                h_his("a_norm", h_q, (j,))
                if j >= 1:
                    act.wait_ge(sumsq_ready, j)
                act.activation(squares, x1[:, 2 * j:2 * j + 2, :], ACT.Square).then_inc(squared, 1)
                if j % 2 == 1:
                    split_hi(0, j // 2)
            act.wait_ge(consts_in, 16 * 7)
            act.activation(fw_hi[:], fw, ACT.Copy).then_inc(fw_hi_ready, 1)

            def gated_hi(og0, c):
                act.wait_ge(og_done, og0 + 2 * c + 3)
                act.activation(gated[:, 4 * c:4 * c + 4, 0:S], og[:, 4 * c:4 * c + 4, :], ACT.Copy).then_inc(og_hi, 1)

            def pair(phase, i, last):
                n = pair0[phase] + i
                unit = UNIT0[phase] + QKVG * i
                output = OUTPUT0[phase] + QKVG * i
                for s in range(PIECES):
                    split_hi(unit + 2, s)
                copy_half(unit + 1, output + 1, 1)
                for s in range(PIECES):
                    split_hi(unit + 3, s)
                act.wait_ge(scaled, 3 * n + 2)
                take_values(unit + 2, output + 2, 0)
                split_hi(unit + 4, 0)
                split_hi(unit + 4, 1)
                act.wait_ge(negmax_ready, n + 1)
                for h in range(2):
                    for t, (a, b) in enumerate(((0, P), (P, 384))):
                        act.activation(scores[:, h, a:b], scores[:, h, a:b], ACT.Exp, bias=row_max[:, t, h:h + 1],
                                       accum_out=row_sum[:, t, h:h + 1]).then_inc(exp_done, 1)
                split_hi(unit + 4, 2)
                split_hi(unit + 4, 3)
                if last:
                    gated_hi(pair0[phase], 0)
                    gated_hi(pair0[phase], 1)
                copy_half(unit + 3, output + 3, 1)
                act.wait_ge(turned, n + 1)
                act.activation(p_t, ps_t[:, :, 0:384], ACT.Copy).then_inc(pt_ready, 1)
                act.wait_ge(scaled, 3 * n + 3)
                act.activation(tanh_g, g_t, ACT.Tanh).then_inc(tanh_done, 1)
                if not last:
                    for s in range(PIECES):
                        split_hi(unit + 5, s)
                    copy_half(unit + 4, output + 4, 0)

            for phase in phases:
                r = phases.index(phase)
                if phase == "B":
                    h_his("b_norm", h_q, range(0, 4))
                root_of(r)
                if phase == "B":
                    h_his("b_norm", h_q, range(4, 8))
                    act.wait_ge(gate_exp_in, 1)
                    act.activation(gate_t, gate_u, ACT.Exp, scale=-1.0).then_inc(gate_exp, 1)
                for s in range(PIECES):
                    split_hi(UNIT0[phase] + 1, s)
                copy_half(UNIT0[phase], OUTPUT0[phase], 0)
                act.wait_ge(rstd_ready, r + 1)
                with act.Fori(0, PAIRS - 1) as i:
                    pair(phase, i, False)
                pair(phase, PAIRS - 1, True)

                unit = UNIT0[phase] + UNITS_ATT
                og0 = pair0[phase]
                for c in range(8):
                    if 1 <= c < 7:
                        gated_hi(og0, c + 1)
                    split_hi(unit + 1 + c // 4, c % 4)

                def out_update(phase, j, bank, last=False):
                    unit = UNIT0[phase] + UNITS_ATT + 2 * j
                    output = OUTPUT0[phase] + UNITS_ATT + j
                    copy_half(unit + 1, output, bank)
                    act.wait_ge(x_updated, 8 * phases.index(phase) + j + 1)
                    if last and phase == "A":
                        h_his("kv_norm", h_kv, (7,))
                    act.activation(squares, x1[:, bass.ds(2 * j, 2), :], ACT.Square).then_inc(squared, 1)

                out_update(phase, 0, 0)
                with act.Fori(0, (OUT_N - 2) // 2) as m:
                    for jj in range(2):
                        j = 2 * m + 1 + jj
                        u = unit + 2 * j
                        for half in range(2):
                            for s in range(PIECES):
                                split_hi(u + 1 + half, s)
                        out_update(phase, j, (1 + jj) % 2)
                j = OUT_N - 1
                u = unit + 2 * j
                for s in range(PIECES):
                    split_hi(u + 1, s)
                if phase == "A":
                    act.wait_ge(pieces_used, PIECES * (u + 2))
                for s in range(PIECES):
                    if phase == "A":
                        h_his("kv_norm", h_kv, (2 * s, 2 * s + 1) if s < 3 else (6,))
                    split_hi(u + 2, s)
                out_update(phase, j, 1, last=True)

            root_of(2)

            def layer_norm(n, g, b, first=False):
                act.wait_ge(ln_summed, n + 1)
                if first:
                    act.activation(ln_mu, ps_s[:, 1, 0:T], ACT.Copy, scale=1.0 / D).then_inc(ln_mu_raw, 1)
                else:
                    act.activation(ln_mu, ps_t[:, 0, 0:T], ACT.Copy, scale=1.0 / D).then_inc(ln_mu_ready, 1)
                for c in range(4):
                    act.wait_ge(centred, 4 * n + c + 1)
                    if c >= 2:
                        act.wait_ge(ln_sq_used, 4 * n + c - 1)
                    act.activation(ln_sq[c % 2], x_res[:, 4 * c:4 * c + 4, :], ACT.Square).then_inc(ln_squared, 1)
                act.wait_ge(ln_mean_ready, n + 1)
                act.activation(ln_root, ln_mean, ACT.Sqrt).then_inc(ln_root_ready, 1)

                def affine(c):
                    act.wait_ge(ln_scaled, 4 * n + c + 1)
                    for k in (4 * c, 4 * c + 1):
                        m = act.activation(x_res[:, k, :], x_res[:, k, :], ACT.Identity, scale=g[:, k:k + 1], bias=b[:, k:k + 1])
                    m.then_inc(affine_act, 1)

                affine(0)
                for c in range(4):
                    if c < 3:
                        affine(c + 1)
                    act.wait_ge(affine_act, 4 * n + c + 1)
                    act.wait_ge(affine_pool, 4 * n + c + 1)
                    act.activation(in_hi[:, 4 * c:4 * c + 4, :], x_res[:, 4 * c:4 * c + 4, :], ACT.Copy).then_inc(in_hi_ready, 1)

            g, b = (gains[:, VECTORS.index(v) * KT:(VECTORS.index(v) + 1) * KT] for v in ("ln_in_g_2", "ln_in_b_2"))
            layer_norm(0, g, b, first=True)

            def copy_output(unit, output, bank, dst, scale=1.0):
                act.wait_ge(pieces_used, PIECES * (unit + 2))
                act.wait_ge(proj_free, output + 2)
                act.activation(dst, proj[:, 2 * bank:2 * bank + 2, 0:T], ACT.Copy, scale=scale).then_inc(proj_free, 1)

            def hi_of(dst, src):
                act.activation(dst, src, ACT.Copy).then_inc(y_hi_ready, 1)

            with act.Fori(0, DEPTH) as l:
                u0 = UNIT_2 + UNITS_2 * l
                o0 = OUTPUT_2 + OUTPUTS_2 * l
                for j in range(4):
                    for s in range(PIECES):
                        split_hi(u0 + j + 1, s)
                    if j == 0:
                        act.wait_ge(exp_lam_in, l + 1)
                        act.activation(small[:, 1, :], small[:, 0, :], ACT.Exp, scale=-1.0).then_inc(exp_lam, 1)
                    copy_output(u0 + j, o0 + j, j % 2, slots[:, 2 * j:2 * j + 2, :], 0.5)
                act.wait_ge(proj_free, o0 + 4 + 2)
                act.activation(tanh_2, slots[:, 4:8, :], ACT.Tanh).then_inc(glu_tanh, 1)
                act.wait_ge(conv_in, l + 1)
                for j in range(4, 10):
                    for s in range(PIECES):
                        split_hi(u0 + j + 1, s)
                    dst = k_raw if j == U_K else v_raw if j == U_V else slots[:, 8 + 2 * (j - U_Q):10 + 2 * (j - U_Q), :]
                    copy_output(u0 + j, o0 + j, j % 2, dst)

                def exponentials(n):
                    act.wait_ge(neg_max_ready, n + 1)
                    for h in range(2):
                        act.activation(s2[:, h, 0:145], s2[:, h, 0:145], ACT.Exp, bias=neg_max[:, 0, h:h + 1],
                                       accum_out=sums_2[:, 0, h:h + 1])
                        act.activation(s2[:, h, 145:418], s2[:, h, 145:418], ACT.Exp, bias=neg_max[:, 1, h:h + 1],
                                       accum_out=sums_2[:, 1, h:h + 1])
                        m = act.activation(sm[0:META, h, :], sm[0:META, h, :], ACT.Exp, bias=neg_max[0:META, 2, h:h + 1],
                                           accum_out=sums_2[0:META, 2, h:h + 1])
                    m.then_inc(exp_2_done, 1)

                def split_part_hi(unit, s, shape):
                    act.wait_ge(raw_landed[s], 16 * unit + 16)
                    act.wait_ge(pieces_used, unit * PIECES + s + 1)
                    act.activation(part_of(w_hi, s, shape), part_of(w_raw, s, shape), ACT.Copy).then_inc(hi_ready, 1)

                def copy_turned(i):
                    act.wait_ge(turned_2, PAIRS_2 * l + i + 1)
                    act.activation(pt2, ps_t[:, :, 0:384], ACT.Copy).then_inc(pt2_ready, 1)

                def copy_head_outputs(i):
                    act.wait_ge(o_2_done, PAIRS_2 * l + i + 1)
                    act.activation(att[:, i, :], ps_t[:, 0, 0:T], ACT.Copy).then_inc(o_2_taken, 1)

                for i in range(PAIRS_2):
                    j = U_RX + i
                    u, o = u0 + j, o0 + j
                    if i == 7:
                        act.wait_ge(c_summed, l + 1)
                        act.wait_ge(rc_tap, 8 * l + 8)
                        act.activation(c_stat[:, 0, :], ps_s[:, 0, 0:T], ACT.Copy, scale=1.0 / CONV_D).then_inc(c_mu_ready, 1)
                    split_next = split_hi if i < 7 else lambda unit, s: split_part_hi(unit, s, "tile")
                    split_next(u + 1, 0)
                    if i >= 1:
                        copy_turned(i - 1)
                    exponentials(PAIRS_2 * l + i)
                    split_next(u + 1, 1)
                    if i >= 1:
                        copy_head_outputs(i - 1)
                    if i == 5:
                        act.wait_ge(rc_tap, 8 * l + 8)
                        hi_of(y_hi[:, 8:12, :], rc)
                    split_next(u + 1, 2)
                    if i == 7:
                        act.wait_ge(c_centred, l + 1)
                        act.activation(conv_sq, conv, ACT.Square).then_inc(c_squared, 1)
                    split_next(u + 1, 3)
                    if i < 2:
                        copy_output(u, o, i % 2, r_pad[:, 2 * i:2 * i + 2, 3:3 + T])
                    elif i < 4:
                        copy_output(u, o, i % 2, c_gates[:, 2 * i - 4:2 * i - 2, :], 0.5)
                    else:
                        if i == 4:
                            act.wait_ge(rc_tap, 8 * l + 8)
                        copy_output(u, o, i % 2, a_gates[:, 2 * i - 8:2 * i - 6, :], 0.5)

                def gate_tanhs(count, src):
                    if count:
                        act.wait_ge(gate_used, 5 * l + count)
                    act.activation(tanh_2, src, ACT.Tanh).then_inc(gate_tanh, 1)

                for t in range(CT):
                    split_hi(u0 + U_RGATE, t)
                    act.wait_ge(proj_free, o0 + O_LRU + t + 2)
                    bank = t % 2
                    act.activation(lru_r[:, t, :], proj[:, 2 * bank, 0:T], ACT.Sigmoid,
                                   bias=vec[:, VEC["lru_ba"] + t:VEC["lru_ba"] + t + 1])
                    act.activation(lru_i[:, t, :], proj[:, 2 * bank + 1, 0:T], ACT.Sigmoid,
                                   bias=vec[:, VEC["lru_bx"] + t:VEC["lru_bx"] + t + 1]).then_inc(proj_free, 1)
                u, o = u0 + U_RGATE, o0 + O_RGATE
                act.wait_ge(c_mean_ready, l + 1)
                act.activation(c_stat[:, 2, :], c_stat[:, 1, :], ACT.Sqrt).then_inc(c_root_ready, 1)
                split_hi(u + 1, 0)
                copy_turned(7)
                split_hi(u + 1, 1)
                copy_head_outputs(7)
                split_hi(u + 1, 2)
                act.wait_ge(c_affine, l + 1)
                gate_tanhs(0, conv)
                act.wait_ge(lru_c_ready, l + 1)
                act.wait_ge(proj_free, o0 + O_LRU + 3 + 3)
                act.wait_ge(lru_ix, l + 1)
                for t in range(CT):
                    act.activation(lru_a[:, t, :], lru_r[:, t, :], ACT.Exp, scale=lru_c8[:, 1, t:t + 1])
                    m = act.activation(lru_t[:, t, :], lru_r[:, t, :], ACT.Tanh, scale=lru_c8[:, 0, t:t + 1])
                m.then_inc(lru_act, 1)
                split_hi(u + 1, 3)
                copy_output(u, o, 0, r_gates[:, 0:2, :], 0.5)
                split_part_hi(u + 2, 0, "columns")
                act.wait_ge(gate_used, 5 * l + 1)
                hi_of(y_hi[:, 12:16, :], conv)
                gate_tanhs(1, a_gates[:, 0:4, :])
                split_part_hi(u + 2, 1, "columns")
                act.wait_ge(lru_v_ready, l + 1)
                act.activation(lru_r, lru_r, ACT.Sqrt).then_inc(lru_root, 1)
                split_part_hi(u + 2, 2, "columns")
                split_part_hi(u + 2, 3, "columns")
                copy_output(u + 1, o + 1, 1, r_gates[:, 2:4, :], 0.5)
                u, o = u0 + U_PW, o0 + O_PW
                for s in range(PIECES):
                    split_hi(u + 1, s)
                    act.wait_ge(proj_free, o + s + 2)
                    act.activation(conv[:, s, :], proj[:, 2 * (s % 2), 0:T], ACT.Identity,
                                   bias=vec[:, VEC["conv_pw_b"] + s:VEC["conv_pw_b"] + s + 1]).then_inc(proj_free, 1)
                    if s == 0:
                        act.wait_ge(y_ready, 2 * l + 1)
                        hi_of(y_hi[:, 0:4, :], att[:, 0:4, :])
                    if s == 1:
                        gate_tanhs(2, a_gates[:, 4:8, :])
                gate_tanhs(3, r_gates)
                act.wait_ge(y_ready_pool, 2 * l + 1)
                hi_of(y_hi[:, 4:8, :], att[:, 4:8, :])
                gate_tanhs(4, c_gates)
                act.wait_ge(y_ready, 2 * l + 2)
                hi_of(y_hi[:, 8:12, :], lru_t)
                act.wait_ge(y_ready_pool, 2 * l + 2)
                hi_of(y_hi[:, 12:16, :], conv)
                with act.Fori(0, OUT_N) as j:
                    for s in range(PIECES):
                        split_hi(u0 + U_OUT + 1 + j, s)
                layer_norm(l + 1, vec[:, 0:KT], vec[:, KT:2 * KT])
            for c in range(4):
                act.wait_ge(rows_turned_out, 2 * c + 2)
                act.activation(out_rows[:, 1, c * 512:(c + 1) * 512], proj[:, (2 * c + 1) % 4, :], ACT.Copy)\
                   .then_inc(copied_out_act, 1)

        @block.tensor
        def _(pe):
            pe.sem_inc(pieces_used, PIECES)

            def multiply(unit, bank, rhs, first=True, last=True, chunk_wait=None):
                for s in range(PIECES):
                    pe.wait_ge(pieces_split, unit * PIECES + s + 1 + PIECES)
                    if chunk_wait is not None:
                        chunk_wait(s)
                    for kk in range(PK):
                        k = s * PK + kk
                        for t in range(2):
                            cols = slice(t * P, (t + 1) * P)
                            end = k == KT - 1
                            pe.matmul(proj[:, 2 * bank + t, :], w_hi[:, s, kk, cols], rhs[:, k, :],
                                      start=first and k == 0, stop=False)
                            m = pe.matmul(proj[:, 2 * bank + t, 0:S], w_lo[:, s, kk, cols], rhs[:, k, 0:S],
                                          start=False, stop=last and end)
                    m.then_inc(pieces_used, 1)

            def multiply_values(unit, bank, operand_kv):
                for s in range(PIECES):
                    pe.wait_ge(pieces_split, unit * PIECES + s + 1 + PIECES)
                    for kk in range(PK):
                        k = s * PK + kk
                        for t in range(2):
                            out = proj[:, 2 * bank + t, 0:UNIT_N]
                            hi = operand_kv[:, k, t * P:(t + 1) * P]
                            lo = operand_kv[:, k, S + t * P:S + (t + 1) * P]
                            pe.matmul(out, hi, w_hi[:, s, kk, :], start=k == 0, stop=False)
                            pe.matmul(out, hi, w_lo[:, s, kk, :], start=False, stop=False)
                            m = pe.matmul(out, lo, w_hi[:, s, kk, :], start=False, stop=k == KT - 1)
                    m.then_inc(pieces_used, 1)

            def norm_sum(n, ready):
                pe.wait_ge(sumsq_ready, ready)
                pe.matmul(ps_t[:, 0, 0:S], ones, sumsq[:, 0, :], start=True, stop=False)
                pe.matmul(ps_t[:, 0, 0:S], ones, sumsq[:, 1, :], start=False, stop=True)
                for t in range(2):
                    for a in range(2):
                        m = pe.matmul(ps_t[:, 1, t:t + 1], sumsq[:, a, t * P:(t + 1) * P], ones[:, 0:1], start=a == 0, stop=a == 1)
                m.then_inc(norm_summed, 1)

            pe.wait_ge(early_in, 16 * 2)
            pe.transpose(ps_s[:, 0, 0:len(VECTORS) * KT], vec_rows[0:len(VECTORS) * KT, :],
                         ident[0:len(VECTORS) * KT, 0:len(VECTORS) * KT]).then_inc(vec_turned, 1)
            for j in range(KT // 2):
                if j % 2 == 0:
                    pe.wait_ge(x_landed[j // 2], 16)
                if j >= 4:
                    pe.wait_ge(x_copied, j - 3)
                for kk in range(2):
                    for t in range(2):
                        k = 2 * j + kk
                        m = pe.transpose(proj[:, j % 4, kk * S + t * P:kk * S + (t + 1) * P],
                                         x_in[:, t, k * P:(k + 1) * P], ident)
                m.then_inc(x_turned, 1)

            def pair(phase, i, last):
                n = pair0[phase] + i
                unit = UNIT0[phase] + QKVG * i
                output = OUTPUT0[phase] + QKVG * i
                other = h_q if phase == "A" else h_kv
                pe.wait_ge(proj_free, output + 2)
                multiply(unit + 1, 1, other)
                pe.wait_ge(proj_free, output + 3)
                multiply_values(unit + 2, 0, other)
                pe.wait_ge(scaled, 3 * n + 2)
                pe.wait_ge(og_done, n + 1)
                for h in range(2):
                    pe.matmul(ps_s[:, h, 0:P], q_t[:, h, 0:P], k_t[:, h, 0:P], start=True, stop=True)
                    m = pe.matmul(ps_s[:, h, P:384], q_t[:, h, P:S], k_t[:, h, :], start=True, stop=True)
                m.then_inc(scores_done, 1)
                multiply(unit + 3, 1, h_q)
                pe.wait_ge(p_ready, n + 1)
                for h in range(2):
                    for c in range(3):
                        m = pe.transpose(ps_t[:, h, c * P:(c + 1) * P], scores[:, h, (0, P, 2 * P)[c]:(0, P, 2 * P)[c] + P], ident)
                m.then_inc(turned, 1)
                if not last:
                    pe.wait_ge(proj_free, output + 5)
                    multiply(unit + 4, 0, h_q)
                    values(n)

            def values(n):
                pe.wait_ge(pt_ready, n + 1)
                for h in range(2):
                    pe.matmul(ps_s[:, h, 0:S], v_tok[:, h, 0:P], p_t[:, h, 0:S], start=True, stop=False)
                    m = pe.matmul(ps_s[:, h, P:S], v_tok[:, h, P:S], p_t[:, h, S:384], start=False, stop=True)
                m.then_inc(o_done, 1)

            def gates():
                pe.wait_ge(fw_split, 1)
                for k in range(KT):
                    if k % 2 == 0:
                        pe.wait_ge(h_split, KT // 2 + k // 2 + 1)
                    for t in range(2):
                        hi = h_kv[:, k, t * P:(t + 1) * P]
                        lo = h_kv[:, k, S + t * P:S + (t + 1) * P]
                        out = ps_s[:, t, 0:HEADS]
                        pe.matmul(out, hi, fw_hi[:, k, :], start=k == 0, stop=False)
                        pe.matmul(out, hi, fw_lo[:, k, :], start=False, stop=False)
                        m = pe.matmul(out, lo, fw_hi[:, k, :], start=False, stop=k == KT - 1)
                m.then_inc(z_done, 1)

            def turn_meta():
                pe.wait_ge(meta_landed, 16)
                for k in range(KT):
                    m = pe.transpose(ps_s[:, 0, k * META:(k + 1) * META], meta_in[:, k * P:(k + 1) * P], ident[0:META, 0:META])
                m.then_inc(meta_turned, 1)

            def running_sums():
                pe.wait_ge(logf_ready, 1)
                pe.matmul(ps_s[:, 0, 0:HEADS], tri, gate[:, 0, :], start=True, stop=True)
                pe.matmul(ps_s[:, 0, HEADS:2 * HEADS], ones, gate[:, 0, :], start=True, stop=False)
                pe.matmul(ps_s[:, 0, HEADS:2 * HEADS], tri, gate[:, 1, :], start=False, stop=True)
                pe.matmul(ps_s[0:HEADS, 1, 0:P], gate[:, 0, :], tri, start=True, stop=True)
                pe.matmul(ps_s[0:HEADS, 1, P:S], gate[:, 0, :], ones, start=True, stop=False)
                pe.matmul(ps_s[0:HEADS, 1, P:S], gate[:, 1, :], tri, start=False, stop=True).then_inc(cum_done, 1)

            for phase in phases:
                r = phases.index(phase)
                if phase == "B":
                    gates()
                else:
                    pe.wait_ge(x_copied, KT // 2 - 2)
                h0 = 0 if phase == "A" else KT
                pe.wait_ge(proj_free, OUTPUT0[phase] + 1)

                def first_wait(s):
                    if s == (2 if phase == "A" else 1):
                        pe.wait_ge(consts_in, 16 * 7)
                        norm_sum(r, 8 * (r + 1))
                    pe.wait_ge(h_split, h0 + 2 * s + 2)

                multiply(UNIT0[phase], 0, h_q, chunk_wait=first_wait)
                if phase == "B":
                    running_sums()
                with pe.Fori(0, PAIRS - 1) as i:
                    pair(phase, i, False)
                pair(phase, PAIRS - 1, True)

                def halves(j, bank, peeled=False, meta=False):
                    unit = UNIT0[phase] + UNITS_ATT + 2 * j
                    pe.wait_ge(proj_free, OUTPUT0[phase] + UNITS_ATT + j + 1)

                    def first_wait(s):
                        if s == 1:
                            values(pair0[phase] + PAIRS - 1)
                        pe.wait_ge(og_split, 8 * r + s + 1)

                    multiply(unit, bank, gated[:, 0:KT], last=False, chunk_wait=first_wait if peeled else None)
                    if meta:
                        turn_meta()
                    wait = (lambda s: pe.wait_ge(og_split, 8 * r + 4 + s + 1)) if peeled else None
                    multiply(unit + 1, bank, gated[:, KT:2 * KT], first=False, chunk_wait=wait)

                halves(0, 0, peeled=True)
                with pe.Fori(0, (OUT_N - 2) // 2) as m:
                    for jj in range(2):
                        halves(2 * m + 1 + jj, (1 + jj) % 2)
                halves(OUT_N - 1, 1, meta=phase == "B")

            norm_sum(2, 24)
            pe.wait_ge(ln_summable, 1)
            pe.wait_ge(gain_summed, OUT_N + 1)
            pe.matmul(ps_s[:, 1, 0:T], ones, ln_sums[:, 0, :], start=True, stop=False)
            pe.matmul(ps_s[:, 1, 0:T], ones, ln_sums[:, 1, :], start=False, stop=True).then_inc(ln_summed, 1)

            def layer_norm_sums(n, summable):
                if summable is not None:
                    pe.wait_ge(ln_summable, summable)
                    pe.matmul(ps_t[:, 0, 0:T], ones, ln_sums[:, 0, :], start=True, stop=False)
                    pe.matmul(ps_t[:, 0, 0:T], ones, ln_sums[:, 1, :], start=False, stop=True).then_inc(ln_summed, 1)
                for c in range(4):
                    pe.wait_ge(ln_squared, 4 * n + c + 1)
                    for k in range(4):
                        m = pe.matmul(ps_t[:, 1, 0:T], ones, ln_sq[c % 2][:, k, :], start=c + k == 0, stop=c + k == 6)
                    m.then_inc(ln_sq_used, 1)

            layer_norm_sums(0, None)

            def products(bank, t, s, kk, cols, hi, lo, first, last):
                out = proj[:, 2 * bank + t, 0:T]
                pe.matmul(out, w_hi[:, s, kk, cols], hi, start=first, stop=False)
                pe.matmul(out, w_hi[:, s, kk, cols], lo, start=False, stop=False)
                return pe.matmul(out, w_lo[:, s, kk, cols], hi, start=False, stop=last)

            def multiply_piece(unit, bank, s, hi, lo, chunk_wait=None):
                pe.wait_ge(pieces_split, unit * PIECES + s + 1 + PIECES)
                if chunk_wait is not None:
                    chunk_wait(s)
                for kk in range(PK):
                    k = s * PK + kk
                    for t in range(2):
                        m = products(bank, t, s, kk, slice(t * P, (t + 1) * P), hi[:, k, :], lo[:, k, :], k == 0, k == KT - 1)
                m.then_inc(pieces_used, 1)

            def multiply_2(unit, output, bank, hi, lo, chunk_wait=None, after=()):
                pe.wait_ge(proj_free, output + 1)
                for s in range(PIECES):
                    multiply_piece(unit, bank, s, hi, lo, chunk_wait)
                    for piece, work, *arguments in after:
                        if piece == s:
                            work(*arguments)

            with pe.Fori(0, DEPTH) as l:
                u0 = UNIT_2 + UNITS_2 * l
                o0 = OUTPUT_2 + OUTPUTS_2 * l

                def turn_rows():
                    pe.wait_ge(rows_landed, 48 * l + 48)
                    pe.transpose(ps_s[:, 0, 0:VEC_ROWS], rows_in[0:VEC_ROWS, 0, :], ident[0:VEC_ROWS, 0:VEC_ROWS])
                    pe.transpose(ps_s[:, 1, 0:CONV_ROWS], rows_in[0:CONV_ROWS, 1, :], ident[0:CONV_ROWS, 0:CONV_ROWS])\
                      .then_inc(rows_turned, 1)

                for j in range(U_K):
                    wait = (lambda s: pe.wait_ge(in_split, 4 * l + s + 1)) if j == 0 else None
                    multiply_2(u0 + j, o0 + j, j % 2, in_hi, in_lo, wait, after=((2, turn_rows),) if j == 0 else ())
                multiply_2(u0 + U_K, o0 + U_K, 0, in_hi, in_lo)
                multiply_2(u0 + U_V, o0 + U_V, 1, in_hi, in_lo)
                pe.wait_ge(consts_2_in, 16 * 5)

                def spread_keys(r):
                    pe.wait_ge(proj_free, o0 + U_K + 3)
                    if r == 1:
                        pe.wait_ge(k_spread_ready, KV_HEADS * l + 2)
                    for e, banks in ((0, ps_s), (1, ps_t)):
                        for turned_side in range(2):
                            m = pe.matmul(banks[:, turned_side, 0:T], spread[:, 2 * e + turned_side, :], k_raw[:, r, :],
                                          start=True, stop=True)
                        m.then_inc(kv_turned, 1)

                def turn_values():
                    pe.wait_ge(k_spread_ready, KV_HEADS * l + 4)
                    pe.wait_ge(proj_free, o0 + U_V + 3)
                    for t in range(2):
                        pe.transpose(ps_s[0:META, 0, t * P:(t + 1) * P], v_raw[:, t, 0:META], ident)
                        for r in range(2):
                            m = pe.transpose(ps_t[:, r, t * P:(t + 1) * P], v_raw[:, t, META + r * P:META + (r + 1) * P], ident)
                    m.then_inc(v_turned, 1)

                def exchange_queries(r, banks):
                    pe.wait_ge(proj_free, o0 + U_Q + r + 3)
                    if r == 0:
                        pe.wait_ge(v_all_ready, 3 * l + 3)
                    if r >= 2:
                        pe.wait_ge(q_rotated, 4 * l + r - 1)
                    for e in range(2):
                        m = pe.matmul(banks[:, e, 0:T], perm, att[:, 2 * r + e, :], start=True, stop=True)
                    m.then_inc(q_turned, 1)

                multiply_2(u0 + U_Q, o0 + U_Q, 0, in_hi, in_lo, after=((1, spread_keys, 0),))
                multiply_2(u0 + U_Q + 1, o0 + U_Q + 1, 1, in_hi, in_lo, after=((1, spread_keys, 1),))
                multiply_2(u0 + U_Q + 2, o0 + U_Q + 2, 0, in_hi, in_lo,
                           after=((0, turn_values), (2, exchange_queries, 0, ps_s)))
                multiply_2(u0 + U_Q + 3, o0 + U_Q + 3, 1, in_hi, in_lo,
                           after=((0, exchange_queries, 1, ps_t), (2, exchange_queries, 2, ps_s)))

                def score(i):
                    pe.wait_ge(q_rotated, 4 * l + (3 if i == 0 else 4))
                    pe.wait_ge(k_spread_ready, KV_HEADS * l + KV_HEADS)
                    if i == 7:
                        pe.wait_ge(c_mu_ready, l + 1)
                    for h in range(2):
                        rows = slice(HD * h, HD * h + HD)
                        q, k = att[rows, i, :], k_spread[rows, i // 2, :]
                        pe.matmul(ps_s[:, h, 0:144], q[:, META:META + P], k[:, 0:META + P], start=True, stop=True)
                        pe.matmul(ps_s[:, h, 144:416], q[:, META + P:T], k, start=True, stop=True)
                        m = pe.matmul(ps_s[0:META, h, 416:432], q[:, 0:META], k[:, 0:META], start=True, stop=True)
                    m.then_inc(scores_2_done, 1)

                def turn_probabilities(i, bank, output_before):
                    pe.wait_ge(p_2_ready, PAIRS_2 * l + i + 1)
                    pe.wait_ge(o_2_taken, PAIRS_2 * l + i + 1)
                    pe.wait_ge(proj_free, output_before + 3)
                    for h in range(2):
                        pe.transpose(ps_t[:, h, 0:P], s2[:, h, META:144], ident)
                        pe.transpose(ps_t[:, h, P:2 * P], s2[:, h, 162:290], ident)
                        pe.transpose(ps_t[:, h, 2 * P:3 * P], s2[:, h, 290:418], ident)
                        out = proj[0:META, 2 * bank + h, :]
                        pe.transpose(out[:, 0:META], sm[0:META, h, 0:META], ident[0:META, 0:META])
                        pe.transpose(out[:, META:144], s2[:, h, 0:META], ident)
                        m = pe.transpose(out[:, 144:T], s2[:, h, 146:162], ident)
                    m.then_inc(turned_2, 1)

                def head_values(i):
                    pe.wait_ge(pt2_ready, PAIRS_2 * l + i + 1)
                    pe.wait_ge(ptm_ready, PAIRS_2 * l + i + 1)
                    values_of = slice(HD * (i // 2), HD * (i // 2) + HD)
                    for h in range(2):
                        out = ps_t[HD * h:HD * h + HD, 0, :]
                        pe.matmul(out[:, 0:T], v_all[0:META, 0, values_of], ptm[0:META, h, :], start=True, stop=False)
                        pe.matmul(out[:, META:T], v_all[:, 1, values_of], pt2[:, h, 0:2 * P], start=False, stop=False)
                        m = pe.matmul(out[:, META + P:T], v_all[:, 2, values_of], pt2[:, h, 2 * P:3 * P], start=False, stop=True)
                    m.then_inc(o_2_done, 1)

                def channel_sums(source, bank, ready, done):
                    ready()
                    pe.wait_ge(neg_max_ready, PAIRS_2 * l + 7 + bank)
                    for t in range(CT):
                        m = pe.matmul(ps_s[:, bank, 0:T], ones, source[:, t, :], start=t == 0, stop=t == CT - 1)
                    m.then_inc(done, 1)

                for i in range(PAIRS_2):
                    j = U_RX + i
                    if i == 0:
                        extra = [(0, exchange_queries, 3, ps_t), (0, score, 0)]
                    else:
                        extra = [(0, turn_probabilities, i - 1, (i + 1) % 2, o0 + j - 1), (0, score, i), (1, head_values, i - 1)]
                    if i == 6:
                        extra.append((3, channel_sums, conv, 0, lambda: pe.wait_ge(conv_tap, TAPS * (l + 1)), c_summed))
                    if i == 7:
                        extra.append((3, channel_sums, conv_sq, 1, lambda: pe.wait_ge(c_squared, l + 1), c_sq_summed))
                    multiply_2(u0 + j, o0 + j, i % 2, in_hi, in_lo, after=extra)

                u, o = u0 + U_LRU, o0 + O_LRU
                pe.wait_ge(y_split, 6 * l + 1)
                for s in range(PIECES):
                    pe.wait_ge(pieces_split, u * PIECES + s + 1 + PIECES)
                    pe.wait_ge(proj_free, o + s + 1)
                    for gate_side in range(2):
                        m = products(s % 2, gate_side, s, 0, slice(gate_side * P, (gate_side + 1) * P),
                                     y_hi[:, 8 + s, :], y_lo[:, 8 + s, :], True, True)
                    m.then_inc(pieces_used, 1)
                multiply_2(u0 + U_RGATE, o0 + O_RGATE, 0, in_hi, in_lo,
                           after=((0, turn_probabilities, 7, 1, o0 + O_LRU + 3), (1, head_values, 7)))
                multiply_2(u0 + U_RGATE + 1, o0 + O_RGATE + 1, 1, in_hi, in_lo)
                u, o = u0 + U_PW, o0 + O_PW
                pe.wait_ge(y_split, 6 * l + 2)
                for s in range(PIECES):
                    pe.wait_ge(pieces_split, u * PIECES + s + 1 + PIECES)
                    pe.wait_ge(proj_free, o + s + 1)
                    for kk in range(CT):
                        m = products(s % 2, 0, s, kk, slice(0, P), y_hi[:, 12 + kk, :], y_lo[:, 12 + kk, :],
                                     kk == 0, kk == CT - 1)
                    m.then_inc(pieces_used, 1)
                splits = (3, 4, 5, 6)
                multiply_2(u0 + U_OUT, o0 + O_OUT, 0, y_hi, y_lo, lambda s: pe.wait_ge(y_split, 6 * l + splits[s]))
                with pe.Fori(0, (OUT_N - 2) // 2) as m3:
                    for jj in range(2):
                        j = 2 * m3 + 1 + jj
                        multiply_2(u0 + U_OUT + j, o0 + O_OUT + j, (1 + jj) % 2, y_hi, y_lo)
                multiply_2(u0 + U_OUT + OUT_N - 1, o0 + O_OUT + OUT_N - 1, 1, y_hi, y_lo)
                layer_norm_sums(l + 1, OUT_N * l + OUT_N + 1)
            for c in range(4):
                pe.wait_ge(affine_act, 4 * DEPTH + c + 1)
                pe.wait_ge(affine_pool, 4 * DEPTH + c + 1)
                for t in range(2):
                    bank = (2 * c + t) % 4
                    if c >= 2:
                        pe.wait_ge(copied_out_dve if t == 0 else copied_out_act, c - 1)
                    for kk in range(4):
                        m = pe.transpose(proj[:, bank, kk * P:(kk + 1) * P],
                                         x_res[:, 4 * c + kk, META + t * P:META + (t + 1) * P], ident)
                    m.then_inc(rows_turned_out, 1)

        @block.vector
        def _(dve):
            step = Steps(dve, dve_step)
            dve.sem_inc(pieces_split, PIECES)
            dve.sem_inc(proj_free, 2)
            dve.sem_inc(og_done, 1)
            dve.sem_inc(bias_ready, 1)

            def split_lo(unit, s):
                dve.wait_ge(hi_ready, unit * PIECES + s + 1)
                dve.tensor_tensor(w_lo[:, s], w_raw[:, s], w_hi[:, s].bitcast(F32), ALU.subtract).then_inc(pieces_split, 1)

            def take_output(output, bank, dst):
                dve.wait_ge(half_copied, output + 1)
                dve.tensor_tensor(dst, proj[:, 2 * bank:2 * bank + 2, 0:S], part, ALU.add).then_inc(proj_free, 1)

            def take_scaled(output, bank, dst, scale=1.0):
                take_output(output, bank, dst)
                dve.wait_ge(proj_free, output + 3)
                dve.scalar_tensor_tensor(dst, dst, scale, rstd.unsqueeze(1).to_broadcast([P, 2, S]), ALU.mult, ALU.mult)\
                   .then_inc(scaled, 1)

            def refine(rstd, mean, spare):
                step(dve.tensor_tensor(spare, mean, rstd, ALU.mult))
                step(dve.scalar_tensor_tensor(spare, spare, -0.5, rstd, ALU.mult, ALU.mult))
                return dve.scalar_tensor_tensor(rstd, spare, 1.5, rstd, ALU.add, ALU.mult)

            def mean_squares(n):
                dve.wait_ge(norm_summed, n + 1)
                dve.tensor_scalar(norm_mean[:, 0:S], ps_t[:, 0, 0:S], 1.0 / D, EPS, ALU.mult, ALU.add)
                dve.tensor_scalar(norm_mean[:, S:S + 2], ps_t[:, 1, 0:2], 1.0 / D, EPS, ALU.mult, ALU.add).then_inc(mean_ready, 1)

            def reciprocal_of_root(n):
                dve.wait_ge(root_ready, n + 1)
                step(dve.reciprocal(norm_rstd, norm_root))
                refine(norm_rstd, norm_mean, norm_spare).then_inc(rstd_ready, 1)
                dve.wait_ge(rstd_ready, n + 1)

            def h_los(first, vector, dst, pairs):
                for pair_of_tiles in pairs:
                    dve.wait_ge(h_hi, first + pair_of_tiles + 1)
                    for k in (2 * pair_of_tiles, 2 * pair_of_tiles + 1):
                        m = dve.scalar_tensor_tensor(dst[:, k, S:512], x1[:, k, :], gain(vector, k),
                                                     dst[:, k, 0:S].bitcast(F32), ALU.mult, ALU.subtract)
                    m.then_inc(h_split, 1)

            step(dve.memset(sumsq, 0.0))
            dve.wait_ge(vec_turned, 1)
            dve.tensor_copy(gains[:], ps_s[:, 0, 0:len(VECTORS) * KT]).then_inc(vec_copied, 1)
            dve.wait_ge(vec_copied, 1)
            for j in range(KT // 2):
                dve.wait_ge(x_turned, j + 1)
                dve.tensor_copy(x1[:, 2 * j:2 * j + 2, :], proj[:, j % 4, :].rearrange("p (k s) -> p k s", k=2))\
                   .then_inc(x_copied, 1)
                if j >= 1:
                    h_los(0, "a_norm", h_q, (j - 1,))
                    dve.wait_ge(squared, j)
                    if j >= 2:
                        dve.wait_ge(sumsq_ready, j - 1)
                    dve.tensor_tensor(sumsq, sumsq, squares, ALU.add).then_inc(sumsq_ready, 1)
                    if j % 2 == 0:
                        split_lo(0, j // 2 - 1)
            h_los(0, "a_norm", h_q, (KT // 2 - 1,))
            split_lo(0, 3)
            dve.wait_ge(squared, KT // 2)
            dve.wait_ge(sumsq_ready, KT // 2 - 1)
            dve.tensor_tensor(sumsq, sumsq, squares, ALU.add).then_inc(sumsq_ready, 1)

            def gated_lo(r, c):
                dve.wait_ge(og_hi, 8 * r + c + 1)
                chunk = slice(4 * c, 4 * c + 4)
                dve.tensor_tensor(gated[:, chunk, S:512], og[:, chunk, :], gated[:, chunk, 0:S].bitcast(F32), ALU.subtract)\
                   .then_inc(og_split, 1)
            dve.wait_ge(fw_hi_ready, 1)
            dve.tensor_tensor(fw_lo[:], fw, fw_hi[:].bitcast(F32), ALU.subtract).then_inc(fw_split, 1)

            def pair(phase, i, last):
                n = pair0[phase] + i
                unit = UNIT0[phase] + QKVG * i
                output = OUTPUT0[phase] + QKVG * i
                for s in range(PIECES):
                    split_lo(unit + 2, s)
                take_scaled(output + 1, 1, k_t)
                for s in range(PIECES):
                    split_lo(unit + 3, s)
                dve.wait_ge(scores_done, n + 1)
                dve.wait_ge(bias_ready, n + 2)
                dve.tensor_tensor(scores, ps_s[:, :, 0:384], bias, ALU.add).then_inc(s_added, 1)
                split_lo(unit + 4, 0)
                dve.wait_ge(s_added, n + 2)
                dve.tensor_reduce(row_max[:, 0, :], scores[:, :, 0:P], AX_X, ALU.max)
                dve.tensor_reduce(row_max[:, 1, :], scores[:, :, P:384], AX_X, ALU.max).then_inc(maxed, 1)
                dve.wait_ge(maxed, n + 1)
                dve.tensor_scalar(row_max, row_max, -1.0, None, ALU.mult).then_inc(negmax_ready, 1)
                split_lo(unit + 4, 1)
                dve.wait_ge(exp_done, 4 * n + 4)
                dve.reciprocal(row_sum, row_sum).then_inc(recip_ready, 1)
                dve.wait_ge(recip_ready, n + 1)
                for h in range(2):
                    for t, (a, b) in enumerate(((0, P), (P, 384))):
                        m = dve.tensor_scalar(scores[:, h, a:b], scores[:, h, a:b], row_sum[:, t, h:h + 1], None, ALU.mult)
                m.then_inc(p_ready, 1)
                split_lo(unit + 4, 2)
                split_lo(unit + 4, 3)
                if last:
                    gated_lo(phases.index(phase), 0)
                    gated_lo(phases.index(phase), 1)
                take_scaled(output + 3, 1, g_t, scale=0.5)
                if not last:
                    split_lo(unit + 5, 0)
                dve.wait_ge(tanh_done, n + 1)
                dve.scalar_tensor_tensor(tanh_g, tanh_g, 1.0, g_t, ALU.add, ALU.mult).then_inc(silu_ready, 1)
                if not last:
                    for s in range(1, PIECES):
                        split_lo(unit + 5, s)
                    take_scaled(output + 4, 0, q_t, scale=SCALE)
                    gate_heads(n, 2 * i)

            def gate_heads(n, head):
                dve.wait_ge(o_done, n + 1)
                dve.wait_ge(silu_ready, n + 1)
                dve.tensor_tensor(og[:, bass.ds(head, 2), :], ps_s[:, :, 0:S], tanh_g, ALU.mult).then_inc(og_done, 1)

            def forget_gates():
                dve.wait_ge(z_done, 1)
                for t in range(2):
                    m = dve.scalar_tensor_tensor(gate[:, t, :], ps_s[:, t, 0:HEADS], rstd_column[:, t:t + 1],
                                                 fb[:, t, :], ALU.mult, ALU.add)
                step(m)
                dve.scalar_tensor_tensor(gate_u, gate, -1.0, gate, ALU.mult, ALU.max).then_inc(gate_exp_in, 1)
                step(dve.tensor_scalar(gate, gate, 0.0, None, ALU.min))
                dve.wait_ge(gate_exp, 1)
                step(dve.tensor_scalar(gate_u, gate_t, 2.0, None, ALU.add))
                step(dve.reciprocal(gate_u, gate_u))
                step(dve.tensor_tensor(gate_t, gate_t, gate_u, ALU.mult))
                step(dve.tensor_tensor(gate_u, gate_t, gate_t, ALU.mult))
                step(dve.tensor_scalar(cum, gate_u, 1.0 / 19, None, ALU.mult))
                for c in range(8, 0, -1):
                    step(dve.scalar_tensor_tensor(cum, cum, 1.0 / (2 * c + 1), gate_u, ALU.add, ALU.mult))
                step(dve.scalar_tensor_tensor(cum, cum, 1.0, gate_t, ALU.add, ALU.mult))
                dve.scalar_tensor_tensor(gate, cum, -2.0, gate, ALU.mult, ALU.add).then_inc(logf_ready, 1)

            def copy_sums():
                dve.wait_ge(cum_done, 1)
                dve.tensor_copy(cum, ps_s[:, 0, 0:2 * HEADS].rearrange("p (t h) -> p t h", t=2))
                dve.tensor_scalar(cum_row, ps_s[0:HEADS, 1, 0:S], -1.0, None, ALU.mult).then_inc(cum_copied, 1)

            for phase in phases:
                r = phases.index(phase)
                if phase == "B":
                    h_los(KT // 2, "kv_norm", h_kv, (7,))
                    dve.wait_ge(squared, 8 * (r + 1))
                    dve.tensor_tensor(sumsq, sumsq, squares, ALU.add).then_inc(sumsq_ready, 1)
                    h_los(KT, "b_norm", h_q, range(0, 2))
                mean_squares(r)
                if phase == "B":
                    h_los(KT, "b_norm", h_q, range(2, 4))
                reciprocal_of_root(r)
                if phase == "B":
                    h_los(KT, "b_norm", h_q, range(4, 8))
                    forget_gates()
                for s in range(PIECES):
                    split_lo(UNIT0[phase] + 1, s)
                if phase == "B":
                    copy_sums()
                take_scaled(OUTPUT0[phase], 0, q_t, scale=SCALE)
                with dve.Fori(0, PAIRS - 1) as i:
                    pair(phase, i, False)
                pair(phase, PAIRS - 1, True)

                unit = UNIT0[phase] + UNITS_ATT

                gate_heads(pair0[phase] + PAIRS - 1, 2 * (PAIRS - 1))
                for c in range(8):
                    if 1 <= c < 7:
                        gated_lo(r, c + 1)
                    split_lo(unit + 1 + c // 4, c % 4)

                def out_update(j, bank, last=False):
                    output = OUTPUT0[phase] + UNITS_ATT + j
                    take_output(output, bank, v_t)
                    dve.wait_ge(proj_free, output + 3)
                    xs = x1[:, bass.ds(2 * j, 2), :]
                    dve.tensor_tensor(xs, xs, v_t, ALU.add).then_inc(x_updated, 1)
                    if phase == "B":
                        dve.wait_ge(x_updated, 8 * r + j + 1)
                        dve.wait_ge(gain_summed, j + 1)
                        for t in range(2):
                            column = VECTORS.index("final_norm") * KT + 2 * j + t
                            m = dve.scalar_tensor_tensor(ln_sums[:, t:t + 1, META:T], x1[:, bass.ds(2 * j + t, 1), :],
                                                         gains[:, bass.ds(column, 1)], ln_sums[:, t:t + 1, META:T],
                                                         ALU.mult, ALU.add)
                        m.then_inc(gain_summed, 1)
                    if not last:
                        dve.wait_ge(squared, 8 * (r + 1) + j + 1)
                        dve.tensor_tensor(sumsq, sumsq, squares, ALU.add).then_inc(sumsq_ready, 1)

                step(dve.memset(sumsq, 0.0))
                if phase == "B":
                    dve.memset(ln_sums, 0.0).then_inc(gain_summed, 1)
                out_update(0, 0)
                with dve.Fori(0, (OUT_N - 2) // 2) as m:
                    for jj in range(2):
                        j = 2 * m + 1 + jj
                        u = unit + 2 * j
                        for half in range(2):
                            for s in range(PIECES):
                                split_lo(u + 1 + half, s)
                        out_update(j, (1 + jj) % 2)
                j = OUT_N - 1
                u = unit + 2 * j
                for s in range(PIECES):
                    split_lo(u + 1, s)
                for s in range(PIECES):
                    if phase == "A":
                        h_los(KT // 2, "kv_norm", h_kv, (2 * s, 2 * s + 1) if s < 3 else (6,))
                    split_lo(u + 2, s)
                if phase == "B":
                    dve.wait_ge(meta_turned, 1)
                    dve.tensor_copy(x_res[:, :, 0:META], ps_s[:, 0, 0:KT * META].rearrange("p (k m) -> p k m", m=META))\
                       .then_inc(meta_copied, 1)
                    dve.wait_ge(meta_copied, 1)
                    dve.tensor_reduce(ln_sums[:, 0, 0:META], x_res[:, :, 0:META].rearrange("p k t -> p t k"), AX_X, ALU.add)\
                       .then_inc(ln_summable, 1)
                out_update(j, 1, last=True)
            dve.wait_ge(squared, 24)
            dve.tensor_tensor(sumsq, sumsq, squares, ALU.add).then_inc(sumsq_ready, 1)
            mean_squares(2)
            reciprocal_of_root(2)
            def over(row, n):
                return row.unsqueeze(1).to_broadcast([P, n, T])

            def centre(c):
                chunk = x_res[:, 4 * c:4 * c + 4, :]
                dve.tensor_tensor(chunk, chunk, over(ln_mu, 4), ALU.subtract).then_inc(centred, 1)

            def final_norm(c):
                for k in range(4 * c, 4 * c + (3 if c else 4)):
                    m = dve.scalar_tensor_tensor(x1[:, k, :], x1[:, k, :], gain("final_norm", k), rstd, ALU.mult, ALU.mult)
                m.then_inc(final_chunk, 1)
                if c == 3:
                    dve.wait_ge(final_chunk, 4)
                    dve.sem_inc(x_normed, 1)

            def layer_norm(n, first=False):
                if first:
                    dve.wait_ge(ln_mu_raw, 1)
                    dve.tensor_tensor(ln_mu[:, META:T], ln_mu[:, META:T], rstd, ALU.mult).then_inc(ln_mu_ready, 1)
                    final_norm(0)
                    final_norm(1)
                    dve.wait_ge(ln_mu_ready, 1)
                    for c in range(4):
                        if c < 2:
                            final_norm(c + 2)
                        dve.wait_ge(final_chunk, c + 1)
                        if c:
                            dve.wait_ge(final_scaled, 2 * c)
                        centre(c)
                else:
                    dve.wait_ge(ln_mu_ready, n + 1)
                    for c in range(4):
                        centre(c)
                dve.wait_ge(ln_sq_used, 4 * n + 4)
                dve.tensor_scalar(ln_mean, ps_t[:, 1, 0:T], 1.0 / D, LN_EPS, ALU.mult, ALU.add).then_inc(ln_mean_ready, 1)
                dve.wait_ge(ln_root_ready, n + 1)
                step(dve.reciprocal(ln_rstd, ln_root))
                step(refine(ln_rstd, ln_mean, ln_spare))

                def scale(c):
                    chunk = x_res[:, 4 * c:4 * c + 4, :]
                    dve.tensor_tensor(chunk, chunk, over(ln_rstd, 4), ALU.mult).then_inc(ln_scaled, 1)

                scale(0)
                scale(1)
                for c in range(4):
                    if c < 2:
                        scale(c + 2)
                    rows = slice(4 * c, 4 * c + 4)
                    dve.wait_ge(in_hi_ready, 4 * n + c + 1)
                    dve.tensor_tensor(in_lo[:, rows, :], x_res[:, rows, :], in_hi[:, rows, :].bitcast(F32), ALU.subtract)\
                       .then_inc(in_split, 1)

            layer_norm(0, first=True)
            steps_before = step.base + step.done
            LAYER_STEPS = 52

            def split_part_lo(unit, s, shape):
                dve.wait_ge(hi_ready, unit * PIECES + s + 1)
                dve.tensor_tensor(part_of(w_lo, s, shape), part_of(w_raw, s, shape), part_of(w_hi, s, shape).bitcast(F32),
                                  ALU.subtract).then_inc(pieces_split, 1)

            def lo_of(count, chunk, src):
                dve.wait_ge(y_hi_ready, 6 * l + count)
                rows = slice(4 * chunk, 4 * chunk + 4)
                return dve.tensor_tensor(y_lo[:, rows, :], src, y_hi[:, rows, :].bitcast(F32), ALU.subtract)\
                          .then_inc(y_split, 1)

            def silu_of(count, dst, half):
                dve.wait_ge(gate_tanh, 5 * l + count)
                dve.scalar_tensor_tensor(dst, tanh_2, 1.0, half, ALU.add, ALU.mult).then_inc(gate_used, 1)
                dve.wait_ge(gate_used, 5 * l + count)

            with dve.Fori(0, DEPTH) as l:
                u0 = UNIT_2 + UNITS_2 * l
                o0 = OUTPUT_2 + OUTPUTS_2 * l
                step.start(steps_before + LAYER_STEPS * l)
                for s in range(3):
                    split_lo(u0 + 1, s)
                dve.wait_ge(rows_turned, l + 1)
                dve.tensor_copy(vec, ps_s[:, 0, 0:VEC_ROWS])
                dve.tensor_copy(taps, ps_s[:, 1, 0:CONV_ROWS]).then_inc(rows_copied, 1)
                dve.wait_ge(rows_copied, l + 1)
                lam = vec[:, VEC["lru_lambda"]:VEC["lru_lambda"] + CT]
                dve.scalar_tensor_tensor(small[:, 0, :], lam, -1.0, lam, ALU.mult, ALU.max).then_inc(exp_lam_in, 1)
                dve.tensor_scalar(small[:, 2, :], lam, -1.0, 0.0, ALU.mult, ALU.max)
                dve.tensor_scalar(half_ln, vec[:, VEC["conv_ln_g"]:VEC["conv_ln_b"] + CT].rearrange("p (a b) -> p a b", a=2),
                                  0.5, None, ALU.mult)
                dve.wait_ge(exp_lam, l + 1)
                step(dve.tensor_scalar(small[:, 0, :], small[:, 1, :], 2.0, None, ALU.add))
                step(dve.reciprocal(small[:, 0, :], small[:, 0, :]))
                step(dve.tensor_tensor(small[:, 1, :], small[:, 1, :], small[:, 0, :], ALU.mult))
                step(dve.tensor_tensor(small[:, 0, :], small[:, 1, :], small[:, 1, :], ALU.mult))
                step(dve.tensor_scalar(small[:, 3, :], small[:, 0, :], 1.0 / 19, None, ALU.mult))
                for c in range(8, 0, -1):
                    step(dve.scalar_tensor_tensor(small[:, 3, :], small[:, 3, :], 1.0 / (2 * c + 1), small[:, 0, :],
                                                  ALU.add, ALU.mult))
                step(dve.scalar_tensor_tensor(small[:, 3, :], small[:, 3, :], 1.0, small[:, 1, :], ALU.add, ALU.mult))
                step(dve.scalar_tensor_tensor(small[:, 3, :], small[:, 3, :], 2.0, small[:, 2, :], ALU.mult, ALU.add))
                dve.tensor_scalar(lru_c8[:, 0, :], small[:, 3, :], LRU_C, None, ALU.mult)
                dve.tensor_scalar(lru_c8[:, 1, :], small[:, 3, :], -LRU_C, None, ALU.mult).then_inc(lru_c_ready, 1)
                split_lo(u0 + 1, 3)
                for j in range(1, 4):
                    for s in range(PIECES):
                        split_lo(u0 + j + 1, s)
                dve.wait_ge(glu_tanh, l + 1)
                dve.wait_ge(pads_ready, 1)
                dve.scalar_tensor_tensor(c_pad[:, :, TAPS - 1:TAPS - 1 + T], tanh_2, 1.0, val, ALU.add, ALU.mult).then_inc(conv_in, 1)
                dve.wait_ge(conv_in, l + 1)
                for t in range(CT):
                    b = VEC["conv_dw_b"] + t
                    m = dve.tensor_scalar(conv[:, t, :], c_pad[:, t, 0:T], taps[:, t:t + 1], vec[:, b:b + 1], ALU.mult, ALU.add)
                m.then_inc(conv_tap, 1)

                taps_done = [1]

                def add_taps(count):
                    for tap in range(taps_done[0], taps_done[0] + count):
                        dve.wait_ge(conv_tap, TAPS * l + tap)
                        for t in range(CT):
                            m = dve.scalar_tensor_tensor(conv[:, t, :], c_pad[:, t, tap:tap + T], taps[:, CT * tap + t:CT * tap + t + 1],
                                                         conv[:, t, :], ALU.mult, ALU.add)
                        m.then_inc(conv_tap, 1)
                    taps_done[0] += count

                def rotate_keys(r):
                    for e, banks in ((0, ps_s), (1, ps_t)):
                        kv = 2 * r + e
                        dve.wait_ge(kv_turned, 4 * l + kv + 1)
                        if kv:
                            dve.wait_ge(k_spread_ready, 4 * l + kv)
                        dve.tensor_tensor(k_spread[:, kv, :], banks[:, 0, 0:T], cos, ALU.mult)
                        step(dve.tensor_tensor(turn_t[:, 0, :], banks[:, 1, 0:T], sin, ALU.mult))
                        dve.tensor_tensor(k_spread[:, kv, :], k_spread[:, kv, :], turn_t[:, 0, :], ALU.add)\
                           .then_inc(k_spread_ready, 1)

                def copy_values():
                    dve.wait_ge(v_turned, l + 1)
                    dve.tensor_copy(v_all[0:META, 0, :], ps_s[0:META, 0, 0:2 * P]).then_inc(v_all_ready, 1)
                    for r in range(2):
                        dve.tensor_copy(v_all[:, 1 + r, :], ps_t[:, r, 0:2 * P]).then_inc(v_all_ready, 1)

                def rotate_queries(r, banks):
                    dve.wait_ge(q_turned, 4 * l + r + 1)
                    if r:
                        dve.wait_ge(q_rotated, 4 * l + r)
                    else:
                        dve.wait_ge(k_spread_ready, KV_HEADS * l + KV_HEADS)
                    q = att[:, 2 * r:2 * r + 2, :]
                    dve.scalar_tensor_tensor(q, q, HD ** -0.5, over(cos, 2), ALU.mult, ALU.mult)
                    step(dve.scalar_tensor_tensor(turn_t, banks[:, :, 0:T], HD ** -0.5, over(sin, 2), ALU.mult, ALU.mult))
                    dve.tensor_tensor(q, q, turn_t, ALU.add).then_inc(q_rotated, 1)

                between = {(U_Q, 1): (rotate_keys, 0), (U_Q + 1, 1): (rotate_keys, 1), (U_Q + 2, 0): (copy_values,),
                           (U_Q + 2, 2): (rotate_queries, 0, ps_s), (U_Q + 3, 0): (rotate_queries, 1, ps_t),
                           (U_Q + 3, 2): (rotate_queries, 2, ps_s)}
                for j in range(U_K, U_RX):
                    for s in range(PIECES):
                        split_lo(u0 + j + 1, s)
                        if (j, s) in between:
                            work, *arguments = between[j, s]
                            work(*arguments)
                    add_taps(TAPS_DURING[j - U_K])

                def copy_meta_turned(i, bank):
                    dve.wait_ge(turned_2, PAIRS_2 * l + i + 1)
                    dve.tensor_copy(ptm[0:META], proj[0:META, 2 * bank:2 * bank + 2, 0:T]).then_inc(ptm_ready, 1)

                def score_maxima(i):
                    n, head = PAIRS_2 * l + i, 2 * i
                    dve.wait_ge(scores_2_done, n + 1)
                    dve.tensor_copy(s2[:, :, 144:146], sinks[:, head:head + 2].unsqueeze(2).to_broadcast([P, 2, 2]))
                    dve.tensor_copy(sm[0:META, :, META:META + 1], sinks[0:META, head:head + 2].unsqueeze(2))
                    dve.tensor_tensor(s2[:, :, 0:144], ps_s[:, :, 0:144],
                                      mask_2[:, 0:144].unsqueeze(1).to_broadcast([P, 2, 144]), ALU.add)
                    dve.tensor_tensor(s2[:, :, 146:418], ps_s[:, :, 144:416],
                                      mask_2[:, 144:416].unsqueeze(1).to_broadcast([P, 2, T]), ALU.add)
                    step(dve.tensor_tensor(sm[0:META, :, 0:META], ps_s[0:META, :, 416:432],
                                           mask_2[0:META, META:2 * META].unsqueeze(1).to_broadcast([META, 2, META]), ALU.add))
                    dve.tensor_reduce(neg_max[:, 0, :], s2[:, :, 0:145], AX_X, ALU.max)
                    dve.tensor_reduce(neg_max[:, 1, :], s2[:, :, 145:418], AX_X, ALU.max)
                    step(dve.tensor_reduce(neg_max[0:META, 2, :], sm[0:META], AX_X, ALU.max))
                    dve.tensor_scalar(neg_max[:, 0:2, :], neg_max[:, 0:2, :], -1.0, None, ALU.mult)
                    dve.tensor_scalar(neg_max[0:META, 2, :], neg_max[0:META, 2, :], -1.0, None, ALU.mult)\
                       .then_inc(neg_max_ready, 1)

                for i in range(PAIRS_2):
                    j = U_RX + i
                    split_next = split_lo if i < 7 else lambda unit, s: split_part_lo(unit, s, "tile")
                    split_next(u0 + j + 1, 0)
                    if i == 0:
                        rotate_queries(3, ps_t)
                    else:
                        copy_meta_turned(i - 1, (i + 1) % 2)
                    score_maxima(i)
                    taps_now = TAPS_DURING[j - U_K] if i < 6 else 0
                    add_taps(min(2, taps_now))
                    if i == 7:
                        dve.wait_ge(c_mu_ready, l + 1)
                        dve.tensor_tensor(conv, conv, over(c_stat[:, 0, :], CT), ALU.subtract).then_inc(c_centred, 1)
                    dve.wait_ge(exp_2_done, PAIRS_2 * l + i + 1)
                    dve.reciprocal(sums_2[:, 0:2, :], sums_2[:, 0:2, :])
                    dve.reciprocal(sums_2[0:META, 2, :], sums_2[0:META, 2, :]).then_inc(recip_2_ready, 1)
                    split_next(u0 + j + 1, 1)
                    if i == 5:
                        lo_of(1, 2, rc)
                    split_next(u0 + j + 1, 2)
                    add_taps(max(0, taps_now - 2))
                    split_next(u0 + j + 1, 3)
                assert taps_done[0] == TAPS, taps_done

                for s in range(PIECES):
                    split_lo(u0 + U_RGATE, s)
                u = u0 + U_RGATE
                dve.wait_ge(c_sq_summed, l + 1)
                dve.tensor_scalar(c_stat[:, 1, :], ps_s[:, 1, 0:T], 1.0 / CONV_D, LN_EPS, ALU.mult, ALU.add)\
                   .then_inc(c_mean_ready, 1)
                split_lo(u + 1, 0)
                copy_meta_turned(7, 1)
                dve.wait_ge(c_root_ready, l + 1)
                step(dve.reciprocal(c_stat[:, 2, :], c_stat[:, 2, :]))
                step(refine(c_stat[:, 2, :], c_stat[:, 1, :], c_stat[:, 0, :]))
                split_lo(u + 1, 1)
                step(dve.tensor_tensor(conv, conv, over(c_stat[:, 2, :], CT), ALU.mult))
                for t in range(CT):
                    m = dve.tensor_scalar(conv[:, t, :], conv[:, t, :], half_ln[:, 0, t:t + 1], half_ln[:, 1, t:t + 1],
                                          ALU.mult, ALU.add)
                m.then_inc(c_affine, 1)
                split_lo(u + 1, 2)
                dve.wait_ge(c_affine, l + 1)
                silu_of(1, conv, conv)
                split_lo(u + 1, 3)
                split_part_lo(u + 2, 0, "columns")
                lo_of(2, 3, conv)
                dve.wait_ge(lru_act, l + 1)
                step(dve.tensor_tensor(lru_r, lru_a, lru_a, ALU.mult))
                dve.scalar_tensor_tensor(lru_r, lru_r, 1.0, lru_t, ALU.add, ALU.mult).then_inc(lru_v_ready, 1)
                split_part_lo(u + 2, 1, "columns")
                silu_of(2, a_gates[:, 0:4, :], a_gates[:, 0:4, :])
                split_part_lo(u + 2, 2, "columns")
                dve.tensor_tensor(att[:, 0:4, :], att[:, 0:4, :], a_gates[:, 0:4, :], ALU.mult).then_inc(y_ready, 1)
                split_part_lo(u + 2, 3, "columns")
                dve.wait_ge(lru_root, l + 1)
                step(dve.tensor_tensor(lru_r, lru_r, lru_i, ALU.mult))
                for t in range(CT):
                    m = dve.tensor_tensor_scan(lru_t[:, t, :], lru_a[:, t, :], lru_r[:, t, :], 0.0, ALU.mult, ALU.add)
                step(m)
                lo_of(3, 0, att[:, 0:4, :])
                split_lo(u0 + U_OUT, 0)
                silu_of(3, a_gates[:, 4:8, :], a_gates[:, 4:8, :])
                split_lo(u0 + U_OUT, 1)
                silu_of(4, r_gates, r_gates)
                dve.tensor_tensor(lru_t, lru_t, r_gates, ALU.mult).then_inc(y_ready, 1)
                lo_of(4, 1, att[:, 4:8, :])
                split_lo(u0 + U_OUT, 2)
                silu_of(5, c_gates, c_gates)
                step(dve.memset(ln_sums, 0.0))
                lo_of(5, 2, lru_t)
                split_lo(u0 + U_OUT, 3)
                lo_of(6, 3, conv)

                def mixed(j, bank):
                    unit = u0 + U_OUT + j
                    output = o0 + O_OUT + j
                    dve.wait_ge(pieces_used, PIECES * (unit + 2))
                    dve.wait_ge(proj_free, output + 2)
                    xs = x_res[:, bass.ds(2 * j, 2), :]
                    dve.scalar_tensor_tensor(xs, xs, ALPHA, proj[:, 2 * bank:2 * bank + 2, 0:T], ALU.mult, ALU.add)\
                       .then_inc(proj_free, 1)
                    dve.wait_ge(proj_free, output + 3)
                    dve.wait_ge(ln_summable, OUT_N * l + j + 1)
                    dve.tensor_tensor(ln_sums, ln_sums, xs, ALU.add).then_inc(ln_summable, 1)

                with dve.Fori(0, OUT_N // 2) as m3:
                    for jj in range(2):
                        j = 2 * m3 + jj
                        for s in range(PIECES):
                            split_lo(u0 + U_OUT + 1 + j, s)
                        mixed(j, jj)
                layer_norm(l + 1)
                assert step.done == LAYER_STEPS, step.done
            for c in range(4):
                dve.wait_ge(rows_turned_out, 2 * c + 1)
                dve.tensor_copy(out_rows[:, 0, c * 512:(c + 1) * 512], proj[:, 2 * c % 4, :]).then_inc(copied_out_dve, 1)


NAMES = ["x", "a_w_in", "a_rel_bias", "a_w_out", "kv_w", "f_w", "f_b", "b_w_in", "b_w_out", "meta_tokens_2", "w_in_2",
         "attn_sinks_2", "w_out_2", "conv_pw_w_2"]


def layout(inputs):
    arrays = {name: np.ascontiguousarray(inputs[name]) for name in NAMES}
    arrays["norm_rows"] = np.ascontiguousarray(np.concatenate([inputs[name].reshape(-1, P) for name in VECTORS], 0))
    rows = [inputs[name + "_2"].reshape(DEPTH, -1, P) for name in LAYER_VECTORS]
    arrays["layer_rows"] = np.ascontiguousarray(np.concatenate(rows, 1))
    arrays["conv_rows"] = np.ascontiguousarray(inputs["conv_dw_w_2"].reshape(DEPTH, -1, P))
    blocks = np.zeros((DEPTH, P, CT, 2 * P), inputs["lru_wa_2"].dtype)
    for g, name in enumerate(("lru_wa_2", "lru_wx_2")):
        w = inputs[name]
        for e in range(2):
            rows, cols = slice(64 * e, 64 * e + 64), slice(P * g + 64 * e, P * g + 64 * e + 64)
            blocks[:, rows, :, cols] = w[:, e::2].transpose(0, 2, 1, 3)
    arrays["lru_blocks"] = blocks
    return arrays


def kernel(**inputs):
    import concourse.bacc as bacc
    from concourse.bass_utils import run_bass_kernel_spmd

    nc = bacc.Bacc("TRN2", target_bir_lowering=False, num_devices=1)
    const_at, constants = shape_constants()
    arrays = layout({name: np.asarray(a) for name, a in inputs.items()})
    arrays["shape_constants"] = constants
    io = {name: nc.dram_tensor(f"in_{name}_dram", a.shape, mybir.dt.from_np(a.dtype), kind="ExternalInput").ap()
          for name, a in arrays.items()}
    io["out"] = nc.dram_tensor("out_dram", (1, S, D), F32, kind="ExternalOutput").ap()
    build_program(nc, io, const_at)
    result = run_bass_kernel_spmd(nc, [{f"in_{name}_dram": a for name, a in arrays.items()}], core_ids=[0])
    return result.results[0]["out_dram"]
```
